# Optimizing a Trainium2 kernel written in Bass

```python
import math
import jax, jax.numpy as jnp
from jax import lax
import numpy as np

D_MODEL = 1024
BATCH = 1
SEQ = 512
DEPTH = 1
DEC_BATCH = 1
DEC_SEQ = 2048
PAST_LEN = 128

HEAD_DIM = 64
EPS = 1e-6
H_A = 4
W_A = H_A * 2 * HEAD_DIM
Q_BLOCK = 128
H_B = 8
W_B = H_B * HEAD_DIM
GRID_W = 64
MAX_KH = 8
KW = 16
H_C = 8
KV_C = 2
W_C = H_C * HEAD_DIM
KV_W_C = KV_C * HEAD_DIM
WINDOW = 128
BLOCK = 128

_SIZES = (W_A, W_A, W_A, W_A,
          W_B, W_B, W_B, W_B,
          W_C, KV_W_C, KV_W_C, W_C,
          D_MODEL, D_MODEL, D_MODEL)
IN_COLS = sum(_SIZES)
SPLIT_POINTS = tuple(sum(_SIZES[:i + 1]) for i in range(len(_SIZES) - 1))

kernel_name = "hybrid_diff_na2d_swa_encoder"

def rms_norm(x, g):
    xf = x.astype(jnp.float32)
    y = xf * lax.rsqrt(jnp.mean(xf * xf, axis=-1, keepdims=True) + EPS)
    return (y * g.astype(jnp.float32)).astype(x.dtype)

def alibi_slopes(n):
    return jnp.asarray(np.array([2.0 ** (-8.0 * (i + 1) / n) for i in range(n)], dtype=np.float32))

def diff_attention(q, k, v, lam, lam_init, subln_g):
    B, T = q.shape[0], q.shape[1]
    nq = T // Q_BLOCK
    slopes = alibi_slopes(H_A)[None, :, None, None, None]
    kpos = jnp.arange(T)
    scale = HEAD_DIM ** -0.5
    qb = q.reshape(B, nq, Q_BLOCK, H_A, 2, HEAD_DIM).transpose(1, 0, 2, 3, 4, 5)

    def block(args):
        qi, i = args
        s = jnp.einsum('bqhcd,bkhcd->bhcqk', qi, k).astype(jnp.float32) * scale
        qpos = i * Q_BLOCK + jnp.arange(Q_BLOCK)
        dist = jnp.abs(qpos[:, None] - kpos[None, :]).astype(jnp.float32)
        p = jax.nn.softmax(s - slopes * dist, axis=-1)
        a = p[:, :, 0] - lam * p[:, :, 1]
        return jnp.einsum('bhqk,bkhe->bqhe', a.astype(v.dtype), v)

    o = lax.map(block, (qb, jnp.arange(nq)))
    o = o.transpose(1, 0, 2, 3, 4).reshape(B, T, H_A, 2 * HEAD_DIM)
    o = rms_norm(o, subln_g) * (1.0 - lam_init)
    return o.reshape(B, T, W_A)

def neighbourhood_attention(q, k, v, rpb):
    B, T = q.shape[0], q.shape[1]
    rows = T // GRID_W
    kh = min(MAX_KH, rows)
    qg = q.reshape(B, rows, GRID_W, H_B, HEAD_DIM)
    kg = k.reshape(B, rows, GRID_W, H_B, HEAD_DIM)
    vg = v.reshape(B, rows, GRID_W, H_B, HEAD_DIM)
    cols = jnp.arange(GRID_W)
    cstart = jnp.clip(cols - KW // 2, 0, GRID_W - KW)
    cidx = cstart[:, None] + jnp.arange(KW)[None, :]
    dc = cidx - cols[:, None] + (KW - 1)
    scale = HEAD_DIM ** -0.5

    def row(r):
        rs = jnp.clip(r - kh // 2, 0, rows - kh)
        q_r = lax.dynamic_index_in_dim(qg, r, axis=1, keepdims=False)
        k_rows = lax.dynamic_slice_in_dim(kg, rs, kh, axis=1)
        v_rows = lax.dynamic_slice_in_dim(vg, rs, kh, axis=1)
        k_n = k_rows[:, :, cidx]
        v_n = v_rows[:, :, cidx]
        dr = rs + jnp.arange(kh) - r + (MAX_KH - 1)
        bias = rpb[:, dr[None, :, None], dc[:, None, :]].astype(jnp.float32)
        s = jnp.einsum('bchd,bicjhd->bhcij', q_r, k_n).astype(jnp.float32) * scale + bias[None]
        p = jax.nn.softmax(s.reshape(B, H_B, GRID_W, kh * KW), axis=-1)
        p = p.reshape(B, H_B, GRID_W, kh, KW).astype(v.dtype)
        return jnp.einsum('bhcij,bicjhd->bchd', p, v_n)

    o = lax.map(row, jnp.arange(rows))
    return o.transpose(1, 0, 2, 3, 4).reshape(B, T, W_B)

def sliding_window_attention(q, k, v, sink):
    B, T = q.shape[0], q.shape[1]
    n = T // BLOCK
    G = H_C // KV_C
    scale = HEAD_DIM ** -0.5

    def band(a):
        ap = jnp.pad(a, ((0, 0), (BLOCK, BLOCK), (0, 0), (0, 0))).reshape(B, n + 2, BLOCK, KV_C, HEAD_DIM)
        return jnp.concatenate([ap[:, :-2], ap[:, 1:-1], ap[:, 2:]], axis=2)

    kb, vb = band(k), band(v)
    qb = q.reshape(B, n, BLOCK, KV_C, G, HEAD_DIM)
    s = jnp.einsum('bnqkgd,bnskd->bnkgqs', qb, kb).astype(jnp.float32) * scale
    qpos = jnp.arange(n)[:, None] * BLOCK + jnp.arange(BLOCK)[None, :]
    kpos = jnp.arange(n)[:, None] * BLOCK - BLOCK + jnp.arange(3 * BLOCK)[None, :]
    dist_i = jnp.abs(qpos[:, :, None] - kpos[:, None, :])
    valid = (dist_i <= WINDOW) & (kpos >= 0)[:, None, :] & (kpos < T)[:, None, :]
    dist = dist_i.astype(jnp.float32)[:, None, None]
    slopes = alibi_slopes(H_C).reshape(KV_C, G)[:, :, None, None]
    s = jnp.where(valid[:, None, None], s - slopes * dist, -1e30)
    sink_col = jnp.broadcast_to(sink.astype(jnp.float32).reshape(KV_C, G)[None, None, :, :, None, None],
                                s.shape[:-1] + (1,))
    p = jax.nn.softmax(jnp.concatenate([s, sink_col], axis=-1), axis=-1)[..., :-1]
    o = jnp.einsum('bnkgqs,bnskd->bnqkgd', p.astype(v.dtype), vb)
    return o.reshape(B, T, W_C)

def trunk(x, norm_g, w_in, qk_gain_a, lambda_a, subln_g_a, qk_gain_b, rpb_b,
          qk_gain_c, sink_c, w_proj_a, w_proj_b, w_proj_c, w_out):
    B, T = x.shape[0], x.shape[1]
    for l in range(DEPTH):
        h = rms_norm(x, norm_g[l])
        p = jnp.einsum('btd,dc->btc', h, w_in[l])
        (qa, ka, va, za, qb, kb, vb, zb, qc, kc, vc, zc,
         ga, gb, gc) = jnp.split(p, SPLIT_POINTS, axis=-1)
        lam_init = 0.8 - 0.6 * math.exp(-0.3 * l)
        lam_vec = lambda_a[l].astype(jnp.float32)
        lam = (jnp.exp(jnp.sum(lam_vec[0] * lam_vec[1])) - jnp.exp(jnp.sum(lam_vec[2] * lam_vec[3]))
               + lam_init)
        qa = rms_norm(qa.reshape(B, T, H_A, 2, HEAD_DIM), qk_gain_a[l, 0])
        ka = rms_norm(ka.reshape(B, T, H_A, 2, HEAD_DIM), qk_gain_a[l, 1])
        oa = diff_attention(qa, ka, va.reshape(B, T, H_A, 2 * HEAD_DIM), lam, lam_init, subln_g_a[l])
        qb = rms_norm(qb.reshape(B, T, H_B, HEAD_DIM), qk_gain_b[l, 0])
        kb = rms_norm(kb.reshape(B, T, H_B, HEAD_DIM), qk_gain_b[l, 1])
        ob = neighbourhood_attention(qb, kb, vb.reshape(B, T, H_B, HEAD_DIM), rpb_b[l])
        qc = rms_norm(qc.reshape(B, T, H_C, HEAD_DIM), qk_gain_c[l, 0])
        kc = rms_norm(kc.reshape(B, T, KV_C, HEAD_DIM), qk_gain_c[l, 1])
        oc = sliding_window_attention(qc, kc, vc.reshape(B, T, KV_C, HEAD_DIM), sink_c[l])
        ya = jnp.einsum('btw,wd->btd', oa * jax.nn.silu(za), w_proj_a[l])
        yb = jnp.einsum('btw,wd->btd', ob * jax.nn.silu(zb), w_proj_b[l])
        yc = jnp.einsum('btw,wd->btd', oc * jax.nn.silu(zc), w_proj_c[l])
        m = jax.nn.sigmoid(ga) * ya + jax.nn.sigmoid(gb) * yb + jax.nn.sigmoid(gc) * yc
        x = x + jnp.einsum('btd,de->bte', m, w_out[l])
    return x

def setup_inputs(seed: int = 0) -> dict:
    key = jax.random.key(seed)
    ks = jax.random.split(key, 16)
    f32 = jnp.float32
    nrm = lambda k, shape, s: (jax.random.normal(k, shape, f32) * s).astype(f32)
    return {
        "x_prompt": nrm(ks[0], (BATCH, SEQ, D_MODEL), 1.0),
        "x_sample": nrm(ks[1], (DEC_BATCH, DEC_SEQ, D_MODEL), 1.0),
        "norm_g": 1.0 + nrm(ks[2], (DEPTH, D_MODEL), 0.1),
        "w_in": nrm(ks[3], (DEPTH, D_MODEL, IN_COLS), D_MODEL ** -0.5),
        "qk_gain_a": 1.0 + nrm(ks[4], (DEPTH, 2, HEAD_DIM), 0.1),
        "lambda_a": nrm(ks[5], (DEPTH, 4, HEAD_DIM), 0.1),
        "subln_g_a": 1.0 + nrm(ks[6], (DEPTH, 2 * HEAD_DIM), 0.1),
        "qk_gain_b": 1.0 + nrm(ks[7], (DEPTH, 2, HEAD_DIM), 0.1),
        "rpb_b": nrm(ks[8], (DEPTH, H_B, 2 * MAX_KH - 1, 2 * KW - 1), 0.5),
        "qk_gain_c": 1.0 + nrm(ks[9], (DEPTH, 2, HEAD_DIM), 0.1),
        "sink_c": nrm(ks[10], (DEPTH, H_C), 1.0),
        "w_proj_a": nrm(ks[11], (DEPTH, W_A, D_MODEL), W_A ** -0.5),
        "w_proj_b": nrm(ks[12], (DEPTH, W_B, D_MODEL), W_B ** -0.5),
        "w_proj_c": nrm(ks[13], (DEPTH, W_C, D_MODEL), W_C ** -0.5),
        "w_out": nrm(ks[14], (DEPTH, D_MODEL, D_MODEL), D_MODEL ** -0.5),
    }

def reference(x_prompt, x_sample, norm_g, w_in, qk_gain_a, lambda_a, subln_g_a, qk_gain_b, rpb_b,
              qk_gain_c, sink_c, w_proj_a, w_proj_b, w_proj_c, w_out):
    y_prompt = trunk(x_prompt, norm_g, w_in, qk_gain_a, lambda_a, subln_g_a, qk_gain_b, rpb_b,
                     qk_gain_c, sink_c, w_proj_a, w_proj_b, w_proj_c, w_out)
    y_sample = trunk(x_sample, norm_g, w_in, qk_gain_a, lambda_a, subln_g_a, qk_gain_b, rpb_b,
                     qk_gain_c, sink_c, w_proj_a, w_proj_b, w_proj_c, w_out)
    return (y_prompt, y_sample)


_drawn_inputs = setup_inputs


def setup_inputs(seed=0):
    import zlib

    import numpy as np

    out = dict(_drawn_inputs(seed))
    spreads = {}
    factors = {'lambda_a': 14.645, 'qk_gain_b': 8.0, 'qk_gain_c': 6.202, 'sink_c': 4.152, 'rpb_b': 3.406}
    for name, (base, spread) in spreads.items():
        noise = np.random.default_rng([zlib.crc32(name.encode()), seed]).standard_normal(out[name].shape)
        drawn = base * np.exp(spread * noise) if base else spread * noise
        out[name] = __import__('jax').numpy.asarray(drawn.astype(out[name].dtype))
    for name, factor in factors.items():
        out[name] = (out[name] * factor).astype(out[name].dtype)
    return out
```

```python
from contextlib import ExitStack

import numpy as np

import concourse.bass as bass
from concourse import mybir

F32 = mybir.dt.float32
F32R = mybir.dt.float32r
ALU = mybir.AluOpType
ACT = mybir.ActivationFunctionType
AX = mybir.AxisListType

P = 128
D = 1024
KD = D // P
T_SAMPLE, T_PROMPT = 2048, 512
TOK = T_SAMPLE + T_PROMPT
BLK = 512
NBLK = TOK // BLK
HD = 64
H_A, H_B, H_C, KV_C = 4, 8, 8, 2
EPS = 1e-6
LAM_INIT = 0.2
NEG = -1e30
GRID_W, MAX_KH, KW = 64, 8, 16
N_NORM, N_V, N_Z, N_G = 21, 9, 12, 24
SEQS = ((0, T_SAMPLE), (T_SAMPLE, T_PROMPT))
BIAS_ROWS, BIAS_COLS = 2 * MAX_KH - 1, 2 * KW - 1
PAD_W = 2 * GRID_W


class Pool:

    def __init__(self, nc, ctx, tag):
        self.nc, self.ctx, self.tag, self.used = nc, ctx, tag, []
        ctx.callback(self.clear)

    def clear(self):
        if self.used:
            self.nc.all_engine_barrier()
            self.nc.clear_and_free_semaphores(self.used)
            self.nc.all_engine_barrier()

    def sb(self, name, shape, dt=F32):
        return self.ctx.enter_context(self.nc.sbuf_tensor(f"{self.tag}_{name}", shape, dt))

    def ps(self, name, shape, dt=F32):
        return self.ctx.enter_context(self.nc.psum_tensor(f"{self.tag}_{name}", shape, dt))

    def sem(self, name):
        self.used.append(self.nc.alloc_semaphore(name=f"{self.tag}_{name}"))
        return self.used[-1]

    def sems(self, name, n):
        return [self.sem(f"{name}{i}") for i in range(n)]


def flat(ap):
    return ap.rearrange("a p n -> (a p) n")


def stage_constants(nc, t, const):
    with ExitStack() as ctx:
        pool = Pool(nc, ctx, "cst")
        loaded, made = pool.sem("loaded"), pool.sem("made")
        exped, stored = pool.sem("exped"), pool.sem("stored")
        lam_in = pool.sb("lam_in", [P, 4, HD])
        lam_prod = pool.sb("lam_prod", [P, 2, HD])
        lam_sum = pool.sb("lam_sum", [P, 2])
        lam_exp = pool.sb("lam_exp", [P, 2])
        ones_f = pool.sb("ones_f", [P, P])
        zeros = pool.sb("zeros", [H_B * BIAS_ROWS, PAD_W])
        rpb = pool.sb("rpb", [H_B * BIAS_ROWS, BIAS_COLS])
        block = ctx.enter_context(nc.Block())
        n_load = 7

        @block.sync
        def _(sp):
            sp.dma_start(const["ident"][:], t["ident"]).then_inc(loaded, 16)
            sp.dma_start(ones_f[:], t["head_ones"]).then_inc(loaded, 16)
            sp.dma_start(const["gains"][:], t["gains"]).then_inc(loaded, 16)
            sp.dma_start(const["sink"][:], bass.AP(t["sink_c"].tensor, 0, [[0, P], [1, H_C]])).then_inc(loaded, 16)
            sp.dma_start(const["subln_g"][:], t["subln_g"].rearrange("a p -> p a")).then_inc(loaded, 16)
            sp.dma_start(lam_in[:], bass.AP(t["lambda_a"].tensor, 0, [[0, P], [HD, 4], [1, HD]])).then_inc(loaded, 16)
            sp.dma_start(rpb[:], t["rpb"]).then_inc(loaded, 16)
            sp.wait_ge(made, 9)
            sp.dma_start(t["rpb_pad"], zeros[:]).then_inc(stored, 16)
            sp.wait_ge(stored, 16)

        @block.vector
        def _(dve):
            dve.wait_ge(loaded, 16 * n_load)
            dve.tensor_copy(const["head_ones"][:], ones_f[:]).then_inc(made, 1)
            for n, (a, b) in enumerate(((4, 8), (12, 16), (20, 21))):
                dve.tensor_scalar(const["gains"][:, a:b], const["gains"][:, a:b], HD ** -0.5, None,
                                  ALU.mult).then_inc(made, 1)
            dve.tensor_scalar(const["subln_g"][:], const["subln_g"][:], 1.0 - LAM_INIT, None,
                              ALU.mult).then_inc(made, 1)
            dve.memset(zeros[:], 0.0).then_inc(made, 1)
            dve.memset(const["eps"][:], EPS).then_inc(made, 1)
            dve.wait_ge(made, 7)
            middle = GRID_W - KW + 1
            dve.tensor_copy(zeros[:, middle:middle + BIAS_COLS], rpb[:]).then_inc(made, 1)
            dve.memset(const["all_ones"][:], 1.0).then_inc(made, 1)
            dve.tensor_tensor(lam_prod[:, 0, :], lam_in[:, 0, :], lam_in[:, 1, :], ALU.mult).then_inc(made, 1)
            dve.tensor_tensor(lam_prod[:, 1, :], lam_in[:, 2, :], lam_in[:, 3, :], ALU.mult).then_inc(made, 1)
            dve.wait_ge(made, 11)
            dve.tensor_reduce(lam_sum[:], lam_prod[:], axis=AX.X, op=ALU.add).then_inc(made, 1)
            dve.wait_ge(exped, 1)
            dve.scalar_tensor_tensor(const["neg_lam"][:], lam_exp[:, 1:2], -LAM_INIT, lam_exp[:, 0:1],
                                     ALU.add, ALU.subtract).then_inc(made, 1)

        @block.scalar
        def _(act):
            act.wait_ge(made, 12)
            act.activation(lam_exp[:], lam_sum[:], ACT.Exp).then_inc(exped, 1)


def stage_normalise(nc, t, const, h_hi, h_lo):
    with ExitStack() as ctx:
        pool = Pool(nc, ctx, "nrm")
        x = [pool.sb(f"x{j}", [P, D]) for j in range(2)]
        h = [pool.sb(f"h{j}", [P, D]) for j in range(2)]
        square = pool.sb("square", [P, D])
        norm_g = pool.sb("norm_g", [P, D])
        g_in = pool.sem("g_in")
        stat = [pool.sb(f"stat{j}", [P, 4]) for j in range(2)]
        bank = [[pool.ps(f"bank{j}{q}", [P, 4, P]) for q in range(2)] for j in range(2)]
        x_in, squared, mean, root = pool.sems("x_in", 2), pool.sem("squared"), pool.sem("mean"), pool.sem("root")
        inv, h_ready, turned = pool.sem("inv"), pool.sem("h_ready"), pool.sem("turned")
        hi_done, lo_done = pool.sem("hi_done"), pool.sem("lo_done")
        block = ctx.enter_context(nc.Block())
        rounds = TOK // P // 2
        x_tiles = t["x"].rearrange("(n p) d -> n p d", p=P)

        @block.sync
        def _(sp):
            sp.dma_start(norm_g[:], bass.AP(t["norm_g"].tensor, 0, [[0, P], [1, D]])).then_inc(g_in, 16)
            with sp.Fori(0, rounds) as i:
                for j in range(2):
                    sp.wait_ge(h_ready, 2 * i)
                    sp.dma_start(x[j][:], flat(x_tiles[bass.ds(2 * i + j, 1)])).then_inc(x_in[j], 16)

        @block.scalar
        def _(act):
            with act.Fori(0, rounds) as i:
                for j in range(2):
                    act.wait_ge(x_in[j], 16 * i + 16)
                    act.wait_ge(squared, 2 * i + j)
                    act.activation(square[:], x[j][:], ACT.Square,
                                   accum_out=stat[j][:, 0:1]).then_inc(squared, 1)
                for j in range(2):
                    act.wait_ge(mean, 2 * i + j + 1)
                    act.activation(stat[j][:, 2:3], stat[j][:, 1:2], ACT.Sqrt).then_inc(root, 1)
                for j in range(2):
                    for q in range(2):
                        act.wait_ge(turned, 4 * i + 2 * j + q + 1)
                        act.activation(h_hi[:, 4 * q:4 * q + 4, bass.ds((2 * i + j) * P, P)],
                                       bank[j][q][:], ACT.Copy).then_inc(hi_done, 1)

        @block.vector
        def _(dve):
            dve.wait_ge(g_in, 16)
            with dve.Fori(0, rounds) as i:
                for j in range(2):
                    dve.wait_ge(squared, 2 * i + j + 1)
                    dve.tensor_scalar(stat[j][:, 1:2], stat[j][:, 0:1], 1.0 / D, EPS,
                                      ALU.mult, ALU.add).then_inc(mean, 1)
                for j in range(2):
                    dve.wait_ge(root, 2 * i + j + 1)
                    dve.reciprocal(stat[j][:, 3:4], stat[j][:, 2:3]).then_inc(inv, 1)
                    dve.wait_ge(inv, 2 * i + j + 1)
                    dve.wait_ge(turned, 4 * i)
                    dve.scalar_tensor_tensor(h[j][:], x[j][:], stat[j][:, 3:4], norm_g[:],
                                             ALU.mult, ALU.mult).then_inc(h_ready, 1)
                for j in range(2):
                    for q in range(2):
                        dve.wait_ge(hi_done, 4 * i + 2 * j + q + 1)
                        cols = bass.ds((2 * i + j) * P, P)
                        dve.tensor_tensor(h_lo[:, 4 * q:4 * q + 4, cols], bank[j][q][:],
                                          h_hi[:, 4 * q:4 * q + 4, cols].bitcast(F32),
                                          ALU.subtract).then_inc(lo_done, 1)

        @block.tensor
        def _(pe):
            with pe.Fori(0, rounds) as i:
                for j in range(2):
                    pe.wait_ge(h_ready, 2 * i + j + 1)
                    pe.wait_ge(lo_done, 4 * i)
                    for q in range(2):
                        for k in range(4):
                            last = pe.transpose(bank[j][q][:, k, :], h[j][:, (4 * q + k) * P:(4 * q + k + 1) * P],
                                                const["ident"][:])
                        last.then_inc(turned, 1)


def stage_project(nc, t, const, h_hi, h_lo, tag, kinds, pairs, first_tile, first_out):
    with ExitStack() as ctx:
        pool = Pool(nc, ctx, tag)
        w_raw = pool.sb("w_raw", [P, KD, P])
        w_hi = [pool.sb(f"w_hi{s}", [P, KD, P], F32R) for s in range(2)]
        w_lo = [pool.sb(f"w_lo{s}", [P, KD, P], F32R) for s in range(2)]
        acc = [pool.ps(f"acc{b}", [P, BLK]) for b in range(NBLK)]
        side = [pool.ps(f"side{s}", [P, BLK]) for s in range(2)]
        out = pool.sb("out", [P, BLK])
        w_in, w_split = pool.sem("w_in"), pool.sem("w_split")
        acc_ready = pool.sems("acc_ready", 2)
        bank_done = pool.sems("bank_done", NBLK)
        side_done, side_read = pool.sem("side_done"), pool.sem("side_read")
        stored = pool.sem("stored")
        if kinds[0] == "norm":
            sq = pool.sb("sq", [P, BLK])
            sq_hi = [pool.sb(f"sq_hi{s}", [P, BLK], F32R) for s in range(2)]
            sq_lo = [pool.sb(f"sq_lo{s}", [P, BLK], F32R) for s in range(2)]
            root = pool.sb("root", [P, BLK])
            qk = pool.sb("qk", [P, BLK])
            qk_hi = [pool.sb(f"qk_hi{s}", [P, BLK], F32R) for s in range(2)]
            qk_lo = [pool.sb(f"qk_lo{s}", [P, BLK], F32R) for s in range(2)]
            sq_ready, sq_split, inv_ready = pool.sem("sq_ready"), pool.sem("sq_split"), pool.sem("inv_ready")
            hi_ready, lo_ready = pool.sem("hi_ready"), pool.sem("lo_ready")
            qk_stored = pool.sems("qk_stored", 2)
        if kinds[0] == "v":
            v_t = [pool.sb(f"v_t{s}", [P, BLK]) for s in range(2)]
            v_out = [pool.sb(f"v_out{s}", [P, BLK]) for s in range(2)]
            v_stored = pool.sems("v_stored", 2)
        block = ctx.enter_context(nc.Block())
        funcs = {"z": ACT.Silu, "g": ACT.Sigmoid}
        dram = {"z": t["z"], "g": t["g"]}
        gates = sum(k in funcs for k in kinds)

        def before(i, b):
            return 5 * i + (b - 1 if b else 0)

        def uses(i, b):
            return (3 * i if b % 2 == 0 else 2 * i) + b // 2

        @block.sync
        def _(sp):
            with sp.Fori(0, pairs) as i:
                for s in range(2):
                    sp.wait_ge(w_split, 2 * (2 * i + s))
                    sp.dma_start(w_raw[:].rearrange("p k c -> p (k c)"),
                                 flat(t["w_in"][bass.ds(2 * i + (first_tile + s), 1)])).then_inc(w_in, 16)

        @block.gpsimd
        def _(pool_e):
            def split_weights(i, s):
                n = 2 * i + s
                pool_e.wait_ge(w_in, 16 * n + 16)
                pool_e.wait_ge(acc_ready[s], NBLK * i)
                halves = [slice(q * KD // 2, (q + 1) * KD // 2) for q in range(2)]
                for q in halves:
                    last = pool_e.tensor_tensor(w_hi[s][:, q, :], w_raw[:, q, :],
                                                const["all_ones"][:].rearrange("p (k c) -> p k c", c=P), ALU.mult)
                last.then_inc(w_split, 1)
                pool_e.wait_ge(w_split, 2 * n + 1)
                pool_e.tensor_tensor(w_lo[s][:], w_raw[:], w_hi[s][:].bitcast(F32),
                                     ALU.subtract).then_inc(w_split, 1)

            def split_squares(i, b):
                m, s = NBLK * i + b, b % 2
                pool_e.wait_ge(sq_ready, m + 1)
                pool_e.wait_ge(side_done, before(i, b))
                pool_e.tensor_tensor(sq_hi[s][:], sq[:], const["all_ones"][:], ALU.mult).then_inc(sq_split, 1)
                pool_e.wait_ge(sq_split, 2 * m + 1)
                pool_e.tensor_tensor(sq_lo[s][:], sq[:], sq_hi[s][:].bitcast(F32),
                                     ALU.subtract).then_inc(sq_split, 1)

            def low_part(i, b):
                m = NBLK * i + b
                pool_e.wait_ge(hi_ready, m + 1)
                pool_e.wait_ge(qk_stored[b % 2], 32 * uses(i, b))
                pool_e.tensor_tensor(qk_lo[b % 2][:], qk[:], qk_hi[b % 2][:].bitcast(F32),
                                     ALU.subtract).then_inc(lo_ready, 1)

            with pool_e.Fori(0, pairs) as i:
                split_weights(i, 0)
                if kinds[0] == "norm":
                    for b in range(NBLK):
                        split_squares(i, b)
                        if b:
                            low_part(i, b - 1)
                        if b == 1:
                            split_weights(i, 1)
                    low_part(i, NBLK - 1)
                else:
                    split_weights(i, 1)

        @block.scalar
        def _(act):
            def square(i, b):
                m = NBLK * i + b
                act.wait_ge(acc_ready[0], m + 1)
                act.wait_ge(sq_split, 2 * m)
                act.activation(sq[:], acc[b][:], ACT.Square).then_inc(sq_ready, 1)

            def root_and_high(i, b):
                m = NBLK * i + b
                act.wait_ge(side_done, m + 1)
                act.wait_ge(inv_ready, m)
                act.activation(root[:], side[b % 2][:], ACT.Sqrt, bias=const["eps"][:],
                               scale=1.0 / HD).then_inc(side_read, 1)
                act.wait_ge(bank_done[b], 2 * i + 1)
                act.wait_ge(qk_stored[b % 2], 32 * uses(i, b))
                act.activation(qk_hi[b % 2][:], qk[:], ACT.Copy).then_inc(hi_ready, 1)

            def store_qk(i, b):
                act.wait_ge(lo_ready, NBLK * i + b + 1)
                cols = slice(b * BLK, (b + 1) * BLK)
                row = bass.ds(i, 1)
                act.dma_start(flat(t["qk_hi"][row, :, cols]), qk_hi[b % 2][:].bitcast(F32)).then_inc(qk_stored[b % 2], 16)
                act.dma_start(flat(t["qk_lo"][row, :, cols]), qk_lo[b % 2][:].bitcast(F32)).then_inc(qk_stored[b % 2], 16)

            def gate(i, s, b):
                act.wait_ge(acc_ready[s], NBLK * i + b + 1)
                turn = s if gates == 2 else 0
                act.wait_ge(stored, 16 * (gates * NBLK * i + (turn * NBLK + b)))
                act.activation(out[:], acc[b][:], funcs[kinds[s]]).then_inc(bank_done[b], 1)
                act.wait_ge(bank_done[b], 2 * i + s + 1)
                act.dma_start(flat(dram[kinds[s]][bass.ds(i + first_out[s], 1), :, b * BLK:(b + 1) * BLK]),
                              out[:]).then_inc(stored, 16)

            def copy_v(i, b):
                act.wait_ge(acc_ready[0], NBLK * i + b + 1)
                act.wait_ge(side_done, before(i, b))
                act.activation(v_t[b % 2][:], acc[b][:], ACT.Copy).then_inc(bank_done[b], 1)

            def store_v(i, b):
                act.wait_ge(side_read, NBLK * i + b + 1)
                act.dma_start(t["v"][b * BLK:(b + 1) * BLK, bass.ds(i * P, P)].rearrange("(n p) c -> p n c", p=P),
                              v_out[b % 2][:].rearrange("p (n c) -> p n c", c=P)).then_inc(v_stored[b % 2], 16)

            with act.Fori(0, pairs) as i:
                if kinds[0] == "norm":
                    for b in range(NBLK):
                        square(i, b)
                        if b:
                            root_and_high(i, b - 1)
                        if b > 1:
                            store_qk(i, b - 2)
                    root_and_high(i, NBLK - 1)
                    store_qk(i, NBLK - 2)
                elif kinds[0] == "v":
                    for b in range(NBLK):
                        copy_v(i, b)
                        if b:
                            store_v(i, b - 1)
                    store_v(i, NBLK - 1)
                else:
                    for b in range(NBLK):
                        gate(i, 0, b)
                for b in range(NBLK):
                    gate(i, 1, b)
                    if b == 0 and kinds[0] == "norm":
                        store_qk(i, NBLK - 1)
            if kinds[0] == "norm":
                act.wait_ge(qk_stored[0], 32 * 3 * pairs)
                act.wait_ge(qk_stored[1], 32 * 2 * pairs)
            if kinds[0] == "v":
                act.wait_ge(v_stored[0], 16 * 3 * pairs)
                act.wait_ge(v_stored[1], 16 * 2 * pairs)
            act.wait_ge(stored, 16 * NBLK * gates * pairs)

        if kinds[0] in ("norm", "v"):
            @block.vector
            def _(dve):
                with dve.Fori(0, pairs) as i:
                    for b in range(NBLK):
                        m = NBLK * i + b
                        if kinds[0] == "norm":
                            dve.wait_ge(side_read, m + 1)
                            dve.wait_ge(lo_ready, m)
                            dve.reciprocal(qk[:], root[:]).then_inc(inv_ready, 1)
                            dve.wait_ge(inv_ready, m + 1)
                            dve.scalar_tensor_tensor(qk[:], acc[b][:], const["gains"][:, bass.ds(i, 1)], qk[:],
                                                     ALU.mult, ALU.mult).then_inc(bank_done[b], 1)
                        else:
                            dve.wait_ge(side_done, m + 1)
                            dve.wait_ge(v_stored[b % 2], 16 * uses(i, b))
                            dve.tensor_copy(v_out[b % 2][:], side[b % 2][:]).then_inc(side_read, 1)

        @block.tensor
        def _(pe):
            def head_sums(i, b):
                m, s = NBLK * i + b, b % 2
                pe.wait_ge(sq_split, 2 * m + 2)
                pe.wait_ge(side_read, before(i, b))
                pe.matmul(side[s][:], const["head_ones"][:], sq_hi[s][:], start=True, stop=False)
                pe.matmul(side[s][:], const["head_ones"][:], sq_lo[s][:], start=False, stop=True).then_inc(side_done, 1)

            def turn_v(i, b):
                s = b % 2
                pe.wait_ge(bank_done[b], 2 * i + 1)
                pe.wait_ge(side_read, before(i, b))
                for n in range(BLK // P):
                    last = pe.transpose(side[s][:, n * P:(n + 1) * P], v_t[s][:, n * P:(n + 1) * P], const["ident"][:])
                last.then_inc(side_done, 1)

            after = {"norm": head_sums, "v": turn_v}.get(kinds[0])
            with pe.Fori(0, pairs) as i:
                for s in range(2):
                    pe.wait_ge(w_split, 2 * (2 * i + s) + 2)
                    for b in range(NBLK):
                        cols = slice(b * BLK, (b + 1) * BLK)
                        pe.wait_ge(bank_done[b], 2 * i + s)
                        for k in range(KD):
                            pe.matmul(acc[b][:], w_hi[s][:, k, :], h_hi[:, k, cols], start=(k == 0), stop=False)
                            pe.matmul(acc[b][:], w_hi[s][:, k, :], h_lo[:, k, cols], start=False, stop=False)
                            last = pe.matmul(acc[b][:], w_lo[s][:, k, :], h_hi[:, k, cols], start=False,
                                             stop=(k == KD - 1))
                        last.then_inc(acc_ready[s], 1)
                        if after and s == 0 and b:
                            after(i, b - 1)
                        if after and s == 1 and b == 0:
                            after(i, NBLK - 1)


def stage_attend_a(nc, t, const, tag, tok0, T):
    nq = T // P
    n_key = T // P
    chunk = min(2 * BLK, T)
    n_chunk = T // chunk
    per_unit = 2 * n_chunk
    groups = T // BLK
    units = 2 * nq
    blocks = units // 2
    head_blocks = blocks // 2
    rounds = H_A // 2
    bias_w = 2 * T - P
    n_dma = 11
    with ExitStack() as ctx:
        pool = Pool(nc, ctx, tag)
        q = [[pool.sb(f"q{s}{c}", [P, T], F32R) for c in range(2)] for s in range(2)]
        k_hi = [[pool.sb(f"k_hi{s}{c}", [P, T], F32R) for c in range(2)] for s in range(2)]
        k_lo = [[pool.sb(f"k_lo{s}{c}", [P, T], F32R) for c in range(2)] for s in range(2)]
        v = [pool.sb(f"v{s}", [P, n_key, P]) for s in range(2)]
        bias = pool.sb("bias", [P, bias_w])
        prob = [[pool.sb(f"prob{s}{c}", [P, T]) for c in range(2)] for s in range(2)]
        stat = [pool.sb(f"stat{s}", [P, 12]) for s in range(2)]
        tick = pool.sb("tick", [P, 2])
        turned = [pool.sb(f"turned{s}", [P, n_key, 2 * P]) for s in range(2)]
        o_sb = [pool.sb(f"o_sb{s}", [P, 2 * P]) for s in range(2)]
        score = [pool.ps(f"score{s}", [P, chunk]) for s in range(2)]
        turn = [pool.ps(f"turn{s}", [P, BLK]) for s in range(2)]
        o_ps = [pool.ps(f"o_ps{s}", [P, BLK]) for s in range(2)]
        bias_in, bias_made = pool.sem("bias_in"), pool.sem("bias_made")
        head_in = pool.sems("head_in", 2)
        scored, masked, max_ready = pool.sem("scored"), pool.sem("masked"), pool.sem("max_ready")
        exp_done, inv0, scaled0 = pool.sem("exp_done"), pool.sem("inv0"), pool.sem("scaled0")
        inv1, factor1, mapped = pool.sem("inv1"), pool.sem("factor1"), pool.sem("mapped")
        turn_done, turn_read = pool.sem("turn_done"), pool.sem("turn_read")
        applied, o_done, o_stored = pool.sems("applied", 2), pool.sem("o_done"), pool.sems("o_stored", 2)
        block = ctx.enter_context(nc.Block())
        toks = slice(tok0, tok0 + T)

        @block.sync
        def _(sp):
            sp.dma_start(bias[:], t["alibi"][:, T_SAMPLE - T:T_SAMPLE - T + bias_w]).then_inc(bias_in, 16)
            with sp.Fori(0, rounds) as g:
                for s in range(2):
                    sp.wait_ge(applied[s], head_blocks * g)
                    q_tile, k_tile = bass.ds(2 * g + s, 1), bass.ds(2 * g + (H_A + s), 1)
                    for c in range(2):
                        rows = slice(c * HD, (c + 1) * HD)
                        hi, lo = t["qk_hi"], t["qk_lo"]
                        sp.dma_start(k_hi[s][c][0:HD, :].bitcast(F32), flat(hi[k_tile, rows, toks])).then_inc(head_in[s], 16)
                        sp.dma_start(k_hi[s][c][HD:P, :].bitcast(F32), flat(hi[k_tile, rows, toks])).then_inc(head_in[s], 16)
                        sp.dma_start(k_lo[s][c][0:HD, :].bitcast(F32), flat(lo[k_tile, rows, toks])).then_inc(head_in[s], 16)
                        sp.dma_start(q[s][c][0:HD, :].bitcast(F32), flat(hi[q_tile, rows, toks])).then_inc(head_in[s], 16)
                        sp.dma_start(q[s][c][HD:P, :].bitcast(F32), flat(lo[q_tile, rows, toks])).then_inc(head_in[s], 16)
                    sp.dma_start(v[s][:], t["v"][toks, bass.ds((2 * g + s) * P, P)].rearrange("(n p) c -> p n c", p=P)).then_inc(head_in[s], 16)

        @block.gpsimd
        def _(pool_e):
            with pool_e.Fori(0, rounds) as g:
                for n in range(blocks):
                    s, at = n // head_blocks, (n % head_blocks) * 2 * P
                    pool_e.wait_ge(o_done, blocks * g + (n + 1))
                    pool_e.dma_start(flat(t["o_a"][bass.ds(2 * g + s, 1), :, tok0 + at:tok0 + at + 2 * P]),
                                     o_sb[n % 2][:]).then_inc(o_stored[n % 2], 16)
            for s in range(2):
                pool_e.wait_ge(o_stored[s], 16 * (blocks // 2) * rounds)

        @block.vector
        def _(dve):
            def scores_of(g, u, c):
                p, st = prob[u % 2][c], stat[u % 2]
                for j in range(n_chunk):
                    n = u * per_unit + c * n_chunk + j
                    dve.wait_ge(scored, g * (units * per_unit) + (n + 1))
                    dve.wait_ge(turn_done, g * (units * groups) + max(u - 1, 0) * groups)
                    dve.memset(tick[:, n % 2:n % 2 + 1], 0.0)
                    at = j * chunk - (u % nq) * P + (T - P)
                    dve.tensor_tensor_reduce(out=p[:, j * chunk:(j + 1) * chunk], in0=score[n % 2][:],
                                             in1=bias[:, at:at + chunk], scale=1.0, scalar=-3e38, op0=ALU.add,
                                             op1=ALU.max, accum_out=st[:, 2 * c + j:2 * c + j + 1]).then_inc(masked, 1)
                n = u * per_unit + (c + 1) * n_chunk
                dve.wait_ge(masked, g * (units * per_unit) + n)
                dve.tensor_reduce(st[:, 4 + c:5 + c], st[:, 2 * c:2 * c + n_chunk], axis=AX.X, op=ALU.max,
                                  negate=True).then_inc(max_ready, 1)

            def combine(g, u):
                st, n = stat[u % 2], units * g + (u + 1)
                dve.wait_ge(exp_done, 2 * n)
                dve.reciprocal(st[:, 9:10], st[:, 7:8]).then_inc(inv1, 1)
                dve.wait_ge(inv1, n)
                dve.tensor_tensor(st[:, 10:11], st[:, 9:10], const["neg_lam"][:], ALU.mult).then_inc(factor1, 1)
                dve.wait_ge(factor1, n)
                dve.wait_ge(scaled0, n)
                dve.scalar_tensor_tensor(prob[u % 2][0][:], prob[u % 2][1][:], st[:, 10:11], prob[u % 2][0][:],
                                         ALU.mult, ALU.add).then_inc(mapped, 1)

            dve.wait_ge(bias_in, 16)
            with dve.Fori(0, rounds) as g:
                for u in range(units + 1):
                    if u < units:
                        if u % nq == 0:
                            dve.tensor_scalar(bias[:], bias[:], 0.25, None, ALU.mult).then_inc(bias_made, 1)
                            dve.wait_ge(bias_made, 2 * g + (u // nq + 1))
                        scores_of(g, u, 0)
                    if u:
                        combine(g, u - 1)
                    if u < units:
                        dve.wait_ge(exp_done, 2 * (units * g + u) + 1)
                        dve.reciprocal(stat[u % 2][:, 8:9], stat[u % 2][:, 6:7]).then_inc(inv0, 1)
                        scores_of(g, u, 1)

        @block.scalar
        def _(act):
            def exponent(g, u, c):
                st, p = stat[u % 2], prob[u % 2][c]
                act.wait_ge(max_ready, 2 * (units * g + u) + (c + 1))
                act.activation(p[:], p[:], ACT.Exp, bias=st[:, 4 + c:5 + c],
                               accum_out=st[:, 6 + c:7 + c]).then_inc(exp_done, 1)

            def take_turned(g, u, which):
                b = u // 2
                s, own = b // head_blocks, b % head_blocks
                for n in which:
                    act.wait_ge(turn_done, g * (units * groups) + u * groups + n + 1)
                    if own >= 2:
                        act.wait_ge(applied[s], head_blocks * g + (own - 1))
                    elif s == 1:
                        act.wait_ge(applied[0], head_blocks * g + (head_blocks - 1 + own))
                    else:
                        act.wait_ge(applied[1], head_blocks * g)
                    act.activation(turned[b % 2][:, 4 * n:4 * n + 4, (u % 2) * P:(u % 2 + 1) * P],
                                   turn[(u * groups + n) % 2][:].rearrange("p (k c) -> p k c", c=P),
                                   ACT.Copy).then_inc(turn_read, 1)

            def take_output(g, b):
                s, own = b // head_blocks, b % head_blocks
                act.wait_ge(applied[s], head_blocks * g + (own + 1))
                act.wait_ge(o_stored[b % 2], 16 * ((blocks // 2) * g + b // 2))
                act.activation(o_sb[b % 2][:], o_ps[b % 2][:, 0:2 * P], ACT.Copy).then_inc(o_done, 1)

            half = groups // 2
            with act.Fori(0, rounds) as g:
                for step in range(units + 4):
                    u = step
                    if step >= 5 and step % 2 == 1:
                        take_output(g, (step - 5) // 2)
                    if u < units:
                        exponent(g, u, 0)
                        act.wait_ge(inv0, units * g + (u + 1))
                        act.activation(prob[u % 2][0][:], prob[u % 2][0][:], ACT.Copy,
                                       scale=stat[u % 2][:, 8:9]).then_inc(scaled0, 1)
                    if 0 < u <= units:
                        take_turned(g, u - 1, range(half))
                    if u < units:
                        exponent(g, u, 1)
                    if 0 < u <= units:
                        take_turned(g, u - 1, range(half, groups))

        @block.tensor
        def _(pe):
            def scores(g, u, j):
                s, qt = u // nq, u % nq
                n = u * per_unit + j
                c, at = j // n_chunk, (j % n_chunk) * chunk
                if qt == 0 and j == 0:
                    pe.wait_ge(head_in[s], 16 * n_dma * (g + 1))
                pe.wait_ge(masked, g * (units * per_unit) + max(n - 1, 0))
                rows = slice(qt * P, (qt + 1) * P)
                for b in range(0, chunk, BLK):
                    pe.matmul(score[n % 2][:, b:b + BLK], q[s][c][:, rows], k_hi[s][c][:, at + b:at + b + BLK],
                              start=True, stop=False)
                    last = pe.matmul(score[n % 2][:, b:b + BLK], q[s][c][0:HD, rows],
                                     k_lo[s][c][0:HD, at + b:at + b + BLK], start=False, stop=True)
                last.then_inc(scored, 1)

            def turn_maps(g, u, n):
                gid = u * groups + n
                pe.wait_ge(mapped, units * g + (u + 1))
                pe.wait_ge(turn_read, g * (units * groups) + max(gid - 1, 0))
                for k in range(4):
                    at = (4 * n + k) * P
                    last = pe.transpose(turn[gid % 2][:, k * P:(k + 1) * P], prob[u % 2][0][:, at:at + P],
                                        const["ident"][:])
                last.then_inc(turn_done, 1)

            def apply(g, b, piece):
                s = b // head_blocks
                if piece == 0:
                    pe.wait_ge(turn_read, g * (units * groups) + (2 * b + 2) * groups)
                    pe.wait_ge(o_done, blocks * g + max(b - 1, 0))
                for k in range(piece * n_key // 8, (piece + 1) * n_key // 8):
                    last = pe.matmul(o_ps[b % 2][:, 0:2 * P], v[s][:, k, :], turned[b % 2][:, k, :],
                                     start=(k == 0), stop=(k == n_key - 1))
                if piece == 7:
                    last.then_inc(applied[s], 1)

            with pe.Fori(0, rounds) as g:
                for step in range(units + 3):
                    for j in range(4):
                        if step < units and j < per_unit:
                            scores(g, step, j)
                        if 0 < step <= units:
                            for n in range(groups):
                                if j == (3 if groups == 1 else 2 + n // (groups // 2)):
                                    turn_maps(g, step - 1, n)
                        if step >= 3:
                            apply(g, (step - 3) // 2, 4 * ((step - 3) % 2) + j)


def stage_attend_window(nc, t, const, tag, tok0, T, heads, per_round, q_tile, k_of, v_col, o_col, window,
                        width, tables, sink):
    nt = T // P
    units = per_round * nt
    rounds = heads // per_round
    shared = sink
    n_kv = 1 if shared else per_round
    n_in = 2 + (0 if shared else 4)
    with ExitStack() as ctx:
        pool = Pool(nc, ctx, tag)
        q = [pool.sb(f"q{s}", [P, T], F32R) for s in range(per_round)]
        k_hi = [pool.sb(f"k_hi{s}", [P, T], F32R) for s in range(n_kv)]
        k_lo = [pool.sb(f"k_lo{s}", [P, T], F32R) for s in range(n_kv)]
        v = [pool.sb(f"v{s}", [P, nt, HD]) for s in range(n_kv)]
        table = [pool.sb(f"table{s}", [P, tables["width"]]) for s in range(2)]
        prob = [pool.sb(f"prob{s}", [P, width]) for s in range(3)]
        turned = [pool.sb(f"turned{s}", [P, width]) for s in range(2)]
        stat = [pool.sb(f"stat{s}", [P, 6]) for s in range(6)]
        sinks = pool.sb("sinks", [P, per_round])
        tick = pool.sb("tick", [P, 1])
        o_sb = pool.sb("o_sb", [P, nt, per_round * HD])
        score = [pool.ps(f"score{s}", [P, 2 * BLK]) for s in range(2)]
        turn = pool.ps("turn", [P, 2 * BLK])
        o_ps = [pool.ps(f"o_ps{s}", [P, BLK]) for s in range(2)]
        q_in = pool.sems("q_in", per_round)
        kv_in = pool.sems("kv_in", n_kv)
        tab_done, sink_done = pool.sem("tab_done"), pool.sem("sink_done")
        scored, masked, max_ready = pool.sem("scored"), pool.sem("masked"), pool.sem("max_ready")
        exp_done, sum_done, inv = pool.sem("exp_done"), pool.sem("sum_done"), pool.sem("inv")
        turn_done, read_a, read_b = pool.sem("turn_done"), pool.sem("read_a"), pool.sem("read_b")
        applied, o_done, o_stored = pool.sem("applied"), pool.sem("o_done"), pool.sem("o_stored")
        block = ctx.enter_context(nc.Block())
        toks = slice(tok0, tok0 + T)
        two_banks = width > BLK
        per_exp = 2 if sink else 1

        @block.sync
        def _(sp):
            with sp.Fori(0, rounds) as g:
                sp.wait_ge(applied, units * g)
                for s in range(per_round):
                    if s < n_kv:
                        k_tile, k_rows, v_cols = k_of(g, s)
                        for dst, src in ((k_hi[s][0:HD, :], t["qk_hi"]), (k_hi[s][HD:P, :], t["qk_hi"]),
                                         (k_lo[s][0:HD, :], t["qk_lo"])):
                            sp.dma_start(dst.bitcast(F32), flat(src[k_tile, k_rows, toks])).then_inc(kv_in[s], 16)
                        sp.dma_start(v[s][:], t["v"][toks, v_cols].rearrange("(n p) c -> p n c", p=P)).then_inc(kv_in[s], 16)
                    tile = bass.ds(g * (per_round // 2) + (q_tile + s // 2), 1)
                    rows = slice((s % 2) * HD, (s % 2 + 1) * HD)
                    sp.dma_start(q[s][0:HD, :].bitcast(F32), flat(t["qk_hi"][tile, rows, toks])).then_inc(q_in[s], 16)
                    sp.dma_start(q[s][HD:P, :].bitcast(F32), flat(t["qk_lo"][tile, rows, toks])).then_inc(q_in[s], 16)

        @block.gpsimd
        def _(pool_e):
            with pool_e.Fori(0, rounds) as g:
                pool_e.wait_ge(o_done, units * (g + 1))
                dst = t["o_win"][toks, bass.ds(g * (per_round * HD) + o_col, per_round * HD)]
                pool_e.dma_start(dst.rearrange("(n p) c -> p n c", p=P), o_sb[:]).then_inc(o_stored, 16)
            pool_e.wait_ge(o_stored, 16 * rounds)

        @block.vector
        def _(dve):
            def scores_of(g, u):
                s, n = u // nt, u % nt
                first, count, col = window(n)
                w = count * P
                dve.wait_ge(scored, units * g + (u + 1))
                dve.wait_ge(turn_done, units * g + max(u - 2, 0))
                dve.memset(tick[:], 0.0)
                dve.tensor_tensor_reduce(out=prob[u % 3][:, 0:w], in0=score[u % 2][:, 0:w],
                                         in1=table[s % 2][:, col:col + w], scale=1.0,
                                         scalar=(sinks[:, s:s + 1] if sink else -3e38), op0=ALU.add, op1=ALU.max,
                                         accum_out=stat[u % 6][:, 0:1]).then_inc(masked, 1)
                dve.wait_ge(masked, units * g + (u + 1))
                dve.tensor_scalar(stat[u % 6][:, 1:2], stat[u % 6][:, 0:1], -1.0, None, ALU.mult).then_inc(max_ready, 1)

            def take_turned(g, u):
                w = window(u % nt)[1] * P
                lo, hi = (BLK, w) if two_banks else (0, w)
                if lo < hi:
                    dve.wait_ge(turn_done, units * g + (u + 1))
                    dve.wait_ge(applied, units * g + max(u - 1, 0))
                    dve.tensor_copy(turned[u % 2][:, lo:hi], turn[:, lo:hi]).then_inc(read_b, 1)

            def take_output(g, u):
                st = stat[u % 6]
                if sink:
                    dve.wait_ge(exp_done, 2 * (units * g) + 2 * (u + 1))
                    dve.tensor_tensor(st[:, 2:3], st[:, 2:3], st[:, 3:4], ALU.add).then_inc(sum_done, 1)
                    dve.wait_ge(sum_done, units * g + (u + 1))
                else:
                    dve.wait_ge(exp_done, units * g + (u + 1))
                dve.reciprocal(st[:, 4:5], st[:, 2:3]).then_inc(inv, 1)
                dve.wait_ge(inv, units * g + (u + 1))
                dve.wait_ge(applied, units * g + (u + 1))
                dve.wait_ge(o_stored, 16 * g)
                s, n = u // nt, u % nt
                dve.tensor_scalar(o_sb[:, n, s * HD:(s + 1) * HD], o_ps[u % 2][:, 0:HD], st[:, 4:5], None,
                                  ALU.mult).then_inc(o_done, 1)

            tables["load"](dve)
            with dve.Fori(0, rounds) as g:
                if sink:
                    dve.tensor_copy(sinks[:], const["sink"][:, bass.ds(g * per_round, per_round)]).then_inc(sink_done, 1)
                    dve.wait_ge(sink_done, g + 1)
                for step in range(units + 4):
                    if 3 <= step < units + 3:
                        take_turned(g, step - 3)
                    if step < units:
                        if step % nt == 0:
                            s = step // nt
                            tables["make"](dve, g, s, per_round, table[s % 2], tab_done)
                        scores_of(g, step)
                    if step >= 4:
                        take_output(g, step - 4)

        @block.scalar
        def _(act):
            with act.Fori(0, rounds) as g:
                for step in range(units + 3):
                    if step >= 3 and two_banks:
                        u = step - 3
                        w = min(window(u % nt)[1] * P, BLK)
                        act.wait_ge(turn_done, units * g + (u + 1))
                        act.wait_ge(applied, units * g + max(u - 1, 0))
                        act.activation(turned[u % 2][:, 0:w], turn[:, 0:w], ACT.Copy).then_inc(read_a, 1)
                    u = step
                    if u < units:
                        s, w, st = u // nt, window(u % nt)[1] * P, stat[u % 6]
                        act.wait_ge(max_ready, units * g + (u + 1))
                        act.activation(prob[u % 3][:, 0:w], prob[u % 3][:, 0:w], ACT.Exp, bias=st[:, 1:2],
                                       accum_out=st[:, 2:3]).then_inc(exp_done, 1)
                        if sink:
                            act.activation(st[:, 3:4], sinks[:, s:s + 1], ACT.Exp, bias=st[:, 1:2]).then_inc(exp_done, 1)

        @block.tensor
        def _(pe):
            wide = [sum(window(m % nt)[1] * P > (BLK if two_banks else 0) for m in range(u)) for u in range(units + 1)]

            def wait_read(g, done):
                if two_banks:
                    pe.wait_ge(read_a, units * g + done)
                if wide[units]:
                    pe.wait_ge(read_b, wide[units] * g + wide[done])

            with pe.Fori(0, rounds) as g:
                for step in range(units + 3):
                    if step < units:
                        u, s = step, step // nt
                        kv = 0 if shared else s
                        n = u % nt
                        first, count, _ = window(n)
                        if n == 0:
                            pe.wait_ge(q_in[s], 32 * (g + 1))
                            if s < n_kv:
                                pe.wait_ge(kv_in[s], 64 * (g + 1))
                        pe.wait_ge(masked, units * g + max(u - 1, 0))
                        rows = slice(n * P, (n + 1) * P)
                        for a in range(0, count * P, BLK):
                            w = min(BLK, count * P - a)
                            at = first * P + a
                            pe.matmul(score[u % 2][:, a:a + w], q[s][:, rows], k_hi[kv][:, at:at + w],
                                      start=True, stop=False)
                            last = pe.matmul(score[u % 2][:, a:a + w], q[s][0:HD, rows], k_lo[kv][0:HD, at:at + w],
                                             start=False, stop=True)
                        last.then_inc(scored, 1)
                    if 2 <= step < units + 2:
                        u = step - 2
                        pe.wait_ge(exp_done, per_exp * (units * g) + per_exp * u + 1)
                        wait_read(g, u)
                        for k in range(window(u % nt)[1]):
                            last = pe.transpose(turn[:, k * P:(k + 1) * P], prob[u % 3][:, k * P:(k + 1) * P],
                                                const["ident"][:])
                        last.then_inc(turn_done, 1)
                    if step >= 3:
                        u = step - 3
                        kv = 0 if shared else u // nt
                        first, count, _ = window(u % nt)
                        wait_read(g, u + 1)
                        pe.wait_ge(o_done, units * g + max(u - 1, 0))
                        for k in range(count):
                            last = pe.matmul(o_ps[u % 2][:, 0:HD], turned[u % 2][:, k * P:(k + 1) * P],
                                             v[kv][:, first + k, :], start=(k == 0), stop=(k == count - 1))
                        last.then_inc(applied, 1)


def stage_attend_grid(nc, t, const):
    full, inner = 14 * GRID_W, 10 * GRID_W
    with ExitStack() as ctx:
        pool = Pool(nc, ctx, "grid")
        bias = pool.sb("bias", [P, H_B, full])
        col_mask = pool.sb("col_mask", [P, full])
        row_mask = pool.sb("row_mask", [P, inner])
        with ExitStack() as load:
            first = Pool(nc, load, "gridload")
            raw = first.sb("raw", [P, H_B, 14, GRID_W])
            loaded, made = first.sem("loaded"), first.sem("made")
            block = load.enter_context(nc.Block())

            @block.sync
            def _(sp):
                sp.dma_start(col_mask[:], t["col_mask"]).then_inc(loaded, 16)
                sp.dma_start(row_mask[:], t["row_mask"]).then_inc(loaded, 16)
                for h in range(H_B):
                    for a in range(2):
                        start = (h * BIAS_ROWS + 1 - a) * PAD_W + 1
                        src = bass.AP(t["rpb_pad"].tensor, start, [[1, GRID_W], [PAD_W, 14], [1, GRID_W]])
                        sp.dma_start(raw[a * GRID_W:(a + 1) * GRID_W, h, :, :], src).then_inc(loaded, 16)

            @block.vector
            def _(dve):
                dve.wait_ge(loaded, 16 * (2 + 2 * H_B))
                for h in range(H_B):
                    dve.tensor_tensor(bias[:, h, :].rearrange("p (e c) -> p e c", c=GRID_W), raw[:, h, :, ::-1],
                                      col_mask[:].rearrange("p (e c) -> p e c", c=GRID_W), ALU.add).then_inc(made, 1)
                dve.wait_ge(made, H_B)

        def make(dve, g, s, per_round, table, done):
            n = 2 * per_round * g + 2 * s
            dve.tensor_copy(table[:, 0:full], bias[:, bass.ds(g * per_round + s, 1), :].rearrange("p a n -> p (a n)")
                            ).then_inc(done, 1)
            dve.wait_ge(done, n + 1)
            dve.tensor_tensor(table[:, full:full + inner], table[:, 2 * GRID_W:2 * GRID_W + inner], row_mask[:],
                              ALU.add).then_inc(done, 1)
            dve.wait_ge(done, n + 2)

        for tag, (tok0, T) in zip(("gs", "gp"), SEQS):
            nt = T // P
            tables = {"width": full + inner, "load": lambda dve: None, "make": make}

            def window(n, nt=nt):
                if nt > 4 and 2 <= n < nt - 2:
                    return n - 2, 5, full
                first = 0 if n < nt - 2 or nt == 4 else nt - 4
                return first, 4, (first - n + 3) * P

            def k_of(g, s):
                return (bass.ds(g + 12, 1), slice(s * HD, (s + 1) * HD), bass.ds(g * P + (512 + s * HD), HD))

            stage_attend_window(nc, t, const, tag, tok0, T, H_B, 2, 8, k_of, 512, 0, window, 5 * P, tables, False)


def stage_attend_slide(nc, t, const):
    with ExitStack() as ctx:
        pool = Pool(nc, ctx, "slide")
        mask = pool.sb("mask", [P, 3 * P])
        for tag, (tok0, T) in zip(("ss", "sp"), SEQS):
            with ExitStack() as own:
                inner = Pool(nc, own, tag + "t")
                dist = inner.sb("dist", [P, 3 * P])
                loaded = inner.sem("loaded")

                def load(dve):
                    dve.wait_ge(loaded, 32)

                def make(dve, g, s, per_round, table, done):
                    n = 2 * per_round * g + 2 * s
                    dve.tensor_scalar(dist[:], dist[:], 0.5, None, ALU.mult).then_inc(done, 1)
                    dve.wait_ge(done, n + 1)
                    dve.tensor_tensor(table[:], dist[:], mask[:], ALU.add).then_inc(done, 1)
                    dve.wait_ge(done, n + 2)

                with nc.Block() as block:
                    @block.sync
                    def _(sp):
                        sp.dma_start(dist[:], t["slide_dist"]).then_inc(loaded, 16)
                        sp.dma_start(mask[:], t["slide_mask"]).then_inc(loaded, 16)
                        sp.wait_ge(loaded, 32)

                nt = T // P

                def window(n, nt=nt):
                    first, end = max(n - 1, 0), min(n + 2, nt)
                    return first, end - first, (first - n + 1) * P

                def k_of(g, s):
                    return slice(20, 21), bass.ds(g * HD, HD), bass.ds(g * HD + 1024, HD)

                tables = {"width": 3 * P, "load": load, "make": make}
                stage_attend_window(nc, t, const, tag, tok0, T, H_C, 4, 16, k_of, 1024, H_B * HD, window, 3 * P,
                                    tables, True)


def stage_merge(nc, t, const):
    n_u = 12
    row_tiles = BLK // P
    halves = D // BLK
    with ExitStack() as ctx:
        pool = Pool(nc, ctx, "mrg")
        wo_hi = pool.sb("wo_hi", [P, KD, D], F32R)
        wo_lo = pool.sb("wo_lo", [P, KD, D], F32R)
        wp_raw = pool.sb("wp_raw", [P, n_u * P])
        wp_hi = [pool.sb(f"wp_hi{s}", [P, n_u, P], F32R) for s in range(2)]
        wp_lo = [pool.sb(f"wp_lo{s}", [P, n_u, P], F32R) for s in range(2)]
        u_hi = pool.sb("u_hi", [P, n_u, BLK], F32R)
        u_lo = pool.sb("u_lo", [P, n_u, BLK], F32R)
        m_hi = pool.sb("m_hi", [P, KD, BLK], F32R)
        m_lo = pool.sb("m_lo", [P, KD, BLK], F32R)
        o_in = [pool.sb(f"o_in{s}", [P, BLK]) for s in range(2)]
        z_in = [pool.sb(f"z_in{s}", [P, BLK]) for s in range(2)]
        root = pool.sb("root", [P, BLK])
        inv = pool.sb("inv", [P, BLK])
        u = pool.sb("u", [P, BLK])
        g_in = pool.sb("g_in", [P, 3, BLK])
        m = pool.sb("m", [P, BLK])
        part = pool.sb("part", [P, BLK])
        xy = [pool.sb(f"xy{s}", [P, BLK]) for s in range(2)]
        acc = [pool.ps(f"acc{b}", [P, BLK]) for b in range(3)]
        y_ps = [pool.ps(f"y_ps{s}", [P, BLK]) for s in range(2)]
        prep = [pool.ps(f"prep{s}", [P, BLK]) for s in range(2)]
        wo_in, wo_split = pool.sem("wo_in"), pool.sem("wo_split")
        wp_in, wp_high, wp_low = pool.sem("wp_in"), pool.sem("wp_high"), pool.sem("wp_low")
        oz_in = pool.sems("oz_in", 2)
        squared, summed, rooted, inverted, normed = (pool.sem(n) for n in ("squared", "summed", "rooted", "inverted", "normed"))
        summed_t = pool.sem("summed_t")
        u_made, u_high, u_low = pool.sem("u_made"), pool.sem("u_high"), pool.sem("u_low")
        acc_ready, gated, g_loaded = pool.sem("acc_ready"), pool.sem("gated"), pool.sem("g_loaded")
        m_high, m_low = pool.sem("m_high"), pool.sem("m_low")
        x_in, y_ready, y_added, y_stored = pool.sems("x_in", 2), pool.sem("y_ready"), pool.sem("y_added"), pool.sems("y_stored", 2)
        block = ctx.enter_context(nc.Block())
        y_jobs = [(r, e) for r in range(row_tiles) for e in range(halves)]
        last_blk = NBLK - 1

        def preps(j):
            return [2 * (j - 2), 2 * (j - 2) + 1] if j >= 2 else []



        @block.sync
        def _(sp):
            def load_prep(i, n):
                s = n % 2
                sp.wait_ge(u_made, n_u * i + max(n - 1, 0))
                cols = bass.ds(i * BLK, BLK)
                if n < H_A:
                    sp.dma_start(o_in[s][:], t["o_a"][n, :, cols]).then_inc(oz_in[s], 16)
                else:
                    c = (n - H_A) * P
                    sp.dma_start(o_in[s][:].rearrange("p (r c) -> p r c", c=P),
                                 t["o_win"][cols, c:c + P].rearrange("(r p) c -> p r c", p=P)).then_inc(oz_in[s], 16)
                sp.dma_start(z_in[s][:], t["z"][n, :, cols]).then_inc(oz_in[s], 16)

            def load_tile(i, d):
                n = KD * i + d
                sp.wait_ge(wp_low, n)
                sp.wait_ge(wp_high, n)
                sp.dma_start(wp_raw[:], t["w_proj"][d]).then_inc(wp_in, 16)
                sp.wait_ge(gated, 5 * n)
                for b in range(3):
                    sp.dma_start(g_in[:, b, :], t["g"][b * KD + d, :, bass.ds(i * BLK, BLK)]).then_inc(g_loaded, 16)

            def load_x(i, j):
                r, e = y_jobs[j]
                sp.wait_ge(y_stored[j % 2], 16 * (4 * i + j // 2))
                rows = bass.ds(i * BLK + r * P, P)
                sp.dma_start(xy[j % 2][:], t["x"][rows, e * BLK:(e + 1) * BLK]).then_inc(x_in[j % 2], 16)

            def round_of(i, last):
                for d in range(KD):
                    load_tile(i, d)
                for j in range(len(y_jobs)):
                    load_x(i, j)
                    if not last:
                        for n in preps(j):
                            load_prep(i + 1, n)

            for k in range(KD):
                sp.wait_ge(wo_split, 2 * k)
                sp.dma_start(wp_raw[:, 0:D], t["w_out"][k]).then_inc(wo_in, 16)
            sp.wait_ge(wo_split, 2 * KD)
            for n in range(n_u):
                load_prep(0, n)
            with sp.Fori(0, last_blk) as i:
                round_of(i, False)
            round_of(last_blk, True)

        @block.gpsimd
        def _(pool_e):
            def low_u(i, n):
                pool_e.wait_ge(u_high, n_u * i + (n + 1))
                pool_e.tensor_tensor(u_lo[:, n, :], u[:], u_hi[:, n, :].bitcast(F32), ALU.subtract).then_inc(u_low, 1)

            def round_of(i, last):
                for d in range(KD):
                    n = KD * i + d
                    pool_e.wait_ge(wp_high, n + 1)
                    pool_e.tensor_tensor(wp_lo[d % 2][:], wp_raw[:].rearrange("p (k c) -> p k c", c=P),
                                         wp_hi[d % 2][:].bitcast(F32), ALU.subtract).then_inc(wp_low, 1)
                if not last:
                    for n in range(n_u):
                        low_u(i + 1, n)

            for k in range(KD):
                pool_e.wait_ge(wo_split, 2 * k + 1)
                pool_e.tensor_tensor(wo_lo[:, k, :], wp_raw[:, 0:D], wo_hi[:, k, :].bitcast(F32),
                                     ALU.subtract).then_inc(wo_split, 1)
            for n in range(n_u):
                low_u(0, n)
            with pool_e.Fori(0, last_blk) as i:
                round_of(i, False)
            round_of(last_blk, True)

        @block.scalar
        def _(act):
            def prepare(i, n):
                at, s = n_u * i + n, n % 2
                if n < H_A:
                    act.wait_ge(oz_in[s], 32 * (n_u // 2) * i + 32 * (n // 2 + 1))
                    act.wait_ge(inverted, H_A * i + n)
                    act.activation(root[:], o_in[s][:], ACT.Square).then_inc(squared, 1)
                    act.wait_ge(summed, H_A * i + n + 1)
                    act.activation(root[:], prep[s][:], ACT.Sqrt, bias=const["eps"][:], scale=1.0 / P).then_inc(rooted, 1)
                act.wait_ge(u_made, at + 1)
                act.activation(u_hi[:, n, :], u[:], ACT.Copy).then_inc(u_high, 1)

            def round_of(i, last):
                for d in range(KD):
                    n = KD * i + d
                    act.wait_ge(wp_in, 16 * (n + 1))
                    act.wait_ge(acc_ready, 24 * i + 3 * max(d - 1, 0))
                    act.activation(wp_hi[d % 2][:], wp_raw[:].rearrange("p (k c) -> p k c", c=P),
                                   ACT.Copy).then_inc(wp_high, 1)
                    if d:
                        high_m(i, d - 1)
                high_m(i, KD - 1)
                for j in range(len(y_jobs)):
                    if not last:
                        for n in preps(j):
                            prepare(i + 1, n)
                    if j:
                        store_y(i, j - 1)
                store_y(i, len(y_jobs) - 1)

            def high_m(i, d):
                act.wait_ge(gated, 5 * (KD * i + d) + 5)
                act.activation(m_hi[:, d, :], m[:], ACT.Copy).then_inc(m_high, 1)

            def store_y(i, j):
                r, e = y_jobs[j]
                act.wait_ge(y_added, 8 * i + j + 1)
                act.dma_start(t["y"][bass.ds(i * BLK + r * P, P), e * BLK:(e + 1) * BLK], xy[j % 2][:]).then_inc(y_stored[j % 2], 16)

            for k in range(KD):
                act.wait_ge(wo_in, 16 * (k + 1))
                act.activation(wo_hi[:, k, :], wp_raw[:, 0:D], ACT.Copy).then_inc(wo_split, 1)
            for n in range(n_u):
                prepare(0, n)
            with act.Fori(0, last_blk) as i:
                round_of(i, False)
            round_of(last_blk, True)
            for s in range(2):
                act.wait_ge(y_stored[s], 16 * (len(y_jobs) // 2) * NBLK)

        @block.vector
        def _(dve):
            def prepare(i, n):
                at, s = n_u * i + n, n % 2
                if n < H_A:
                    dve.wait_ge(rooted, H_A * i + n + 1)
                    dve.wait_ge(u_low, at)
                    dve.reciprocal(inv[:], root[:]).then_inc(inverted, 1)
                    dve.wait_ge(inverted, H_A * i + n + 1)
                    dve.scalar_tensor_tensor(inv[:], o_in[s][:], const["subln_g"][:], inv[:],
                                             ALU.mult, ALU.mult).then_inc(normed, 1)
                    dve.wait_ge(normed, H_A * i + n + 1)
                    dve.tensor_tensor(u[:], inv[:], z_in[s][:], ALU.mult).then_inc(u_made, 1)
                else:
                    dve.wait_ge(summed_t, (n_u - H_A) * i + (n - H_A) + 1)
                    dve.wait_ge(u_low, at)
                    dve.tensor_tensor(u[:], prep[s][:], z_in[s][:], ALU.mult).then_inc(u_made, 1)

            def merge_tile(i, d):
                n = KD * i + d
                dve.wait_ge(g_loaded, 48 * (n + 1))
                dve.wait_ge(m_low, n)
                for b in range(3):
                    dve.wait_ge(acc_ready, 3 * n + b + 1)
                    dve.tensor_tensor((part if b else m)[:], acc[b][:], g_in[:, b, :], ALU.mult).then_inc(gated, 1)
                    dve.wait_ge(gated, 5 * n + (1, 2, 4)[b])
                    if b:
                        dve.tensor_tensor(m[:], m[:], part[:], ALU.add).then_inc(gated, 1)
                        dve.wait_ge(gated, 5 * n + (3 if b == 1 else 5))
                dve.wait_ge(m_high, n + 1)
                dve.tensor_tensor(m_lo[:, d, :], m[:], m_hi[:, d, :].bitcast(F32), ALU.subtract).then_inc(m_low, 1)

            def round_of(i, last):
                for d in range(KD):
                    merge_tile(i, d)
                for j in range(len(y_jobs)):
                    dve.wait_ge(y_ready, 8 * i + j + 1)
                    dve.wait_ge(x_in[j % 2], 16 * (4 * i + j // 2 + 1))
                    dve.tensor_tensor(xy[j % 2][:], y_ps[j % 2][:], xy[j % 2][:], ALU.add).then_inc(y_added, 1)
                    if not last:
                        for n in preps(j):
                            prepare(i + 1, n)

            for n in range(n_u):
                prepare(0, n)
            with dve.Fori(0, last_blk) as i:
                round_of(i, False)
            round_of(last_blk, True)

        @block.tensor
        def _(pe):
            def prepare(i, n):
                at, s = n_u * i + n, n % 2
                pe.wait_ge(u_made, n_u * i + max(n - 1, 0))
                if n < H_A:
                    pe.wait_ge(squared, H_A * i + n + 1)
                    pe.matmul(prep[s][:], const["all_ones"][:, 0:P], root[:], start=True, stop=True).then_inc(summed, 1)
                else:
                    pe.wait_ge(oz_in[s], 32 * (n_u // 2) * i + 32 * (n // 2 + 1))
                    for r in range(row_tiles):
                        last = pe.transpose(prep[s][:, r * P:(r + 1) * P], o_in[s][:, r * P:(r + 1) * P], const["ident"][:])
                    last.then_inc(summed_t, 1)

            def round_of(i, last):
                pe.wait_ge(u_low, n_u * i + n_u)
                for d in range(KD):
                    n = KD * i + d
                    pe.wait_ge(wp_low, n + 1)
                    for b in range(3):
                        pe.wait_ge(gated, 5 * KD * i + (5 * (d - 1) + (1, 2, 4)[b] if d else 0))
                        for k in range(4):
                            w = 4 * b + k
                            pe.matmul(acc[b][:], wp_hi[d % 2][:, w, :], u_hi[:, w, :], start=(k == 0), stop=False)
                            pe.matmul(acc[b][:], wp_hi[d % 2][:, w, :], u_lo[:, w, :], start=False, stop=False)
                            mm = pe.matmul(acc[b][:], wp_lo[d % 2][:, w, :], u_hi[:, w, :], start=False, stop=(k == 3))
                        mm.then_inc(acc_ready, 1)
                for j, (r, e) in enumerate(y_jobs):
                    if j == 0:
                        pe.wait_ge(m_low, KD * (i + 1))
                    pe.wait_ge(y_added, 8 * i + max(j - 1, 0))
                    rows, cols = slice(r * P, (r + 1) * P), slice(e * BLK, (e + 1) * BLK)
                    for k in range(KD):
                        pe.matmul(y_ps[j % 2][:], m_hi[:, k, rows], wo_hi[:, k, cols], start=(k == 0), stop=False)
                        pe.matmul(y_ps[j % 2][:], m_hi[:, k, rows], wo_lo[:, k, cols], start=False, stop=False)
                        mm = pe.matmul(y_ps[j % 2][:], m_lo[:, k, rows], wo_hi[:, k, cols], start=False, stop=(k == KD - 1))
                    mm.then_inc(y_ready, 1)
                    if not last:
                        for n in preps(j):
                            prepare(i + 1, n)

            for n in range(n_u):
                prepare(0, n)
            with pe.Fori(0, last_blk) as i:
                round_of(i, False)
            round_of(last_blk, True)


def scratch(nc, t):
    def dram(name, shape):
        t[name] = nc.dram_tensor(name, shape, F32, kind="Internal").ap()
    dram("qk_hi", [N_NORM, P, TOK])
    dram("qk_lo", [N_NORM, P, TOK])
    dram("v", [TOK, N_V * P])
    dram("z", [N_Z, P, TOK])
    dram("g", [N_G, P, TOK])
    dram("o_a", [H_A, P, TOK])
    dram("o_win", [TOK, (H_B + H_C) * HD])
    dram("rpb_pad", [H_B * BIAS_ROWS, PAD_W])


def build_program(nc, t):
    scratch(nc, t)
    with ExitStack() as ctx:
        keep = Pool(nc, ctx, "keep")
        const = {
            "ident": keep.sb("ident", [P, P]), "head_ones": keep.sb("head_ones", [P, P], F32R),
            "all_ones": keep.sb("all_ones", [P, BLK]), "gains": keep.sb("gains", [P, N_NORM]),
            "sink": keep.sb("sink", [P, H_C]), "subln_g": keep.sb("subln_g", [P, 1]),
            "eps": keep.sb("eps", [P, 1]), "neg_lam": keep.sb("neg_lam", [P, 1]),
        }
        with ExitStack() as first:
            early = Pool(nc, first, "early")
            stage_constants(nc, t, const)
            h_hi = early.sb("h_hi", [P, KD, TOK], F32R)
            h_lo = early.sb("h_lo", [P, KD, TOK], F32R)
            stage_normalise(nc, t, const, h_hi, h_lo)
            tile = 0
            for tag, kinds, pairs, outs in (("pqk", ("norm", "g"), N_NORM, (0, 0)),
                                            ("pvz", ("v", "z"), N_V, (0, 0)),
                                            ("pzg", ("z", "g"), N_Z - N_V, (N_V, N_NORM))):
                stage_project(nc, t, const, h_hi, h_lo, tag, kinds, pairs, tile, outs)
                tile += 2 * pairs
        for tag, (tok0, T) in zip(("as", "ap"), SEQS):
            stage_attend_a(nc, t, const, tag, tok0, T)
        stage_attend_grid(nc, t, const)
        stage_attend_slide(nc, t, const)
        stage_merge(nc, t, const)


def column_tiles():
    starts, at = {}, 0
    for name, width in (("qa", 512), ("ka", 512), ("va", 512), ("za", 512), ("qb", 512), ("kb", 512), ("vb", 512),
                        ("zb", 512), ("qc", 512), ("kc", 128), ("vc", 128), ("zc", 512),
                        ("ga", 1024), ("gb", 1024), ("gc", 1024)):
        starts[name] = list(range(at // P, (at + width) // P))
        at += width
    kinds = {"norm": ("qa", "ka", "qb", "kb", "qc", "kc"), "v": ("va", "vb", "vc"), "z": ("za", "zb", "zc"),
             "g": ("ga", "gb", "gc")}
    tiles = {k: [n for name in names for n in starts[name]] for k, names in kinds.items()}
    order = []
    for i in range(N_NORM):
        order += [tiles["norm"][i], tiles["g"][i]]
    for i in range(N_V):
        order += [tiles["v"][i], tiles["z"][i]]
    for i in range(N_Z - N_V):
        order += [tiles["z"][N_V + i], tiles["g"][N_NORM + i]]
    return order


def shape_constants():
    p = np.arange(P)
    out = {"ident": np.eye(P, dtype=np.float32)}
    out["head_ones"] = (p[:, None] // HD == p[None, :] // HD).astype(np.float32)
    x = np.arange(2 * T_SAMPLE - P)
    out["alibi"] = -np.abs(p[:, None] - (x[None, :] - (T_SAMPLE - P))).astype(np.float32)
    dist = np.abs(p[:, None] + P - np.arange(3 * P)[None, :])
    out["slide_dist"] = -dist.astype(np.float32)
    out["slide_mask"] = np.where(dist <= P, 0.0, NEG).astype(np.float32)
    col, row = p % GRID_W, p // GRID_W
    start = np.clip(col - KW // 2, 0, GRID_W - KW)
    key = np.arange(GRID_W)
    seen = (key[None, :] >= start[:, None]) & (key[None, :] < start[:, None] + KW)
    out["col_mask"] = np.tile(np.where(seen, 0.0, NEG).astype(np.float32), (1, 14))
    delta = np.arange(-4, 6)[None, :] - row[:, None]
    rows = np.where((delta >= -(MAX_KH // 2)) & (delta < MAX_KH // 2), 0.0, NEG).astype(np.float32)
    out["row_mask"] = np.repeat(rows, GRID_W, axis=1)
    return out


def laid_out(a):
    a = {k: np.asarray(v) for k, v in a.items()}
    out = {"x": np.concatenate([a["x_sample"][0], a["x_prompt"][0]], axis=0)}
    w = a["w_in"][0].reshape(KD, P, -1, P).transpose(2, 1, 0, 3)[column_tiles()]
    out["w_in"] = w.reshape(w.shape[0], P, KD * P)
    out["norm_g"] = a["norm_g"]
    gains = []
    for name, n_q, n_k in (("qk_gain_a", 4, 4), ("qk_gain_b", 4, 4), ("qk_gain_c", 4, 1)):
        gains += [a[name][0, 0]] * n_q + [a[name][0, 1]] * n_k
    out["gains"] = np.stack([np.concatenate([g, g]) for g in gains], axis=1)
    out["lambda_a"], out["subln_g"], out["sink_c"] = a["lambda_a"][0], a["subln_g_a"], a["sink_c"]
    out["rpb"] = a["rpb_b"][0].reshape(H_B * BIAS_ROWS, BIAS_COLS)[:, ::-1].copy()
    w3 = [a[f"w_proj_{n}"][0].reshape(4, P, KD, P) for n in "abc"]
    out["w_proj"] = np.stack(w3).transpose(3, 2, 0, 1, 4).reshape(KD, P, 12 * P)
    out["w_out"] = a["w_out"][0].reshape(KD, P, D)
    out.update(shape_constants())
    return {k: np.ascontiguousarray(v) for k, v in out.items()}


def kernel(**inputs):
    import concourse.bacc as bacc
    from concourse.bass_utils import run_bass_kernel_spmd

    nc = bacc.Bacc("TRN2", target_bir_lowering=False, num_devices=1)
    arrays = laid_out(inputs)
    t = {n: nc.dram_tensor(f"in_{n}", a.shape, mybir.dt.from_np(a.dtype), kind="ExternalInput").ap()
         for n, a in arrays.items()}
    t["y"] = nc.dram_tensor("y", (TOK, D), F32, kind="ExternalOutput").ap()
    build_program(nc, t)
    result = run_bass_kernel_spmd(nc, [{f"in_{n}": a for n, a in arrays.items()}], core_ids=[0])
    y = result.results[0]["y"]
    return y[T_SAMPLE:].reshape(1, T_PROMPT, D), y[:T_SAMPLE].reshape(1, T_SAMPLE, D)
```

```python
from contextlib import ExitStack

import numpy as np

import concourse.bass as bass
from concourse import mybir

F32 = mybir.dt.float32
F32R = mybir.dt.float32r
ALU = mybir.AluOpType
ACT = mybir.ActivationFunctionType
AX = mybir.AxisListType

P = 128
D = 1024
KD = D // P
T_SAMPLE, T_PROMPT = 2048, 512
TOK = T_SAMPLE + T_PROMPT
BLK = 512
NBLK = TOK // BLK
HD = 64
H_A, H_B, H_C, KV_C = 4, 8, 8, 2
EPS = 1e-6
LAM_INIT = 0.2
NEG = -1e30
GRID_W, MAX_KH, KW = 64, 8, 16
N_NORM, N_V, N_Z, N_G = 21, 9, 12, 24
SEQS = ((0, T_SAMPLE), (T_SAMPLE, T_PROMPT))
BIAS_ROWS, BIAS_COLS = 2 * MAX_KH - 1, 2 * KW - 1
PAD_W = 2 * GRID_W


class Pool:

    def __init__(self, nc, ctx, tag):
        self.nc, self.ctx, self.tag, self.used = nc, ctx, tag, []
        ctx.callback(self.clear)

    def clear(self):
        if self.used:
            self.nc.all_engine_barrier()
            self.nc.clear_and_free_semaphores(self.used)
            self.nc.all_engine_barrier()

    def sb(self, name, shape, dt=F32):
        return self.ctx.enter_context(self.nc.sbuf_tensor(f"{self.tag}_{name}", shape, dt))

    def ps(self, name, shape, dt=F32):
        return self.ctx.enter_context(self.nc.psum_tensor(f"{self.tag}_{name}", shape, dt))

    def sem(self, name):
        self.used.append(self.nc.alloc_semaphore(name=f"{self.tag}_{name}"))
        return self.used[-1]

    def sems(self, name, n):
        return [self.sem(f"{name}{i}") for i in range(n)]


def flat(ap):
    return ap.rearrange("a p n -> (a p) n")


def stage_constants(nc, t, const):
    with ExitStack() as ctx:
        pool = Pool(nc, ctx, "cst")
        loaded, made = pool.sem("loaded"), pool.sem("made")
        exped, stored = pool.sem("exped"), pool.sem("stored")
        lam_in = pool.sb("lam_in", [P, 4, HD])
        lam_prod = pool.sb("lam_prod", [P, 2, HD])
        lam_sum = pool.sb("lam_sum", [P, 2])
        lam_exp = pool.sb("lam_exp", [P, 2])
        ones_f = pool.sb("ones_f", [P, P])
        zeros = pool.sb("zeros", [H_B * BIAS_ROWS, PAD_W])
        rpb = pool.sb("rpb", [H_B * BIAS_ROWS, BIAS_COLS])
        block = ctx.enter_context(nc.Block())
        n_load = 7

        @block.sync
        def _(sp):
            sp.dma_start(const["ident"][:], t["ident"]).then_inc(loaded, 16)
            sp.dma_start(ones_f[:], t["head_ones"]).then_inc(loaded, 16)
            sp.dma_start(const["gains"][:], t["gains"]).then_inc(loaded, 16)
            sp.dma_start(const["sink"][:], bass.AP(t["sink_c"].tensor, 0, [[0, P], [1, H_C]])).then_inc(loaded, 16)
            sp.dma_start(const["subln_g"][:], t["subln_g"].rearrange("a p -> p a")).then_inc(loaded, 16)
            sp.dma_start(lam_in[:], bass.AP(t["lambda_a"].tensor, 0, [[0, P], [HD, 4], [1, HD]])).then_inc(loaded, 16)
            sp.dma_start(rpb[:], t["rpb"]).then_inc(loaded, 16)
            sp.wait_ge(made, 9)
            sp.dma_start(t["rpb_pad"], zeros[:]).then_inc(stored, 16)
            sp.wait_ge(stored, 16)

        @block.vector
        def _(dve):
            dve.wait_ge(loaded, 16 * n_load)
            dve.tensor_copy(const["head_ones"][:], ones_f[:]).then_inc(made, 1)
            for n, (a, b) in enumerate(((4, 8), (12, 16), (20, 21))):
                dve.tensor_scalar(const["gains"][:, a:b], const["gains"][:, a:b], HD ** -0.5, None,
                                  ALU.mult).then_inc(made, 1)
            dve.tensor_scalar(const["subln_g"][:], const["subln_g"][:], 1.0 - LAM_INIT, None,
                              ALU.mult).then_inc(made, 1)
            dve.memset(zeros[:], 0.0).then_inc(made, 1)
            dve.memset(const["eps"][:], EPS).then_inc(made, 1)
            dve.wait_ge(made, 7)
            middle = GRID_W - KW + 1
            dve.tensor_copy(zeros[:, middle:middle + BIAS_COLS], rpb[:]).then_inc(made, 1)
            dve.memset(const["all_ones"][:], 1.0).then_inc(made, 1)
            dve.tensor_tensor(lam_prod[:, 0, :], lam_in[:, 0, :], lam_in[:, 1, :], ALU.mult).then_inc(made, 1)
            dve.tensor_tensor(lam_prod[:, 1, :], lam_in[:, 2, :], lam_in[:, 3, :], ALU.mult).then_inc(made, 1)
            dve.wait_ge(made, 11)
            dve.tensor_reduce(lam_sum[:], lam_prod[:], axis=AX.X, op=ALU.add).then_inc(made, 1)
            dve.wait_ge(exped, 1)
            dve.scalar_tensor_tensor(const["neg_lam"][:], lam_exp[:, 1:2], -LAM_INIT, lam_exp[:, 0:1],
                                     ALU.add, ALU.subtract).then_inc(made, 1)

        @block.scalar
        def _(act):
            act.wait_ge(made, 12)
            act.activation(lam_exp[:], lam_sum[:], ACT.Exp).then_inc(exped, 1)


def stage_normalise(nc, t, const, h_hi, h_lo):
    with ExitStack() as ctx:
        pool = Pool(nc, ctx, "nrm")
        x = [pool.sb(f"x{j}", [P, D]) for j in range(2)]
        h = [pool.sb(f"h{j}", [P, D]) for j in range(2)]
        square = pool.sb("square", [P, D])
        norm_g = pool.sb("norm_g", [P, D])
        g_in = pool.sem("g_in")
        stat = [pool.sb(f"stat{j}", [P, 4]) for j in range(2)]
        bank = [[pool.ps(f"bank{j}{q}", [P, 4, P]) for q in range(2)] for j in range(2)]
        x_in, squared, mean, root = pool.sems("x_in", 2), pool.sem("squared"), pool.sem("mean"), pool.sem("root")
        inv, h_ready, turned = pool.sem("inv"), pool.sem("h_ready"), pool.sem("turned")
        hi_done, lo_done = pool.sem("hi_done"), pool.sem("lo_done")
        block = ctx.enter_context(nc.Block())
        rounds = TOK // P // 2
        x_tiles = t["x"].rearrange("(n p) d -> n p d", p=P)

        @block.sync
        def _(sp):
            sp.dma_start(norm_g[:], bass.AP(t["norm_g"].tensor, 0, [[0, P], [1, D]])).then_inc(g_in, 16)
            with sp.Fori(0, rounds) as i:
                for j in range(2):
                    sp.wait_ge(h_ready, 2 * i)
                    sp.dma_start(x[j][:], flat(x_tiles[bass.ds(2 * i + j, 1)])).then_inc(x_in[j], 16)

        @block.scalar
        def _(act):
            with act.Fori(0, rounds) as i:
                for j in range(2):
                    act.wait_ge(x_in[j], 16 * i + 16)
                    act.wait_ge(squared, 2 * i + j)
                    act.activation(square[:], x[j][:], ACT.Square,
                                   accum_out=stat[j][:, 0:1]).then_inc(squared, 1)
                for j in range(2):
                    act.wait_ge(mean, 2 * i + j + 1)
                    act.activation(stat[j][:, 2:3], stat[j][:, 1:2], ACT.Sqrt).then_inc(root, 1)
                for j in range(2):
                    for q in range(2):
                        act.wait_ge(turned, 4 * i + 2 * j + q + 1)
                        act.activation(h_hi[:, 4 * q:4 * q + 4, bass.ds((2 * i + j) * P, P)],
                                       bank[j][q][:], ACT.Copy).then_inc(hi_done, 1)

        @block.vector
        def _(dve):
            dve.wait_ge(g_in, 16)
            with dve.Fori(0, rounds) as i:
                for j in range(2):
                    dve.wait_ge(squared, 2 * i + j + 1)
                    dve.tensor_scalar(stat[j][:, 1:2], stat[j][:, 0:1], 1.0 / D, EPS,
                                      ALU.mult, ALU.add).then_inc(mean, 1)
                for j in range(2):
                    dve.wait_ge(root, 2 * i + j + 1)
                    dve.reciprocal(stat[j][:, 3:4], stat[j][:, 2:3]).then_inc(inv, 1)
                    dve.wait_ge(inv, 2 * i + j + 1)
                    dve.wait_ge(turned, 4 * i)
                    dve.scalar_tensor_tensor(h[j][:], x[j][:], stat[j][:, 3:4], norm_g[:],
                                             ALU.mult, ALU.mult).then_inc(h_ready, 1)
                for j in range(2):
                    for q in range(2):
                        dve.wait_ge(hi_done, 4 * i + 2 * j + q + 1)
                        cols = bass.ds((2 * i + j) * P, P)
                        dve.tensor_tensor(h_lo[:, 4 * q:4 * q + 4, cols], bank[j][q][:],
                                          h_hi[:, 4 * q:4 * q + 4, cols].bitcast(F32),
                                          ALU.subtract).then_inc(lo_done, 1)

        @block.tensor
        def _(pe):
            with pe.Fori(0, rounds) as i:
                for j in range(2):
                    pe.wait_ge(h_ready, 2 * i + j + 1)
                    pe.wait_ge(lo_done, 4 * i)
                    for q in range(2):
                        for k in range(4):
                            last = pe.transpose(bank[j][q][:, k, :], h[j][:, (4 * q + k) * P:(4 * q + k + 1) * P],
                                                const["ident"][:])
                        last.then_inc(turned, 1)


def stage_project(nc, t, const, h_hi, h_lo, tag, kinds, pairs, first_tile, first_out):
    with ExitStack() as ctx:
        pool = Pool(nc, ctx, tag)
        w_raw = pool.sb("w_raw", [P, KD, P])
        w_hi = [pool.sb(f"w_hi{s}", [P, KD, P], F32R) for s in range(2)]
        w_lo = [pool.sb(f"w_lo{s}", [P, KD, P], F32R) for s in range(2)]
        acc = [pool.ps(f"acc{b}", [P, BLK]) for b in range(NBLK)]
        side = [pool.ps(f"side{s}", [P, BLK]) for s in range(2)]
        out = pool.sb("out", [P, BLK])
        w_in, w_split = pool.sem("w_in"), pool.sem("w_split")
        acc_ready = pool.sems("acc_ready", 2)
        bank_done = pool.sems("bank_done", NBLK)
        side_done, side_read = pool.sem("side_done"), pool.sem("side_read")
        stored = pool.sem("stored")
        if kinds[0] == "norm":
            sq = pool.sb("sq", [P, BLK])
            sq_hi = [pool.sb(f"sq_hi{s}", [P, BLK], F32R) for s in range(2)]
            sq_lo = [pool.sb(f"sq_lo{s}", [P, BLK], F32R) for s in range(2)]
            root = pool.sb("root", [P, BLK])
            qk = pool.sb("qk", [P, BLK])
            qk_hi = [pool.sb(f"qk_hi{s}", [P, BLK], F32R) for s in range(2)]
            qk_lo = [pool.sb(f"qk_lo{s}", [P, BLK], F32R) for s in range(2)]
            sq_ready, sq_split, inv_ready = pool.sem("sq_ready"), pool.sem("sq_split"), pool.sem("inv_ready")
            hi_ready, lo_ready = pool.sem("hi_ready"), pool.sem("lo_ready")
            qk_stored = pool.sems("qk_stored", 2)
        if kinds[0] == "v":
            v_t = [pool.sb(f"v_t{s}", [P, BLK]) for s in range(2)]
            v_out = [pool.sb(f"v_out{s}", [P, BLK]) for s in range(2)]
            v_stored = pool.sems("v_stored", 2)
        block = ctx.enter_context(nc.Block())
        funcs = {"z": ACT.Silu, "g": ACT.Sigmoid}
        dram = {"z": t["z"], "g": t["g"]}
        gates = sum(k in funcs for k in kinds)

        def before(i, b):
            return 5 * i + (b - 1 if b else 0)

        def uses(i, b):
            return (3 * i if b % 2 == 0 else 2 * i) + b // 2

        @block.sync
        def _(sp):
            with sp.Fori(0, pairs) as i:
                for s in range(2):
                    sp.wait_ge(w_split, 2 * (2 * i + s))
                    sp.dma_start(w_raw[:].rearrange("p k c -> p (k c)"),
                                 flat(t["w_in"][bass.ds(2 * i + (first_tile + s), 1)])).then_inc(w_in, 16)

        @block.gpsimd
        def _(pool_e):
            def split_weights(i, s):
                n = 2 * i + s
                pool_e.wait_ge(w_in, 16 * n + 16)
                pool_e.wait_ge(acc_ready[s], NBLK * i)
                halves = [slice(q * KD // 2, (q + 1) * KD // 2) for q in range(2)]
                for q in halves:
                    last = pool_e.tensor_tensor(w_hi[s][:, q, :], w_raw[:, q, :],
                                                const["all_ones"][:].rearrange("p (k c) -> p k c", c=P), ALU.mult)
                last.then_inc(w_split, 1)
                pool_e.wait_ge(w_split, 2 * n + 1)
                pool_e.tensor_tensor(w_lo[s][:], w_raw[:], w_hi[s][:].bitcast(F32),
                                     ALU.subtract).then_inc(w_split, 1)

            def split_squares(i, b):
                m, s = NBLK * i + b, b % 2
                pool_e.wait_ge(sq_ready, m + 1)
                pool_e.wait_ge(side_done, before(i, b))
                pool_e.tensor_tensor(sq_hi[s][:], sq[:], const["all_ones"][:], ALU.mult).then_inc(sq_split, 1)
                pool_e.wait_ge(sq_split, 2 * m + 1)
                pool_e.tensor_tensor(sq_lo[s][:], sq[:], sq_hi[s][:].bitcast(F32),
                                     ALU.subtract).then_inc(sq_split, 1)

            def low_part(i, b):
                m = NBLK * i + b
                pool_e.wait_ge(hi_ready, m + 1)
                pool_e.wait_ge(qk_stored[b % 2], 32 * uses(i, b))
                pool_e.tensor_tensor(qk_lo[b % 2][:], qk[:], qk_hi[b % 2][:].bitcast(F32),
                                     ALU.subtract).then_inc(lo_ready, 1)

            with pool_e.Fori(0, pairs) as i:
                split_weights(i, 0)
                split_weights(i, 1)
                if kinds[0] == "norm":
                    for b in range(NBLK):
                        split_squares(i, b)
                        if b:
                            low_part(i, b - 1)
                    low_part(i, NBLK - 1)

        @block.scalar
        def _(act):
            def square(i, b):
                m = NBLK * i + b
                act.wait_ge(acc_ready[0], m + 1)
                act.wait_ge(sq_split, 2 * m)
                act.activation(sq[:], acc[b][:], ACT.Square).then_inc(sq_ready, 1)

            def root_and_high(i, b):
                m = NBLK * i + b
                act.wait_ge(side_done, m + 1)
                act.wait_ge(inv_ready, m)
                act.activation(root[:], side[b % 2][:], ACT.Sqrt, bias=const["eps"][:],
                               scale=1.0 / HD).then_inc(side_read, 1)
                act.wait_ge(bank_done[b], 2 * i + 1)
                act.wait_ge(qk_stored[b % 2], 32 * uses(i, b))
                act.activation(qk_hi[b % 2][:], qk[:], ACT.Copy).then_inc(hi_ready, 1)

            def store_qk(i, b):
                act.wait_ge(lo_ready, NBLK * i + b + 1)
                cols = slice(b * BLK, (b + 1) * BLK)
                row = bass.ds(i, 1)
                act.dma_start(flat(t["qk_hi"][row, :, cols]), qk_hi[b % 2][:].bitcast(F32)).then_inc(qk_stored[b % 2], 16)
                act.dma_start(flat(t["qk_lo"][row, :, cols]), qk_lo[b % 2][:].bitcast(F32)).then_inc(qk_stored[b % 2], 16)

            def gate(i, s, b):
                act.wait_ge(acc_ready[s], NBLK * i + b + 1)
                turn = s if gates == 2 else 0
                act.wait_ge(stored, 16 * (gates * NBLK * i + (turn * NBLK + b)))
                act.activation(out[:], acc[b][:], funcs[kinds[s]]).then_inc(bank_done[b], 1)
                act.wait_ge(bank_done[b], 2 * i + s + 1)
                act.dma_start(flat(dram[kinds[s]][bass.ds(i + first_out[s], 1), :, b * BLK:(b + 1) * BLK]),
                              out[:]).then_inc(stored, 16)

            def copy_v(i, b):
                act.wait_ge(acc_ready[0], NBLK * i + b + 1)
                act.wait_ge(side_done, before(i, b))
                act.activation(v_t[b % 2][:], acc[b][:], ACT.Copy).then_inc(bank_done[b], 1)

            def store_v(i, b):
                act.wait_ge(side_read, NBLK * i + b + 1)
                act.dma_start(t["v"][b * BLK:(b + 1) * BLK, bass.ds(i * P, P)].rearrange("(n p) c -> p n c", p=P),
                              v_out[b % 2][:].rearrange("p (n c) -> p n c", c=P)).then_inc(v_stored[b % 2], 16)

            with act.Fori(0, pairs) as i:
                if kinds[0] == "norm":
                    for b in range(NBLK):
                        square(i, b)
                        if b:
                            root_and_high(i, b - 1)
                        if b > 1:
                            store_qk(i, b - 2)
                    root_and_high(i, NBLK - 1)
                    store_qk(i, NBLK - 2)
                elif kinds[0] == "v":
                    for b in range(NBLK):
                        copy_v(i, b)
                        if b:
                            store_v(i, b - 1)
                    store_v(i, NBLK - 1)
                else:
                    for b in range(NBLK):
                        gate(i, 0, b)
                for b in range(NBLK):
                    gate(i, 1, b)
                    if b == 0 and kinds[0] == "norm":
                        store_qk(i, NBLK - 1)
            if kinds[0] == "norm":
                act.wait_ge(qk_stored[0], 32 * 3 * pairs)
                act.wait_ge(qk_stored[1], 32 * 2 * pairs)
            if kinds[0] == "v":
                act.wait_ge(v_stored[0], 16 * 3 * pairs)
                act.wait_ge(v_stored[1], 16 * 2 * pairs)
            act.wait_ge(stored, 16 * NBLK * gates * pairs)

        if kinds[0] in ("norm", "v"):
            @block.vector
            def _(dve):
                with dve.Fori(0, pairs) as i:
                    for b in range(NBLK):
                        m = NBLK * i + b
                        if kinds[0] == "norm":
                            dve.wait_ge(side_read, m + 1)
                            dve.wait_ge(lo_ready, m)
                            dve.reciprocal(qk[:], root[:]).then_inc(inv_ready, 1)
                            dve.wait_ge(inv_ready, m + 1)
                            dve.scalar_tensor_tensor(qk[:], acc[b][:], const["gains"][:, bass.ds(i, 1)], qk[:],
                                                     ALU.mult, ALU.mult).then_inc(bank_done[b], 1)
                        else:
                            dve.wait_ge(side_done, m + 1)
                            dve.wait_ge(v_stored[b % 2], 16 * uses(i, b))
                            dve.tensor_copy(v_out[b % 2][:], side[b % 2][:]).then_inc(side_read, 1)

        @block.tensor
        def _(pe):
            def head_sums(i, b):
                m, s = NBLK * i + b, b % 2
                pe.wait_ge(sq_split, 2 * m + 2)
                pe.wait_ge(side_read, before(i, b))
                pe.matmul(side[s][:], const["head_ones"][:], sq_hi[s][:], start=True, stop=False)
                pe.matmul(side[s][:], const["head_ones"][:], sq_lo[s][:], start=False, stop=True).then_inc(side_done, 1)

            def turn_v(i, b):
                s = b % 2
                pe.wait_ge(bank_done[b], 2 * i + 1)
                pe.wait_ge(side_read, before(i, b))
                for n in range(BLK // P):
                    last = pe.transpose(side[s][:, n * P:(n + 1) * P], v_t[s][:, n * P:(n + 1) * P], const["ident"][:])
                last.then_inc(side_done, 1)

            after = {"norm": head_sums, "v": turn_v}.get(kinds[0])
            with pe.Fori(0, pairs) as i:
                for s in range(2):
                    pe.wait_ge(w_split, 2 * (2 * i + s) + 2)
                    for b in range(NBLK):
                        cols = slice(b * BLK, (b + 1) * BLK)
                        pe.wait_ge(bank_done[b], 2 * i + s)
                        for k in range(KD):
                            pe.matmul(acc[b][:], w_hi[s][:, k, :], h_hi[:, k, cols], start=(k == 0), stop=False)
                            pe.matmul(acc[b][:], w_hi[s][:, k, :], h_lo[:, k, cols], start=False, stop=False)
                            last = pe.matmul(acc[b][:], w_lo[s][:, k, :], h_hi[:, k, cols], start=False,
                                             stop=(k == KD - 1))
                        last.then_inc(acc_ready[s], 1)
                        if after and s == 0 and b:
                            after(i, b - 1)
                        if after and s == 1 and b == 0:
                            after(i, NBLK - 1)


def stage_attend_a(nc, t, const, tag, tok0, T):
    nq = T // P
    n_key = T // P
    chunk = min(2 * BLK, T)
    n_chunk = T // chunk
    per_unit = 2 * n_chunk
    groups = T // BLK
    units = 2 * nq
    blocks = units // 2
    head_blocks = blocks // 2
    rounds = H_A // 2
    bias_w = 2 * T - P
    n_dma = 11
    with ExitStack() as ctx:
        pool = Pool(nc, ctx, tag)
        q = [[pool.sb(f"q{s}{c}", [P, T], F32R) for c in range(2)] for s in range(2)]
        k_hi = [[pool.sb(f"k_hi{s}{c}", [P, T], F32R) for c in range(2)] for s in range(2)]
        k_lo = [pool.sb(f"k_lo{s}", [P, T], F32R) for s in range(2)]
        v = [pool.sb(f"v{s}", [P, n_key, P]) for s in range(2)]
        bias = pool.sb("bias", [P, bias_w])
        prob = [[pool.sb(f"prob{c}{s}", [P, T]) for s in range(3 - c)] for c in range(2)]
        stat = [pool.sb(f"stat{s}", [P, 12]) for s in range(2)]
        tick = pool.sb("tick", [P, 2])
        turned = [pool.sb(f"turned{s}", [P, n_key, 2 * P]) for s in range(2)]
        o_sb = [pool.sb(f"o_sb{s}", [P, 2 * P]) for s in range(2)]
        score = [pool.ps(f"score{s}", [P, chunk]) for s in range(2)]
        turn = [pool.ps(f"turn{s}", [P, BLK]) for s in range(2)]
        o_ps = [pool.ps(f"o_ps{s}", [P, BLK]) for s in range(2)]
        bias_in, bias_made = pool.sem("bias_in"), pool.sem("bias_made")
        head_in = pool.sems("head_in", 2)
        scored, masked, max_ready = pool.sem("scored"), pool.sem("masked"), pool.sem("max_ready")
        exp_done, inv0, scaled0 = pool.sem("exp_done"), pool.sem("inv0"), pool.sem("scaled0")
        inv1, factor1, mapped = pool.sem("inv1"), pool.sem("factor1"), pool.sem("mapped")
        turn_done, turn_read = pool.sem("turn_done"), pool.sem("turn_read")
        applied, o_done, o_stored = pool.sems("applied", 2), pool.sem("o_done"), pool.sems("o_stored", 2)
        block = ctx.enter_context(nc.Block())
        toks = slice(tok0, tok0 + T)

        @block.sync
        def _(sp):
            sp.dma_start(bias[:], t["alibi"][:, T_SAMPLE - T:T_SAMPLE - T + bias_w]).then_inc(bias_in, 16)
            with sp.Fori(0, rounds) as g:
                for s in range(2):
                    sp.wait_ge(applied[s], head_blocks * g)
                    q_tile, k_tile = bass.ds(2 * g + s, 1), bass.ds(2 * g + (H_A + s), 1)
                    for c in range(2):
                        rows = slice(c * HD, (c + 1) * HD)
                        hi, lo = t["qk_hi"], t["qk_lo"]
                        sp.dma_start(k_hi[s][c][0:HD, :].bitcast(F32), flat(hi[k_tile, rows, toks])).then_inc(head_in[s], 16)
                        sp.dma_start(k_hi[s][c][HD:P, :].bitcast(F32), flat(hi[k_tile, rows, toks])).then_inc(head_in[s], 16)
                        sp.dma_start(k_lo[s][rows, :].bitcast(F32), flat(lo[k_tile, rows, toks])).then_inc(head_in[s], 16)
                        other = slice((1 - c) * HD, (2 - c) * HD)
                        sp.dma_start(q[s][c][rows, :].bitcast(F32), flat(hi[q_tile, rows, toks])).then_inc(head_in[s], 16)
                        sp.dma_start(q[s][c][other, :].bitcast(F32), flat(lo[q_tile, rows, toks])).then_inc(head_in[s], 16)
                    sp.dma_start(v[s][:], t["v"][toks, bass.ds((2 * g + s) * P, P)].rearrange("(n p) c -> p n c", p=P)).then_inc(head_in[s], 16)

        @block.gpsimd
        def _(pool_e):
            with pool_e.Fori(0, rounds) as g:
                for u in range(units):
                    pool_e.wait_ge(inv0, units * g + (u + 1))
                    p = prob[0][u % 3]
                    pool_e.tensor_tensor(p[:], p[:], stat[u % 2][:, 8:9].broadcast_to([P, T]), ALU.mult).then_inc(scaled0, 1)

        @block.vector
        def _(dve):
            def scores_of(g, u, c, j):
                p, st = prob[c][u % (3 - c)], stat[u % 2]
                n = u * per_unit + c * n_chunk + j
                dve.wait_ge(scored, g * (units * per_unit) + (n + 1))
                if c == 0:
                    dve.wait_ge(turn_done, g * (units * groups) + max(u - 2, 0) * groups)
                else:
                    dve.wait_ge(mapped, units * g + max(u - 1, 0))
                dve.memset(tick[:, n % 2:n % 2 + 1], 0.0)
                at = j * chunk - (u % nq) * P + (T - P)
                dve.tensor_tensor_reduce(out=p[:, j * chunk:(j + 1) * chunk], in0=score[n % 2][:],
                                         in1=bias[:, at:at + chunk], scale=1.0, scalar=-3e38, op0=ALU.add,
                                         op1=ALU.max, accum_out=st[:, 2 * c + j:2 * c + j + 1]).then_inc(masked, 1)

            def maximum(g, u, c):
                st = stat[u % 2]
                dve.wait_ge(masked, g * (units * per_unit) + u * per_unit + (c + 1) * n_chunk)
                dve.tensor_reduce(st[:, 4 + c:5 + c], st[:, 2 * c:2 * c + n_chunk], axis=AX.X, op=ALU.max,
                                  negate=True).then_inc(max_ready, 1)

            def combine(g, u):
                st, n = stat[u % 2], units * g + (u + 1)
                dve.wait_ge(exp_done, 2 * n)
                dve.reciprocal(st[:, 9:10], st[:, 7:8]).then_inc(inv1, 1)
                dve.wait_ge(inv1, n)
                dve.tensor_tensor(st[:, 10:11], st[:, 9:10], const["neg_lam"][:], ALU.mult).then_inc(factor1, 1)
                dve.wait_ge(factor1, n)
                dve.wait_ge(scaled0, n)
                dve.scalar_tensor_tensor(prob[0][u % 3][:], prob[1][u % 2][:], st[:, 10:11], prob[0][u % 3][:],
                                         ALU.mult, ALU.add).then_inc(mapped, 1)

            dve.wait_ge(bias_in, 16)
            with dve.Fori(0, rounds) as g:
                for u in range(units + 1):
                    if u < units:
                        if u % nq == 0:
                            dve.tensor_scalar(bias[:], bias[:], 0.25, None, ALU.mult).then_inc(bias_made, 1)
                            dve.wait_ge(bias_made, 2 * g + (u // nq + 1))
                        for j in range(n_chunk):
                            scores_of(g, u, 0, j)
                        maximum(g, u, 0)
                    if u:
                        combine(g, u - 1)
                    if u < units:
                        scores_of(g, u, 1, 0)
                        dve.wait_ge(exp_done, 2 * (units * g + u) + 1)
                        dve.reciprocal(stat[u % 2][:, 8:9], stat[u % 2][:, 6:7]).then_inc(inv0, 1)
                        for j in range(1, n_chunk):
                            scores_of(g, u, 1, j)
                        maximum(g, u, 1)

        @block.scalar
        def _(act):
            def exponent(g, u, c):
                st, p = stat[u % 2], prob[c][u % (3 - c)]
                act.wait_ge(max_ready, 2 * (units * g + u) + (c + 1))
                act.activation(p[:], p[:], ACT.Exp, bias=st[:, 4 + c:5 + c],
                               accum_out=st[:, 6 + c:7 + c]).then_inc(exp_done, 1)

            def take_turned(g, u, which):
                b = u // 2
                s, own = b // head_blocks, b % head_blocks
                for n in which:
                    act.wait_ge(turn_done, g * (units * groups) + u * groups + n + 1)
                    if own >= 2:
                        act.wait_ge(applied[s], head_blocks * g + (own - 1))
                    elif s == 1:
                        act.wait_ge(applied[0], head_blocks * g + (head_blocks - 1 + own))
                    else:
                        act.wait_ge(applied[1], head_blocks * g)
                    act.activation(turned[b % 2][:, 4 * n:4 * n + 4, (u % 2) * P:(u % 2 + 1) * P],
                                   turn[(u * groups + n) % 2][:].rearrange("p (k c) -> p k c", c=P),
                                   ACT.Copy).then_inc(turn_read, 1)

            def take_output(g, b):
                s, own = b // head_blocks, b % head_blocks
                act.wait_ge(applied[s], head_blocks * g + (own + 1))
                act.wait_ge(o_stored[b % 2], 16 * ((blocks // 2) * g + b // 2))
                act.activation(o_sb[b % 2][:], o_ps[b % 2][:, 0:2 * P], ACT.Copy).then_inc(o_done, 1)

            def store(g, b):
                s, at = b // head_blocks, (b % head_blocks) * 2 * P
                act.wait_ge(o_done, blocks * g + (b + 1))
                act.dma_start(flat(t["o"][bass.ds(2 * g + s, 1), :, tok0 + at:tok0 + at + 2 * P]),
                              o_sb[b % 2][:]).then_inc(o_stored[b % 2], 16)

            half = groups // 2
            with act.Fori(0, rounds) as g:
                for step in range(units + 6):
                    u = step
                    if step >= 7 and step % 2 == 1:
                        store(g, (step - 7) // 2)
                    if 1 <= step <= units:
                        exponent(g, u - 1, 1)
                    if 2 <= step < units + 2:
                        take_turned(g, u - 2, range(half))
                    if u < units:
                        exponent(g, u, 0)
                    if 2 <= step < units + 2:
                        take_turned(g, u - 2, range(half, groups))
                    if step >= 6 and step % 2 == 0:
                        take_output(g, (step - 6) // 2)
            for s in range(2):
                act.wait_ge(o_stored[s], 16 * (blocks // 2) * rounds)

        @block.tensor
        def _(pe):
            def scores(g, u, j):
                s, qt = u // nq, u % nq
                n = u * per_unit + j
                c, at = j // n_chunk, (j % n_chunk) * chunk
                if qt == 0 and j == 0:
                    pe.wait_ge(head_in[s], 16 * n_dma * (g + 1))
                pe.wait_ge(masked, g * (units * per_unit) + max(n - 1, 0))
                rows, low = slice(qt * P, (qt + 1) * P), slice(c * HD, (c + 1) * HD)
                for b in range(0, chunk, BLK):
                    pe.matmul(score[n % 2][:, b:b + BLK], q[s][c][:, rows], k_hi[s][c][:, at + b:at + b + BLK],
                              start=True, stop=False)
                    last = pe.matmul(score[n % 2][:, b:b + BLK], q[s][c][low, rows],
                                     k_lo[s][low, at + b:at + b + BLK], start=False, stop=True)
                last.then_inc(scored, 1)

            def turn_maps(g, u, n):
                gid = u * groups + n
                pe.wait_ge(mapped, units * g + (u + 1))
                pe.wait_ge(turn_read, g * (units * groups) + max(gid - 1, 0))
                for k in range(4):
                    at = (4 * n + k) * P
                    last = pe.transpose(turn[gid % 2][:, k * P:(k + 1) * P], prob[0][u % 3][:, at:at + P],
                                        const["ident"][:])
                last.then_inc(turn_done, 1)

            def apply(g, b, piece):
                s = b // head_blocks
                if piece == 0:
                    pe.wait_ge(turn_read, g * (units * groups) + (2 * b + 2) * groups)
                    pe.wait_ge(o_done, blocks * g + max(b - 1, 0))
                for k in range(piece * n_key // 8, (piece + 1) * n_key // 8):
                    last = pe.matmul(o_ps[b % 2][:, 0:2 * P], v[s][:, k, :], turned[b % 2][:, k, :],
                                     start=(k == 0), stop=(k == n_key - 1))
                if piece == 7:
                    last.then_inc(applied[s], 1)

            with pe.Fori(0, rounds) as g:
                for step in range(units + 4):
                    for j in range(4):
                        if step < units and j < per_unit:
                            scores(g, step, j)
                        if step >= 4:
                            apply(g, (step - 4) // 2, 4 * (step % 2) + j)
                        if 2 <= step < units + 2 and j < groups:
                            turn_maps(g, step - 2, j)


def stage_attend_window(nc, t, const, tag, tok0, T, heads, per_round, q_tile, kv_of, n_kv, window, width, tables,
                        sink, o_tile):
    nt = T // P
    units = per_round * nt
    rounds = heads // per_round
    lag = 5
    group = 4
    n_turn = 1 if width > BLK else 2
    stores = per_round // 2
    with ExitStack() as ctx:
        pool = Pool(nc, ctx, tag)
        q = [pool.sb(f"q{s}", [P, T], F32R) for s in range(per_round)]
        k_hi = [pool.sb(f"k_hi{s}", [P, T], F32R) for s in range(n_kv)]
        k_lo = [pool.sb(f"k_lo{s}", [P, T], F32R) for s in range(n_kv)]
        v = [pool.sb(f"v{s}", [P, nt, HD]) for s in range(n_kv)]
        table = [pool.sb(f"table{s}", [P, tables["width"]]) for s in range(2)]
        prob = [pool.sb(f"prob{s}", [P, width]) for s in range(4)]
        turned = [pool.sb(f"turned{s}", [P, width]) for s in range(2)]
        stat = [pool.sb(f"stat{s}", [P, 6]) for s in range(8)]
        sinks = pool.sb("sinks", [P, per_round])
        tick = pool.sb("tick", [P, 1])
        o_sb = pool.sb("o_sb", [P, per_round // 2, T])
        score = [pool.ps(f"score{s}", [P, width if width <= BLK else 2 * BLK]) for s in range(2)]
        turn = [pool.ps(f"turn{s}", [P, width if width <= BLK else 2 * BLK]) for s in range(n_turn)]
        o_ps = [pool.ps(f"o_ps{s}", [P, BLK]) for s in range(2)]
        q_in, k_in, v_in = pool.sems("q_in", per_round), pool.sems("k_in", n_kv), pool.sems("v_in", n_kv)
        tab_done, sink_done = pool.sem("tab_done"), pool.sem("sink_done")
        scored, masked, max_ready = pool.sem("scored"), pool.sem("masked"), pool.sem("max_ready")
        exp_done, sum_done, inv, divided = pool.sem("exp_done"), pool.sem("sum_done"), pool.sem("inv"), pool.sem("divided")
        turn_done, read_a, read_b = pool.sem("turn_done"), pool.sem("read_a"), pool.sem("read_b")
        applied, o_done, o_stored = pool.sem("applied"), pool.sem("o_done"), pool.sem("o_stored")
        block = ctx.enter_context(nc.Block())
        toks = slice(tok0, tok0 + T)
        per_exp = 2 if sink else 1
        wide = [sum(window(m % nt)[1] * P > BLK for m in range(u)) for u in range(units + 1)]

        def done(g, n):
            return max(units * g + n, 0) if isinstance(g, int) else units * g + n

        def done_wide(g, n):
            if isinstance(g, int):
                return wide[units] * g + wide[n] if n >= 0 else max(wide[units] * (g - 1) + wide[n + units], 0)
            return wide[units] * g + (wide[n] if n >= 0 else wide[n + units] - wide[units])

        def groups_done(g, n):
            per = units // group
            return max(per * g + n, 0) if isinstance(g, int) else per * g + n

        def steps(g, last):
            return range(units + lag + 2 if last else units)

        def live(g, u, last):
            return u < units and (u >= 0 or not (isinstance(g, int) and g == 0))

        def run(eng, round_of):
            round_of(0, rounds == 1)
            if rounds > 3:
                with eng.Fori(1, rounds - 1) as g:
                    round_of(g, False)
            if rounds > 1:
                round_of(rounds - 1, True)

        @block.sync
        def _(sp):
            def round_of(g, last):
                for s in range(per_round):
                    n, keys = kv_of(g, s)
                    sp.wait_ge(scored, done(g - 1, (s + 1) * nt))
                    if keys:
                        k_tile, k_rows, v_cols = keys
                        for dst, src in ((k_hi[n][0:HD, :], t["qk_hi"]), (k_hi[n][HD:P, :], t["qk_hi"]),
                                         (k_lo[n][0:HD, :], t["qk_lo"])):
                            sp.dma_start(dst.bitcast(F32), flat(src[k_tile, k_rows, toks])).then_inc(k_in[n], 16)
                    tile = bass.ds(g * (per_round // 2) + (q_tile + s // 2), 1)
                    rows = slice((s % 2) * HD, (s % 2 + 1) * HD)
                    sp.dma_start(q[s][0:HD, :].bitcast(F32), flat(t["qk_hi"][tile, rows, toks])).then_inc(q_in[s], 16)
                    sp.dma_start(q[s][HD:P, :].bitcast(F32), flat(t["qk_lo"][tile, rows, toks])).then_inc(q_in[s], 16)
                    if keys:
                        sp.wait_ge(applied, done(g - 1, (s + 1) * nt))
                        sp.dma_start(v[n][:], t["v"][toks, v_cols].rearrange("(n p) c -> p n c", p=P)).then_inc(v_in[n], 16)

            run(sp, round_of)

        @block.gpsimd
        def _(pool_e):
            def divide(g, u):
                w, st = window(u % nt)[1] * P, stat[u % 8]
                pool_e.wait_ge(inv, done(g, u + 1))
                pool_e.tensor_tensor(prob[u % 4][:, 0:w], prob[u % 4][:, 0:w], st[:, 4:5].broadcast_to([P, w]),
                                     ALU.mult).then_inc(divided, 1)

            def round_of(g, last):
                for step in steps(g, last):
                    if live(g, step - 2, last):
                        divide(g, step - 2)

            run(pool_e, round_of)

        @block.vector
        def _(dve):
            def take_turned(g, u):
                w = window(u % nt)[1] * P
                if w > BLK:
                    dve.wait_ge(turn_done, done(g, u + 1))
                    dve.wait_ge(applied, done(g, u - 1))
                    dve.tensor_copy(turned[u % 2][:, BLK:w], turn[u % n_turn][:, BLK:w]).then_inc(read_b, 1)

            def invert_sum(g, u):
                st = stat[u % 8]
                dve.wait_ge(exp_done, per_exp * done(g, u + 1))
                if sink:
                    dve.tensor_tensor(st[:, 2:3], st[:, 2:3], st[:, 3:4], ALU.add).then_inc(sum_done, 1)
                    dve.wait_ge(sum_done, done(g, u + 1))
                dve.reciprocal(st[:, 4:5], st[:, 2:3]).then_inc(inv, 1)

            def take_output(g, u):
                m = (u % units) // group
                s, at = m * group // nt, (m * group % nt) * P
                rows = slice((s % 2) * HD, (s % 2 + 1) * HD)
                dve.wait_ge(applied, done(g, u + 1))
                dve.wait_ge(o_stored, 16 * stores * (g if u >= 0 else g - 1))
                dve.tensor_copy(o_sb[rows, s // 2, at:at + group * P], o_ps[m % 2][rows, :]).then_inc(o_done, 1)

            def scores_of(g, u):
                s, n = u // nt, u % nt
                first, count, col = window(n)
                w = count * P
                dve.wait_ge(scored, done(g, u + 1))
                dve.wait_ge(turn_done, done(g, u - 3))
                dve.memset(tick[:], 0.0)
                dve.tensor_tensor_reduce(out=prob[u % 4][:, 0:w], in0=score[u % 2][:, 0:w],
                                         in1=table[s % 2][:, col:col + w], scale=1.0,
                                         scalar=(sinks[:, s:s + 1] if sink else -3e38), op0=ALU.add, op1=ALU.max,
                                         accum_out=stat[u % 8][:, 0:1]).then_inc(masked, 1)
                dve.wait_ge(masked, done(g, u + 1))
                dve.tensor_scalar(stat[u % 8][:, 1:2], stat[u % 8][:, 0:1], -1.0, None, ALU.mult).then_inc(max_ready, 1)

            def round_of(g, last):
                for step in steps(g, last):
                    if live(g, step - 4, last):
                        take_turned(g, step - 4)
                    if live(g, step - 2, last):
                        invert_sum(g, step - 2)
                    if (step - 5) % group == group - 1 and live(g, step - 5, last):
                        take_output(g, step - 5)
                    if step < units:
                        if step == 0 and sink:
                            dve.wait_ge(exp_done, per_exp * done(g, 0))
                            dve.tensor_copy(sinks[:], const["sink"][:, bass.ds(g * per_round, per_round)]).then_inc(sink_done, 1)
                            dve.wait_ge(sink_done, g + 1)
                        if step % nt == 0:
                            tables["make"](dve, g, step // nt, per_round, table[step // nt % 2], tab_done)
                        scores_of(g, step)

            run(dve, round_of)

        @block.scalar
        def _(act):
            def take_turned(g, u):
                w = min(window(u % nt)[1] * P, BLK)
                act.wait_ge(turn_done, done(g, u + 1))
                act.wait_ge(applied, done(g, u - 1))
                act.activation(turned[u % 2][:, 0:w], turn[u % n_turn][:, 0:w], ACT.Copy).then_inc(read_a, 1)

            def exponent(g, u):
                s, w, st = u % units // nt, window(u % nt)[1] * P, stat[u % 8]
                act.wait_ge(max_ready, done(g, u + 1))
                act.activation(prob[u % 4][:, 0:w], prob[u % 4][:, 0:w], ACT.Exp, bias=st[:, 1:2],
                               accum_out=st[:, 2:3]).then_inc(exp_done, 1)
                if sink:
                    act.activation(st[:, 3:4], sinks[:, s:s + 1], ACT.Exp, bias=st[:, 1:2]).then_inc(exp_done, 1)

            def store(g, round_before):
                n = g if round_before else g + 1
                act.wait_ge(o_done, groups_done(n, 0))
                for c in range(stores):
                    tile = bass.ds(n * stores + (o_tile - stores + c), 1)
                    act.dma_start(flat(t["o"][tile, :, toks]), o_sb[:, c, :]).then_inc(o_stored, 16)

            def round_of(g, last):
                for step in steps(g, last):
                    if live(g, step - 4, last):
                        take_turned(g, step - 4)
                    if live(g, step - 1, last):
                        exponent(g, step - 1)
                    if step == 6 and live(g, -1, last):
                        store(g, True)
                    if step == units + 6:
                        store(g, False)

            run(act, round_of)
            act.wait_ge(o_stored, 16 * stores * rounds)

        @block.tensor
        def _(pe):
            def scores(g, u):
                s, n = u // nt, u % nt
                kv, _ = kv_of(g, s)
                first, count, _ = window(n)
                if n == 0:
                    pe.wait_ge(q_in[s], 32 * (g + 1))
                    pe.wait_ge(k_in[kv], 48 * (g + 1 if n_kv == per_round else 1))
                pe.wait_ge(masked, done(g, u - 1))
                rows = slice(n * P, (n + 1) * P)
                for a in range(0, count * P, BLK):
                    w = min(BLK, count * P - a)
                    at = first * P + a
                    pe.matmul(score[u % 2][:, a:a + w], q[s][:, rows], k_hi[kv][:, at:at + w],
                              start=True, stop=False)
                    last = pe.matmul(score[u % 2][:, a:a + w], q[s][0:HD, rows], k_lo[kv][0:HD, at:at + w],
                                     start=False, stop=True)
                last.then_inc(scored, 1)

            def turn_map(g, u):
                pe.wait_ge(divided, done(g, u + 1))
                pe.wait_ge(read_a, done(g, u + 1 - n_turn))
                if wide[units]:
                    pe.wait_ge(read_b, done_wide(g, u + 1 - n_turn))
                for k in range(window(u % nt)[1]):
                    last = pe.transpose(turn[u % n_turn][:, k * P:(k + 1) * P], prob[u % 4][:, k * P:(k + 1) * P],
                                        const["ident"][:])
                last.then_inc(turn_done, 1)

            def apply(g, u):
                before, m = u < 0, (u % units) // group
                s, n = u % units // nt, u % nt
                kv, _ = kv_of(g - 1 if before else g, s)
                first, count, _ = window(n)
                if n == 0:
                    pe.wait_ge(v_in[kv], 16 * ((g if before else g + 1) if n_kv == per_round else 1))
                pe.wait_ge(read_a, done(g, u + 1))
                if wide[units]:
                    pe.wait_ge(read_b, done_wide(g, u + 1))
                if u % group == 0:
                    pe.wait_ge(o_done, groups_done(g, u // group - 1))
                rows, at = slice((s % 2) * HD, (s % 2 + 1) * HD), u % group * P
                for k in range(count):
                    last = pe.matmul(o_ps[m % 2][rows, at:at + P], v[kv][:, first + k, :],
                                     turned[u % 2][:, k * P:(k + 1) * P], start=(k == 0), stop=(k == count - 1))
                last.then_inc(applied, 1)

            def round_of(g, last):
                for step in steps(g, last):
                    if step < units:
                        scores(g, step)
                    if live(g, step - 3, last):
                        turn_map(g, step - 3)
                    if live(g, step - 4, last):
                        apply(g, step - 4)

            run(pe, round_of)


def stage_attend_grid(nc, t, const):
    full, inner = 14 * GRID_W, 10 * GRID_W
    with ExitStack() as ctx:
        pool = Pool(nc, ctx, "grid")
        bias = pool.sb("bias", [P, H_B, full])
        col_mask = pool.sb("col_mask", [P, full])
        row_mask = pool.sb("row_mask", [P, inner])
        with ExitStack() as load:
            first = Pool(nc, load, "gridload")
            raw = first.sb("raw", [P, H_B, 14, GRID_W])
            loaded, made = first.sem("loaded"), first.sem("made")
            block = load.enter_context(nc.Block())

            @block.sync
            def _(sp):
                sp.dma_start(col_mask[:], t["col_mask"]).then_inc(loaded, 16)
                sp.dma_start(row_mask[:], t["row_mask"]).then_inc(loaded, 16)
                for h in range(H_B):
                    for a in range(2):
                        start = (h * BIAS_ROWS + 1 - a) * PAD_W + 1
                        src = bass.AP(t["rpb_pad"].tensor, start, [[1, GRID_W], [PAD_W, 14], [1, GRID_W]])
                        sp.dma_start(raw[a * GRID_W:(a + 1) * GRID_W, h, :, :], src).then_inc(loaded, 16)

            @block.vector
            def _(dve):
                dve.wait_ge(loaded, 16 * (2 + 2 * H_B))
                for h in range(H_B):
                    dve.tensor_tensor(bias[:, h, :].rearrange("p (e c) -> p e c", c=GRID_W), raw[:, h, :, ::-1],
                                      col_mask[:].rearrange("p (e c) -> p e c", c=GRID_W), ALU.add).then_inc(made, 1)
                dve.wait_ge(made, H_B)

        def make(dve, g, s, per_round, table, done):
            n = 2 * per_round * g + 2 * s
            dve.tensor_copy(table[:, 0:full], bias[:, bass.ds(g * per_round + s, 1), :].rearrange("p a n -> p (a n)")
                            ).then_inc(done, 1)
            dve.wait_ge(done, n + 1)
            dve.tensor_tensor(table[:, full:full + inner], table[:, 2 * GRID_W:2 * GRID_W + inner], row_mask[:],
                              ALU.add).then_inc(done, 1)
            dve.wait_ge(done, n + 2)

        for tag, (tok0, T) in zip(("gs", "gp"), SEQS):
            nt = T // P
            tables = {"width": full + inner, "make": make}

            def window(n, nt=nt):
                if nt > 4 and 2 <= n < nt - 2:
                    return n - 2, 5, full
                first = 0 if n < nt - 2 or nt == 4 else nt - 4
                return first, 4, (first - n + 3) * P

            def kv_of(g, s):
                return s, (bass.ds(g + 12, 1), slice(s * HD, (s + 1) * HD), bass.ds(g * P + (512 + s * HD), HD))

            stage_attend_window(nc, t, const, tag, tok0, T, H_B, 2, 8, kv_of, 2, window, 5 * P if nt > 4 else 4 * P,
                                tables, False, H_A)


def stage_attend_slide(nc, t, const):
    with ExitStack() as ctx:
        pool = Pool(nc, ctx, "slide")
        mask = pool.sb("mask", [P, 3 * P])
        for tag, (tok0, T) in zip(("ss", "sp"), SEQS):
            with ExitStack() as own:
                inner = Pool(nc, own, tag + "t")
                dist = inner.sb("dist", [P, 3 * P])
                loaded = inner.sem("loaded")

                def make(dve, g, s, per_round, table, done):
                    n = 2 * per_round * g + 2 * s
                    dve.tensor_scalar(dist[:], dist[:], 0.5, None, ALU.mult).then_inc(done, 1)
                    dve.wait_ge(done, n + 1)
                    dve.tensor_tensor(table[:], dist[:], mask[:], ALU.add).then_inc(done, 1)
                    dve.wait_ge(done, n + 2)

                with nc.Block() as block:
                    @block.sync
                    def _(sp):
                        sp.dma_start(dist[:], t["slide_dist"]).then_inc(loaded, 16)
                        sp.dma_start(mask[:], t["slide_mask"]).then_inc(loaded, 16)
                        sp.wait_ge(loaded, 32)

                nt = T // P

                def window(n, nt=nt):
                    first, end = max(n - 1, 0), min(n + 2, nt)
                    return first, end - first, (first - n + 1) * P

                def kv_of(g, s):
                    return g, (slice(20, 21), slice(g * HD, (g + 1) * HD), slice(1024 + g * HD, 1024 + (g + 1) * HD)) if s == 0 else None

                tables = {"width": 3 * P, "make": make}
                stage_attend_window(nc, t, const, tag, tok0, T, H_C, 4, 16, kv_of, KV_C, window, 3 * P,
                                    tables, True, H_A + H_B // 2)


def stage_merge(nc, t, const):
    n_u = 12
    row_tiles = BLK // P
    halves = D // BLK
    y_jobs = [(r, e) for r in range(row_tiles) for e in range(halves)]
    n_y = len(y_jobs)
    last_blk = NBLK - 1
    order = [0, 4, 1, 5, 2, 6, 3, 7, 8, 9, 10, 11]

    def preps(j):
        return [p for p in (2 * j - 1, 2 * j) if 0 <= p < n_u]

    def in_a(p):
        return order[p] < H_A

    with ExitStack() as ctx:
        pool = Pool(nc, ctx, "mrg")
        wo_hi = pool.sb("wo_hi", [P, KD, D], F32R)
        wo_lo = pool.sb("wo_lo", [P, KD, D], F32R)
        w_raw = [pool.sb(f"w_raw{s}", [P, n_u * P]) for s in range(2)]
        wp_hi = [pool.sb(f"wp_hi{s}", [P, n_u, P], F32R) for s in range(2)]
        wp_lo = [pool.sb(f"wp_lo{s}", [P, n_u, P], F32R) for s in range(2)]
        u_hi = pool.sb("u_hi", [P, n_u, BLK], F32R)
        u_lo = pool.sb("u_lo", [P, n_u, BLK], F32R)
        m_hi = pool.sb("m_hi", [P, KD, BLK], F32R)
        m_lo = pool.sb("m_lo", [P, KD, BLK], F32R)
        root = pool.sb("root", [P, BLK])
        g_in = pool.sb("g_in", [P, 3, BLK])
        m = pool.sb("m", [P, BLK])
        part = pool.sb("part", [P, BLK])
        o_in = [pool.sb(f"o_in{s}", [P, BLK]) for s in range(2)] + [part]
        z_in = [pool.sb(f"z_in{s}", [P, BLK]) for s in range(2)] + [m]
        xy = [pool.sb(f"xy{s}", [P, BLK]) for s in range(2)]
        acc = [pool.ps(f"acc{b}", [P, BLK]) for b in range(3)]
        y_ps = [pool.ps(f"y_ps{s}", [P, BLK]) for s in range(2)]
        sums = pool.ps("sums", [P, BLK])
        wo_in, wo_high, wo_low = pool.sems("wo_in", 2), pool.sem("wo_high"), pool.sem("wo_low")
        w_in, wp_high, wp_low = pool.sems("w_in", 2), pool.sem("wp_high"), pool.sem("wp_low")
        oz_in = pool.sems("oz_in", 3)
        squared, summed, rooted, inverted, normed = (pool.sem(n) for n in ("squared", "summed", "rooted", "inverted", "normed"))
        u_made, u_high, u_low = pool.sem("u_made"), pool.sem("u_high"), pool.sem("u_low")
        acc_ready, gated, g_loaded = pool.sem("acc_ready"), pool.sem("gated"), pool.sems("g_loaded", 3)
        m_high, m_low = pool.sem("m_high"), pool.sem("m_low")
        x_in, y_ready, y_added, y_stored = pool.sems("x_in", 2), pool.sem("y_ready"), pool.sem("y_added"), pool.sems("y_stored", 2)
        block = ctx.enter_context(nc.Block())

        def product_step(n, b):
            return 5 * n + (1, 2, 4)[b]

        @block.sync
        def _(sp):
            def load_prep(i, p):
                n, s = order[p], p % 3
                sp.wait_ge(u_low, n_u * i + max(p - 2, 0))
                if p == 2:
                    sp.wait_ge(m_low, KD * i)
                cols = bass.ds(i * BLK, BLK)
                sp.dma_start(o_in[s][:], t["o"][n, :, cols]).then_inc(oz_in[s], 16)
                sp.dma_start(z_in[s][:], t["z"][n, :, cols]).then_inc(oz_in[s], 16)

            def load_weights(i, d):
                sp.wait_ge(wp_low, KD * i + max(d - 1, 0))
                sp.dma_start(w_raw[d % 2][:], t["w_proj"][d]).then_inc(w_in[d % 2], 16)

            def load_gates(i, d):
                for b in range(3):
                    sp.wait_ge(gated, 5 * KD * i + (product_step(d - 1, b) if d else 0))
                    sp.dma_start(g_in[:, b, :], t["g"][b * KD + d, :, bass.ds(i * BLK, BLK)]).then_inc(g_loaded[b], 16)

            def load_x(i, j):
                r, e = y_jobs[j]
                sp.wait_ge(y_stored[j % 2], 16 * (4 * i + j // 2))
                rows = bass.ds(i * BLK + r * P, P)
                sp.dma_start(xy[j % 2][:], t["x"][rows, e * BLK:(e + 1) * BLK]).then_inc(x_in[j % 2], 16)

            def round_of(i, last):
                for d in range(KD):
                    if d + 1 < KD:
                        load_weights(i, d + 1)
                    load_gates(i, d)
                if not last:
                    load_weights(i + 1, 0)
                    for p in range(3):
                        load_prep(i + 1, p)
                for j in range(n_y):
                    load_x(i, j)
                    if not last:
                        for p in (2 * j + 3, 2 * j + 4):
                            if p < n_u:
                                load_prep(i + 1, p)

            for k in range(KD):
                if k >= 2:
                    sp.wait_ge(wo_high, k - 1)
                    sp.wait_ge(wo_low, k - 1)
                sp.dma_start(w_raw[k % 2][:, 0:D], t["w_out"][k]).then_inc(wo_in[k % 2], 16)
                load_prep(0, k)
            sp.wait_ge(wo_high, KD)
            sp.wait_ge(wo_low, KD)
            load_weights(0, 0)
            for p in range(KD, n_u):
                load_prep(0, p)
            with sp.Fori(0, last_blk) as i:
                round_of(i, False)
            round_of(last_blk, True)

        @block.gpsimd
        def _(pool_e):
            def low_u(i, p):
                pool_e.wait_ge(u_high, n_u * i + (p + 1))
                pool_e.tensor_tensor(u_lo[:, order[p], :], z_in[p % 3][:], u_hi[:, order[p], :].bitcast(F32),
                                     ALU.subtract).then_inc(u_low, 1)

            def low_weights(i, d):
                pool_e.wait_ge(wp_high, KD * i + (d + 1))
                pool_e.tensor_tensor(wp_lo[d % 2][:], w_raw[d % 2][:].rearrange("p (k c) -> p k c", c=P),
                                     wp_hi[d % 2][:].bitcast(F32), ALU.subtract).then_inc(wp_low, 1)

            def round_of(i, last):
                for d in range(1, KD):
                    low_weights(i, d)
                if not last:
                    low_weights(i + 1, 0)
                    for p in range(n_u):
                        low_u(i + 1, p)

            for p in range(n_u):
                if p < KD:
                    pool_e.wait_ge(wo_high, p + 1)
                    pool_e.tensor_tensor(wo_lo[:, p, :], w_raw[p % 2][:, 0:D], wo_hi[:, p, :].bitcast(F32),
                                         ALU.subtract).then_inc(wo_low, 1)
                if p:
                    low_u(0, p - 1)
                if p == KD:
                    low_weights(0, 0)
            low_u(0, n_u - 1)
            with pool_e.Fori(0, last_blk) as i:
                round_of(i, False)
            round_of(last_blk, True)

        @block.scalar
        def _(act):
            def square(i, p):
                a = order[p]
                act.wait_ge(oz_in[p % 3], 32 * (n_u // 3) * i + 32 * (p // 3 + 1))
                act.wait_ge(normed, H_A * i + a)
                act.activation(root[:], o_in[p % 3][:], ACT.Square).then_inc(squared, 1)

            def take_root(i, p):
                act.wait_ge(summed, H_A * i + (order[p] + 1))
                act.activation(root[:], sums[:], ACT.Sqrt, bias=const["eps"][:], scale=1.0 / P).then_inc(rooted, 1)

            def high_u(i, p):
                act.wait_ge(u_made, n_u * i + (p + 1))
                act.activation(u_hi[:, order[p], :], z_in[p % 3][:], ACT.Copy).then_inc(u_high, 1)

            def high_weights(i, d):
                act.wait_ge(w_in[d % 2], 16 * (KD // 2) * i + 16 * (d // 2 + 1))
                if d or not isinstance(i, int) or i:
                    act.wait_ge(acc_ready, 24 * i + 3 * (d - 1))
                act.activation(wp_hi[d % 2][:], w_raw[d % 2][:].rearrange("p (k c) -> p k c", c=P),
                               ACT.Copy).then_inc(wp_high, 1)

            def high_m(i, d):
                act.wait_ge(gated, 5 * KD * i + 5 * (d + 1))
                act.activation(m_hi[:, d, :], m[:], ACT.Copy).then_inc(m_high, 1)

            def store_y(i, j):
                r, e = y_jobs[j]
                act.wait_ge(y_added, n_y * i + (j + 1))
                act.dma_start(t["y"][bass.ds(i * BLK + r * P, P), e * BLK:(e + 1) * BLK], xy[j % 2][:]).then_inc(y_stored[j % 2], 16)

            def round_of(i, last):
                for d in range(KD):
                    if d + 1 < KD:
                        high_weights(i, d + 1)
                    elif not last:
                        high_weights(i + 1, 0)
                        square(i + 1, 0)
                    high_m(i, d)
                for j in range(n_y):
                    if not last:
                        for p in preps(j):
                            if in_a(p):
                                take_root(i + 1, p)
                        for p in preps(j):
                            if in_a(p) and order[p] + 1 < H_A:
                                square(i + 1, p + 2)
                            high_u(i + 1, p)
                    if j:
                        store_y(i, j - 1)
                store_y(i, n_y - 1)

            for p in range(n_u):
                if p < KD:
                    act.wait_ge(wo_in[p % 2], 16 * (p // 2 + 1))
                    act.activation(wo_hi[:, p, :], w_raw[p % 2][:, 0:D], ACT.Copy).then_inc(wo_high, 1)
                if in_a(p):
                    square(0, p)
                    take_root(0, p)
                if p:
                    high_u(0, p - 1)
                if p == KD:
                    high_weights(0, 0)
            high_u(0, n_u - 1)
            with act.Fori(0, last_blk) as i:
                round_of(i, False)
            round_of(last_blk, True)
            for s in range(2):
                act.wait_ge(y_stored[s], 16 * (n_y // 2) * NBLK)

        @block.vector
        def _(dve):
            def prepare(i, p):
                n, s = order[p], p % 3
                if n < H_A:
                    at = H_A * i + (n + 1)
                    dve.wait_ge(rooted, at)
                    dve.reciprocal(root[:], root[:]).then_inc(inverted, 1)
                    dve.wait_ge(inverted, at)
                    dve.scalar_tensor_tensor(o_in[s][:], o_in[s][:], const["subln_g"][:], root[:],
                                             ALU.mult, ALU.mult).then_inc(normed, 1)
                    dve.wait_ge(normed, at)
                    dve.tensor_tensor(z_in[s][:], o_in[s][:], z_in[s][:], ALU.mult).then_inc(u_made, 1)
                else:
                    dve.wait_ge(oz_in[s], 32 * (n_u // 3) * i + 32 * (p // 3 + 1))
                    dve.tensor_tensor(z_in[s][:], o_in[s][:], z_in[s][:], ALU.mult).then_inc(u_made, 1)

            def merge_tile(i, d):
                n = KD * i + d
                dve.wait_ge(m_low, n)
                for b in range(3):
                    dve.wait_ge(g_loaded[b], 16 * (n + 1))
                    dve.wait_ge(acc_ready, 3 * n + b + 1)
                    dve.tensor_tensor((part if b else m)[:], acc[b][:], g_in[:, b, :], ALU.mult).then_inc(gated, 1)
                    dve.wait_ge(gated, product_step(n, b))
                    if b:
                        dve.tensor_tensor(m[:], m[:], part[:], ALU.add).then_inc(gated, 1)
                        dve.wait_ge(gated, product_step(n, b) + 1)
                dve.wait_ge(m_high, n + 1)
                dve.tensor_tensor(m_lo[:, d, :], m[:], m_hi[:, d, :].bitcast(F32), ALU.subtract).then_inc(m_low, 1)

            def round_of(i, last):
                for d in range(KD):
                    merge_tile(i, d)
                for j in range(n_y):
                    if not last:
                        for p in preps(j):
                            prepare(i + 1, p)
                    dve.wait_ge(y_ready, n_y * i + (j + 1))
                    dve.wait_ge(x_in[j % 2], 16 * (n_y // 2) * i + 16 * (j // 2 + 1))
                    dve.tensor_tensor(xy[j % 2][:], y_ps[j % 2][:], xy[j % 2][:], ALU.add).then_inc(y_added, 1)

            for p in range(n_u):
                prepare(0, p)
            with dve.Fori(0, last_blk) as i:
                round_of(i, False)
            round_of(last_blk, True)

        @block.tensor
        def _(pe):
            def sum_squares(i, p):
                pe.wait_ge(squared, H_A * i + (order[p] + 1))
                pe.matmul(sums[:], const["all_ones"][:, 0:P], root[:], start=True, stop=True).then_inc(summed, 1)

            def project(i, d):
                pe.wait_ge(wp_low, KD * i + (d + 1))
                for b in range(3):
                    pe.wait_ge(gated, 5 * KD * i + (product_step(d - 1, b) if d else 0))
                    for k in range(4):
                        w = 4 * b + k
                        pe.matmul(acc[b][:], wp_hi[d % 2][:, w, :], u_hi[:, w, :], start=(k == 0), stop=False)
                        pe.matmul(acc[b][:], wp_hi[d % 2][:, w, :], u_lo[:, w, :], start=False, stop=False)
                        last = pe.matmul(acc[b][:], wp_lo[d % 2][:, w, :], u_hi[:, w, :], start=False, stop=(k == 3))
                    last.then_inc(acc_ready, 1)

            def output(i, j, last_round):
                r, e = y_jobs[j]
                rows, cols = slice(r * P, (r + 1) * P), slice(e * BLK, (e + 1) * BLK)
                if not last_round:
                    for p in preps(j):
                        if in_a(p):
                            sum_squares(i + 1, p)
                pe.wait_ge(y_added, n_y * i + max(j - 1, 0))
                for k in range(KD):
                    if j == 0:
                        pe.wait_ge(m_low, KD * i + (k + 1))
                    pe.matmul(y_ps[j % 2][:], m_hi[:, k, rows], wo_hi[:, k, cols], start=(k == 0), stop=False)
                    pe.matmul(y_ps[j % 2][:], m_hi[:, k, rows], wo_lo[:, k, cols], start=False, stop=False)
                    last = pe.matmul(y_ps[j % 2][:], m_lo[:, k, rows], wo_hi[:, k, cols], start=False, stop=(k == KD - 1))
                last.then_inc(y_ready, 1)

            def round_of(i, last):
                pe.wait_ge(u_low, n_u * (i + 1))
                for d in range(KD):
                    project(i, d)
                for j in range(n_y):
                    output(i, j, last)

            for p in range(n_u):
                if in_a(p):
                    sum_squares(0, p)
            with pe.Fori(0, last_blk) as i:
                round_of(i, False)
            round_of(last_blk, True)


def scratch(nc, t):
    def dram(name, shape):
        t[name] = nc.dram_tensor(name, shape, F32, kind="Internal").ap()
    dram("qk_hi", [N_NORM, P, TOK])
    dram("qk_lo", [N_NORM, P, TOK])
    dram("v", [TOK, N_V * P])
    dram("z", [N_Z, P, TOK])
    dram("g", [N_G, P, TOK])
    dram("o", [(H_A * 2 + H_B + H_C) // 2, P, TOK])
    dram("rpb_pad", [H_B * BIAS_ROWS, PAD_W])


def build_program(nc, t):
    scratch(nc, t)
    with ExitStack() as ctx:
        keep = Pool(nc, ctx, "keep")
        const = {
            "ident": keep.sb("ident", [P, P]), "head_ones": keep.sb("head_ones", [P, P], F32R),
            "all_ones": keep.sb("all_ones", [P, BLK]), "gains": keep.sb("gains", [P, N_NORM]),
            "sink": keep.sb("sink", [P, H_C]), "subln_g": keep.sb("subln_g", [P, 1]),
            "eps": keep.sb("eps", [P, 1]), "neg_lam": keep.sb("neg_lam", [P, 1]),
        }
        with ExitStack() as first:
            early = Pool(nc, first, "early")
            stage_constants(nc, t, const)
            h_hi = early.sb("h_hi", [P, KD, TOK], F32R)
            h_lo = early.sb("h_lo", [P, KD, TOK], F32R)
            stage_normalise(nc, t, const, h_hi, h_lo)
            tile = 0
            for tag, kinds, pairs, outs in (("pqk", ("norm", "g"), N_NORM, (0, 0)),
                                            ("pvz", ("v", "z"), N_V, (0, 0)),
                                            ("pzg", ("z", "g"), N_Z - N_V, (N_V, N_NORM))):
                stage_project(nc, t, const, h_hi, h_lo, tag, kinds, pairs, tile, outs)
                tile += 2 * pairs
        for tag, (tok0, T) in zip(("as", "ap"), SEQS):
            stage_attend_a(nc, t, const, tag, tok0, T)
        stage_attend_grid(nc, t, const)
        stage_attend_slide(nc, t, const)
        stage_merge(nc, t, const)


def column_tiles():
    starts, at = {}, 0
    for name, width in (("qa", 512), ("ka", 512), ("va", 512), ("za", 512), ("qb", 512), ("kb", 512), ("vb", 512),
                        ("zb", 512), ("qc", 512), ("kc", 128), ("vc", 128), ("zc", 512),
                        ("ga", 1024), ("gb", 1024), ("gc", 1024)):
        starts[name] = list(range(at // P, (at + width) // P))
        at += width
    kinds = {"norm": ("qa", "ka", "qb", "kb", "qc", "kc"), "v": ("va", "vb", "vc"), "z": ("za", "zb", "zc"),
             "g": ("ga", "gb", "gc")}
    tiles = {k: [n for name in names for n in starts[name]] for k, names in kinds.items()}
    order = []
    for i in range(N_NORM):
        order += [tiles["norm"][i], tiles["g"][i]]
    for i in range(N_V):
        order += [tiles["v"][i], tiles["z"][i]]
    for i in range(N_Z - N_V):
        order += [tiles["z"][N_V + i], tiles["g"][N_NORM + i]]
    return order


def shape_constants():
    p = np.arange(P)
    out = {"ident": np.eye(P, dtype=np.float32)}
    out["head_ones"] = (p[:, None] // HD == p[None, :] // HD).astype(np.float32)
    x = np.arange(2 * T_SAMPLE - P)
    out["alibi"] = -np.abs(p[:, None] - (x[None, :] - (T_SAMPLE - P))).astype(np.float32)
    dist = np.abs(p[:, None] + P - np.arange(3 * P)[None, :])
    out["slide_dist"] = -dist.astype(np.float32)
    out["slide_mask"] = np.where(dist <= P, 0.0, NEG).astype(np.float32)
    col, row = p % GRID_W, p // GRID_W
    start = np.clip(col - KW // 2, 0, GRID_W - KW)
    key = np.arange(GRID_W)
    seen = (key[None, :] >= start[:, None]) & (key[None, :] < start[:, None] + KW)
    out["col_mask"] = np.tile(np.where(seen, 0.0, NEG).astype(np.float32), (1, 14))
    delta = np.arange(-4, 6)[None, :] - row[:, None]
    rows = np.where((delta >= -(MAX_KH // 2)) & (delta < MAX_KH // 2), 0.0, NEG).astype(np.float32)
    out["row_mask"] = np.repeat(rows, GRID_W, axis=1)
    return out


def laid_out(a):
    a = {k: np.asarray(v) for k, v in a.items()}
    out = {"x": np.concatenate([a["x_sample"][0], a["x_prompt"][0]], axis=0)}
    w = a["w_in"][0].reshape(KD, P, -1, P).transpose(2, 1, 0, 3)[column_tiles()]
    out["w_in"] = w.reshape(w.shape[0], P, KD * P)
    out["norm_g"] = a["norm_g"]
    gains = []
    for name, n_q, n_k in (("qk_gain_a", 4, 4), ("qk_gain_b", 4, 4), ("qk_gain_c", 4, 1)):
        gains += [a[name][0, 0]] * n_q + [a[name][0, 1]] * n_k
    out["gains"] = np.stack([np.concatenate([g, g]) for g in gains], axis=1)
    out["lambda_a"], out["subln_g"], out["sink_c"] = a["lambda_a"][0], a["subln_g_a"], a["sink_c"]
    out["rpb"] = a["rpb_b"][0].reshape(H_B * BIAS_ROWS, BIAS_COLS)[:, ::-1].copy()
    w3 = [a[f"w_proj_{n}"][0].reshape(4, P, KD, P) for n in "abc"]
    out["w_proj"] = np.stack(w3).transpose(3, 2, 0, 1, 4).reshape(KD, P, 12 * P)
    out["w_out"] = a["w_out"][0].reshape(KD, P, D)
    out.update(shape_constants())
    return {k: np.ascontiguousarray(v) for k, v in out.items()}


def kernel(**inputs):
    import concourse.bacc as bacc
    from concourse.bass_utils import run_bass_kernel_spmd

    nc = bacc.Bacc("TRN2", target_bir_lowering=False, num_devices=1)
    arrays = laid_out(inputs)
    t = {n: nc.dram_tensor(f"in_{n}", a.shape, mybir.dt.from_np(a.dtype), kind="ExternalInput").ap()
         for n, a in arrays.items()}
    t["y"] = nc.dram_tensor("y", (TOK, D), F32, kind="ExternalOutput").ap()
    build_program(nc, t)
    result = run_bass_kernel_spmd(nc, [{f"in_{n}": a for n, a in arrays.items()}], core_ids=[0])
    y = result.results[0]["y"]
    return y[T_SAMPLE:].reshape(1, T_PROMPT, D), y[:T_SAMPLE].reshape(1, T_SAMPLE, D)
```

```python
from contextlib import ExitStack

import numpy as np

import concourse.bass as bass
from concourse import mybir

F32 = mybir.dt.float32
F32R = mybir.dt.float32r
ALU = mybir.AluOpType
ACT = mybir.ActivationFunctionType
AX = mybir.AxisListType

P = 128
D = 1024
KD = D // P
T_SAMPLE, T_PROMPT = 2048, 512
TOK = T_SAMPLE + T_PROMPT
BLK = 512
NBLK = TOK // BLK
HD = 64
H_A, H_B, H_C, KV_C = 4, 8, 8, 2
EPS = 1e-6
LAM_INIT = 0.2
NEG = -1e30
GRID_W, MAX_KH, KW = 64, 8, 16
N_NORM, N_V, N_Z, N_G = 21, 9, 12, 24
SEQS = ((0, T_SAMPLE), (T_SAMPLE, T_PROMPT))
BIAS_ROWS, BIAS_COLS = 2 * MAX_KH - 1, 2 * KW - 1
PAD_W = 2 * GRID_W


class Pool:

    def __init__(self, nc, ctx, tag):
        self.nc, self.ctx, self.tag, self.used = nc, ctx, tag, []
        ctx.callback(self.clear)

    def clear(self):
        if self.used:
            self.nc.all_engine_barrier()
            self.nc.clear_and_free_semaphores(self.used)
            self.nc.all_engine_barrier()

    def sb(self, name, shape, dt=F32):
        return self.ctx.enter_context(self.nc.sbuf_tensor(f"{self.tag}_{name}", shape, dt))

    def ps(self, name, shape, dt=F32):
        return self.ctx.enter_context(self.nc.psum_tensor(f"{self.tag}_{name}", shape, dt))

    def sem(self, name):
        self.used.append(self.nc.alloc_semaphore(name=f"{self.tag}_{name}"))
        return self.used[-1]

    def sems(self, name, n):
        return [self.sem(f"{name}{i}") for i in range(n)]


def flat(ap):
    return ap.rearrange("a p n -> (a p) n")


def stage_constants(nc, t, const):
    with ExitStack() as ctx:
        pool = Pool(nc, ctx, "cst")
        loaded, made = pool.sem("loaded"), pool.sem("made")
        exped, stored = pool.sem("exped"), pool.sem("stored")
        lam_in = pool.sb("lam_in", [P, 4, HD])
        lam_prod = pool.sb("lam_prod", [P, 2, HD])
        lam_sum = pool.sb("lam_sum", [P, 2])
        lam_exp = pool.sb("lam_exp", [P, 2])
        ones_f = pool.sb("ones_f", [P, P])
        zeros = pool.sb("zeros", [H_B * BIAS_ROWS, PAD_W])
        rpb = pool.sb("rpb", [H_B * BIAS_ROWS, BIAS_COLS])
        block = ctx.enter_context(nc.Block())
        n_load = 7

        @block.sync
        def _(sp):
            sp.dma_start(const["ident"][:], t["ident"]).then_inc(loaded, 16)
            sp.dma_start(ones_f[:], t["head_ones"]).then_inc(loaded, 16)
            sp.dma_start(const["gains"][:], t["gains"]).then_inc(loaded, 16)
            sp.dma_start(const["sink"][:], bass.AP(t["sink_c"].tensor, 0, [[0, P], [1, H_C]])).then_inc(loaded, 16)
            sp.dma_start(const["subln_g"][:], t["subln_g"].rearrange("a p -> p a")).then_inc(loaded, 16)
            sp.dma_start(lam_in[:], bass.AP(t["lambda_a"].tensor, 0, [[0, P], [HD, 4], [1, HD]])).then_inc(loaded, 16)
            sp.dma_start(rpb[:], t["rpb"]).then_inc(loaded, 16)
            sp.wait_ge(made, 9)
            sp.dma_start(t["rpb_pad"], zeros[:]).then_inc(stored, 16)
            sp.wait_ge(stored, 16)

        @block.vector
        def _(dve):
            dve.wait_ge(loaded, 16 * n_load)
            dve.tensor_copy(const["head_ones"][:], ones_f[:]).then_inc(made, 1)
            for n, (a, b) in enumerate(((4, 8), (12, 16), (20, 21))):
                dve.tensor_scalar(const["gains"][:, a:b], const["gains"][:, a:b], HD ** -0.5, None,
                                  ALU.mult).then_inc(made, 1)
            dve.tensor_scalar(const["subln_g"][:], const["subln_g"][:], 1.0 - LAM_INIT, None,
                              ALU.mult).then_inc(made, 1)
            dve.memset(zeros[:], 0.0).then_inc(made, 1)
            dve.memset(const["eps"][:], EPS).then_inc(made, 1)
            dve.wait_ge(made, 7)
            middle = GRID_W - KW + 1
            dve.tensor_copy(zeros[:, middle:middle + BIAS_COLS], rpb[:]).then_inc(made, 1)
            dve.memset(const["all_ones"][:], 1.0).then_inc(made, 1)
            dve.tensor_tensor(lam_prod[:, 0, :], lam_in[:, 0, :], lam_in[:, 1, :], ALU.mult).then_inc(made, 1)
            dve.tensor_tensor(lam_prod[:, 1, :], lam_in[:, 2, :], lam_in[:, 3, :], ALU.mult).then_inc(made, 1)
            dve.wait_ge(made, 11)
            dve.tensor_reduce(lam_sum[:], lam_prod[:], axis=AX.X, op=ALU.add).then_inc(made, 1)
            dve.wait_ge(exped, 1)
            dve.scalar_tensor_tensor(const["neg_lam"][:], lam_exp[:, 1:2], -LAM_INIT, lam_exp[:, 0:1],
                                     ALU.add, ALU.subtract).then_inc(made, 1)

        @block.scalar
        def _(act):
            act.wait_ge(made, 12)
            act.activation(lam_exp[:], lam_sum[:], ACT.Exp).then_inc(exped, 1)


def stage_normalise(nc, t, const, h_hi, h_lo):
    per, lag = 4, 2
    rounds = TOK // P // per
    with ExitStack() as ctx:
        pool = Pool(nc, ctx, "nrm")
        x = [pool.sb(f"x{s}", [P, D]) for s in range(per)]
        h = [pool.sb(f"h{s}", [P, D]) for s in range(2)]
        square = pool.sb("square", [P, D])
        norm_g = pool.sb("norm_g", [P, D])
        stat = [pool.sb(f"stat{s}", [P, 4]) for s in range(per)]
        bank = [[pool.ps(f"bank{s}{q}", [P, 4, P]) for q in range(2)] for s in range(per)]
        g_in, x_in = pool.sem("g_in"), pool.sems("x_in", per)
        squared, mean, root = pool.sem("squared"), pool.sem("mean"), pool.sem("root")
        inv, h_ready, turned = pool.sem("inv"), pool.sem("h_ready"), pool.sem("turned")
        hi_done, lo_done = pool.sem("hi_done"), pool.sem("lo_done")
        block = ctx.enter_context(nc.Block())
        x_tiles = t["x"].rearrange("(n p) d -> n p d", p=P)

        def done(g, n):
            return max(per * g + n, 0) if isinstance(g, int) else per * g + n

        def steps(last):
            return range(per + lag if last else per)

        def live(g, n):
            return n < per and (n >= 0 or not (isinstance(g, int) and g == 0))

        def run(eng, round_of):
            round_of(0, False)
            with eng.Fori(1, rounds - 1) as g:
                round_of(g, False)
            round_of(rounds - 1, True)

        @block.sync
        def _(sp):
            def round_of(g, last):
                for n in range(per):
                    sp.wait_ge(h_ready, done(g - 1, n + 1))
                    sp.dma_start(x[n][:], flat(x_tiles[bass.ds(per * g + n, 1)])).then_inc(x_in[n], 16)
                    if n == 0 and isinstance(g, int) and g == 0:
                        sp.dma_start(norm_g[:], bass.AP(t["norm_g"].tensor, 0, [[0, P], [1, D]])).then_inc(g_in, 16)

            run(sp, round_of)

        @block.scalar
        def _(act):
            def take_root(g, n):
                act.wait_ge(mean, done(g, n + 1))
                act.activation(stat[n % per][:, 2:3], stat[n % per][:, 1:2], ACT.Sqrt).then_inc(root, 1)

            def sum_squares(g, n):
                act.wait_ge(x_in[n], 16 * (g + 1))
                act.wait_ge(squared, done(g, n))
                act.activation(square[:], x[n][:], ACT.Square, accum_out=stat[n][:, 0:1]).then_inc(squared, 1)

            def high_part(g, n):
                for q in range(2):
                    act.wait_ge(turned, 2 * done(g, n) + q + 1)
                    act.activation(h_hi[:, 4 * q:4 * q + 4, bass.ds((per * g + n) * P, P)],
                                   bank[n % per][q][:], ACT.Copy).then_inc(hi_done, 1)

            def round_of(g, last):
                for step in steps(last):
                    if live(g, step - 1):
                        take_root(g, step - 1)
                    if step < per:
                        sum_squares(g, step)
                    if live(g, step - 2):
                        high_part(g, step - 2)

            run(act, round_of)

        @block.vector
        def _(dve):
            def mean_of(g, n):
                dve.wait_ge(squared, done(g, n + 1))
                dve.tensor_scalar(stat[n][:, 1:2], stat[n][:, 0:1], 1.0 / D, EPS, ALU.mult, ALU.add).then_inc(mean, 1)

            def normal(g, n):
                st = stat[n % per]
                dve.wait_ge(root, done(g, n + 1))
                dve.reciprocal(st[:, 3:4], st[:, 2:3]).then_inc(inv, 1)
                dve.wait_ge(inv, done(g, n + 1))
                dve.wait_ge(turned, 2 * done(g, n - 1))
                dve.scalar_tensor_tensor(h[n % 2][:], x[n % per][:], st[:, 3:4], norm_g[:],
                                         ALU.mult, ALU.mult).then_inc(h_ready, 1)

            def low_part(g, n):
                for q in range(2):
                    dve.wait_ge(hi_done, 2 * done(g, n) + q + 1)
                    cols = bass.ds((per * g + n) * P, P)
                    dve.tensor_tensor(h_lo[:, 4 * q:4 * q + 4, cols], bank[n % per][q][:],
                                      h_hi[:, 4 * q:4 * q + 4, cols].bitcast(F32), ALU.subtract).then_inc(lo_done, 1)

            def round_of(g, last):
                for step in steps(last):
                    if live(g, step - 1):
                        normal(g, step - 1)
                    if step < per:
                        mean_of(g, step)
                    if live(g, step - 2):
                        low_part(g, step - 2)

            dve.wait_ge(g_in, 16)
            run(dve, round_of)

        @block.tensor
        def _(pe):
            def turn(g, n):
                pe.wait_ge(h_ready, done(g, n + 1))
                pe.wait_ge(lo_done, 2 * done(g, n - per + 1))
                for q in range(2):
                    for k in range(4):
                        last = pe.transpose(bank[n % per][q][:, k, :], h[n % 2][:, (4 * q + k) * P:(4 * q + k + 1) * P],
                                            const["ident"][:])
                    last.then_inc(turned, 1)

            def round_of(g, last):
                for step in steps(last):
                    if live(g, step - 1):
                        turn(g, step - 1)

            run(pe, round_of)


def stage_project(nc, t, const, h_hi, h_lo, tag, kinds, pairs, first_tile, first_out):
    with ExitStack() as ctx:
        pool = Pool(nc, ctx, tag)
        w_raw = pool.sb("w_raw", [P, KD, P])
        w_hi = [pool.sb(f"w_hi{s}", [P, KD, P], F32R) for s in range(2)]
        w_lo = [pool.sb(f"w_lo{s}", [P, KD, P], F32R) for s in range(2)]
        acc = [pool.ps(f"acc{b}", [P, BLK]) for b in range(NBLK)]
        side = [pool.ps(f"side{s}", [P, BLK]) for s in range(2)]
        out = pool.sb("out", [P, BLK])
        w_in, w_split = pool.sem("w_in"), pool.sem("w_split")
        acc_ready = pool.sems("acc_ready", 2)
        bank_done = pool.sems("bank_done", NBLK)
        side_done, side_read = pool.sem("side_done"), pool.sem("side_read")
        stored = pool.sem("stored")
        if kinds[0] == "norm":
            sq = pool.sb("sq", [P, BLK])
            sq_hi = [pool.sb(f"sq_hi{s}", [P, BLK], F32R) for s in range(2)]
            sq_lo = [pool.sb(f"sq_lo{s}", [P, BLK], F32R) for s in range(2)]
            qk = [pool.sb(f"qk{s}", [P, BLK]) for s in range(2)]
            qk_hi = [pool.sb(f"qk_hi{s}", [P, BLK], F32R) for s in range(2)]
            qk_lo = [pool.sb(f"qk_lo{s}", [P, BLK], F32R) for s in range(2)]
            sq_ready, sq_split, inv_ready = pool.sem("sq_ready"), pool.sem("sq_split"), pool.sem("inv_ready")
            hi_ready, lo_ready = pool.sem("hi_ready"), pool.sem("lo_ready")
            qk_stored = pool.sems("qk_stored", 2)
        if kinds[0] == "v":
            v_t = [pool.sb(f"v_t{s}", [P, BLK]) for s in range(2)]
            v_out = [pool.sb(f"v_out{s}", [P, BLK]) for s in range(2)]
            v_stored = pool.sems("v_stored", 2)
        block = ctx.enter_context(nc.Block())
        funcs = {"z": ACT.Silu, "g": ACT.Sigmoid}
        dram = {"z": t["z"], "g": t["g"]}
        gates = sum(k in funcs for k in kinds)

        def before(i, b):
            return 5 * i + (b - 1 if b else 0)

        def uses(i, b):
            return (3 * i if b % 2 == 0 else 2 * i) + b // 2

        @block.sync
        def _(sp):
            with sp.Fori(0, pairs) as i:
                for s in range(2):
                    sp.wait_ge(w_split, 2 * (2 * i + s))
                    sp.dma_start(w_raw[:].rearrange("p k c -> p (k c)"),
                                 flat(t["w_in"][bass.ds(2 * i + (first_tile + s), 1)])).then_inc(w_in, 16)

        @block.gpsimd
        def _(pool_e):
            def split_weights(i, s):
                n = 2 * i + s
                pool_e.wait_ge(w_in, 16 * n + 16)
                pool_e.wait_ge(acc_ready[s], NBLK * i)
                halves = [slice(q * KD // 2, (q + 1) * KD // 2) for q in range(2)]
                for q in halves:
                    last = pool_e.tensor_tensor(w_hi[s][:, q, :], w_raw[:, q, :],
                                                const["all_ones"][:].rearrange("p (k c) -> p k c", c=P), ALU.mult)
                last.then_inc(w_split, 1)
                pool_e.wait_ge(w_split, 2 * n + 1)
                pool_e.tensor_tensor(w_lo[s][:], w_raw[:], w_hi[s][:].bitcast(F32),
                                     ALU.subtract).then_inc(w_split, 1)

            def split_squares(i, b):
                m, s = NBLK * i + b, b % 2
                pool_e.wait_ge(sq_ready, 2 * m + 2)
                pool_e.tensor_tensor(sq_lo[s][:], sq[:], sq_hi[s][:].bitcast(F32),
                                     ALU.subtract).then_inc(sq_split, 1)

            def low_part(i, b):
                m = NBLK * i + b
                pool_e.wait_ge(hi_ready, m + 1)
                pool_e.wait_ge(qk_stored[b % 2], 32 * uses(i, b))
                pool_e.tensor_tensor(qk_lo[b % 2][:], qk[b % 2][:], qk_hi[b % 2][:].bitcast(F32),
                                     ALU.subtract).then_inc(lo_ready, 1)

            with pool_e.Fori(0, pairs) as i:
                split_weights(i, 0)
                split_weights(i, 1)
                if kinds[0] == "norm":
                    for b in range(NBLK + 1):
                        if b < NBLK:
                            split_squares(i, b)
                        if b:
                            low_part(i, b - 1)

        @block.scalar
        def _(act):
            def square(i, b):
                m = NBLK * i + b
                act.wait_ge(acc_ready[0], m + 1)
                act.wait_ge(sq_split, m)
                act.activation(sq[:], acc[b][:], ACT.Square).then_inc(sq_ready, 1)
                act.wait_ge(side_done, before(i, b))
                act.activation(sq_hi[b % 2][:], acc[b][:], ACT.Square).then_inc(sq_ready, 1)

            def take_root(i, b):
                act.wait_ge(side_done, NBLK * i + b + 1)
                act.wait_ge(lo_ready, before(i, b))
                act.activation(qk[b % 2][:], side[b % 2][:], ACT.Sqrt, bias=const["eps"][:],
                               scale=1.0 / HD).then_inc(side_read, 1)

            def high_part(i, b):
                act.wait_ge(bank_done[b], 2 * i + 1)
                act.wait_ge(qk_stored[b % 2], 32 * uses(i, b))
                act.activation(qk_hi[b % 2][:], qk[b % 2][:], ACT.Copy).then_inc(hi_ready, 1)

            def store_qk(i, b):
                act.wait_ge(lo_ready, NBLK * i + b + 1)
                cols = slice(b * BLK, (b + 1) * BLK)
                row = bass.ds(i, 1)
                act.dma_start(flat(t["qk_hi"][row, :, cols]), qk_hi[b % 2][:].bitcast(F32)).then_inc(qk_stored[b % 2], 16)
                act.dma_start(flat(t["qk_lo"][row, :, cols]), qk_lo[b % 2][:].bitcast(F32)).then_inc(qk_stored[b % 2], 16)

            def gate(i, s, b):
                act.wait_ge(acc_ready[s], NBLK * i + b + 1)
                turn = s if gates == 2 else 0
                act.wait_ge(stored, 16 * (gates * NBLK * i + (turn * NBLK + b)))
                act.activation(out[:], acc[b][:], funcs[kinds[s]]).then_inc(bank_done[b], 1)
                act.wait_ge(bank_done[b], 2 * i + s + 1)
                act.dma_start(flat(dram[kinds[s]][bass.ds(i + first_out[s], 1), :, b * BLK:(b + 1) * BLK]),
                              out[:]).then_inc(stored, 16)

            def copy_v(i, b):
                act.wait_ge(acc_ready[0], NBLK * i + b + 1)
                act.wait_ge(side_done, before(i, b))
                act.activation(v_t[b % 2][:], acc[b][:], ACT.Copy).then_inc(bank_done[b], 1)

            def store_v(i, b):
                act.wait_ge(side_read, NBLK * i + b + 1)
                act.dma_start(t["v"][b * BLK:(b + 1) * BLK, bass.ds(i * P, P)].rearrange("(n p) c -> p n c", p=P),
                              v_out[b % 2][:].rearrange("p (n c) -> p n c", c=P)).then_inc(v_stored[b % 2], 16)

            with act.Fori(0, pairs) as i:
                if kinds[0] == "norm":
                    for b in range(NBLK + 2):
                        if b < NBLK:
                            square(i, b)
                        if 1 <= b <= NBLK:
                            take_root(i, b - 1)
                        if b >= 2:
                            high_part(i, b - 2)
                        if b >= 3:
                            store_qk(i, b - 3)
                elif kinds[0] == "v":
                    for b in range(NBLK):
                        copy_v(i, b)
                        if b:
                            store_v(i, b - 1)
                    store_v(i, NBLK - 1)
                else:
                    for b in range(NBLK):
                        gate(i, 0, b)
                for b in range(NBLK):
                    gate(i, 1, b)
                    if b == 0 and kinds[0] == "norm":
                        store_qk(i, NBLK - 1)
            if kinds[0] == "norm":
                act.wait_ge(qk_stored[0], 32 * 3 * pairs)
                act.wait_ge(qk_stored[1], 32 * 2 * pairs)
            if kinds[0] == "v":
                act.wait_ge(v_stored[0], 16 * 3 * pairs)
                act.wait_ge(v_stored[1], 16 * 2 * pairs)
            act.wait_ge(stored, 16 * NBLK * gates * pairs)

        if kinds[0] in ("norm", "v"):
            @block.vector
            def _(dve):
                with dve.Fori(0, pairs) as i:
                    for b in range(NBLK):
                        m = NBLK * i + b
                        if kinds[0] == "norm":
                            dve.wait_ge(side_read, m + 1)
                            dve.reciprocal(qk[b % 2][:], qk[b % 2][:]).then_inc(inv_ready, 1)
                            dve.wait_ge(inv_ready, m + 1)
                            dve.scalar_tensor_tensor(qk[b % 2][:], acc[b][:], const["gains"][:, bass.ds(i, 1)], qk[b % 2][:],
                                                     ALU.mult, ALU.mult).then_inc(bank_done[b], 1)
                        else:
                            dve.wait_ge(side_done, m + 1)
                            dve.wait_ge(v_stored[b % 2], 16 * uses(i, b))
                            dve.tensor_copy(v_out[b % 2][:], side[b % 2][:]).then_inc(side_read, 1)

        @block.tensor
        def _(pe):
            def head_sums(i, b):
                m, s = NBLK * i + b, b % 2
                pe.wait_ge(sq_split, m + 1)
                pe.wait_ge(side_read, before(i, b))
                pe.matmul(side[s][:], const["head_ones"][:], sq_hi[s][:], start=True, stop=False)
                pe.matmul(side[s][:], const["head_ones"][:], sq_lo[s][:], start=False, stop=True).then_inc(side_done, 1)

            def turn_v(i, b):
                s = b % 2
                pe.wait_ge(bank_done[b], 2 * i + 1)
                pe.wait_ge(side_read, before(i, b))
                for n in range(BLK // P):
                    last = pe.transpose(side[s][:, n * P:(n + 1) * P], v_t[s][:, n * P:(n + 1) * P], const["ident"][:])
                last.then_inc(side_done, 1)

            after = {"norm": head_sums, "v": turn_v}.get(kinds[0])
            with pe.Fori(0, pairs) as i:
                for s in range(2):
                    pe.wait_ge(w_split, 2 * (2 * i + s) + 2)
                    for b in range(NBLK):
                        cols = slice(b * BLK, (b + 1) * BLK)
                        pe.wait_ge(bank_done[b], 2 * i + s)
                        for k in range(KD):
                            pe.matmul(acc[b][:], w_hi[s][:, k, :], h_hi[:, k, cols], start=(k == 0), stop=False)
                            pe.matmul(acc[b][:], w_hi[s][:, k, :], h_lo[:, k, cols], start=False, stop=False)
                            last = pe.matmul(acc[b][:], w_lo[s][:, k, :], h_hi[:, k, cols], start=False,
                                             stop=(k == KD - 1))
                        last.then_inc(acc_ready[s], 1)
                        if after and s == 0 and b:
                            after(i, b - 1)
                        if after and s == 1 and b == 0:
                            after(i, NBLK - 1)


def stage_attend_a(nc, t, const, tag, tok0, T):
    nq = T // P
    n_key = T // P
    chunk = min(2 * BLK, T)
    n_chunk = T // chunk
    per_unit = 2 * n_chunk
    groups = T // BLK
    units = 2 * nq
    blocks = units // 2
    head_blocks = blocks // 2
    rounds = H_A // 2
    bias_w = 2 * T - P
    with ExitStack() as ctx:
        pool = Pool(nc, ctx, tag)
        q = [[pool.sb(f"q{s}{c}", [P, T], F32R) for c in range(2)] for s in range(2)]
        k_hi = [[pool.sb(f"k_hi{s}{c}", [P, T], F32R) for c in range(2)] for s in range(2)]
        k_lo = [pool.sb(f"k_lo{s}", [P, T], F32R) for s in range(2)]
        v = [pool.sb(f"v{s}", [P, n_key, P]) for s in range(2)]
        bias = pool.sb("bias", [P, bias_w])
        prob = [[pool.sb(f"prob{c}{s}", [P, T]) for s in range(3 - c)] for c in range(2)]
        stat = [pool.sb(f"stat{s}", [P, 12]) for s in range(2)]
        tick = pool.sb("tick", [P, 2])
        turned = [pool.sb(f"turned{s}", [P, n_key, 2 * P]) for s in range(2)]
        o_sb = [pool.sb(f"o_sb{s}", [P, 2 * P]) for s in range(2)]
        score = [pool.ps(f"score{s}", [P, chunk]) for s in range(2)]
        turn = [pool.ps(f"turn{s}", [P, BLK]) for s in range(2)]
        o_ps = [pool.ps(f"o_ps{s}", [P, BLK]) for s in range(2)]
        bias_in, bias_made = pool.sem("bias_in"), pool.sem("bias_made")
        map_in, v_in = [pool.sems(f"map_in{s}", 2) for s in range(2)], pool.sems("v_in", 2)
        scored, masked, max_ready = pool.sem("scored"), pool.sem("masked"), pool.sem("max_ready")
        exp_done, inv0, scaled0 = pool.sem("exp_done"), pool.sem("inv0"), pool.sem("scaled0")
        inv1, factor1, mapped = pool.sem("inv1"), pool.sem("factor1"), pool.sem("mapped")
        turn_done, turn_read = pool.sem("turn_done"), pool.sem("turn_read")
        applied, o_done, o_stored = pool.sems("applied", 2), pool.sem("o_done"), pool.sems("o_stored", 2)
        block = ctx.enter_context(nc.Block())
        toks = slice(tok0, tok0 + T)

        @block.sync
        def _(sp):
            with sp.Fori(0, rounds) as g:
                for s in range(2):
                    sp.wait_ge(applied[s], head_blocks * g)
                    q_tile, k_tile = bass.ds(2 * g + s, 1), bass.ds(2 * g + (H_A + s), 1)
                    for c in range(2):
                        rows, other = slice(c * HD, (c + 1) * HD), slice((1 - c) * HD, (2 - c) * HD)
                        hi, lo = t["qk_hi"], t["qk_lo"]
                        sp.dma_start(q[s][c][rows, :].bitcast(F32), flat(hi[q_tile, rows, toks])).then_inc(map_in[s][c], 16)
                        sp.dma_start(q[s][c][other, :].bitcast(F32), flat(lo[q_tile, rows, toks])).then_inc(map_in[s][c], 16)
                        sp.dma_start(k_hi[s][c][0:HD, :].bitcast(F32), flat(hi[k_tile, rows, toks])).then_inc(map_in[s][c], 16)
                        sp.dma_start(k_hi[s][c][HD:P, :].bitcast(F32), flat(hi[k_tile, rows, toks])).then_inc(map_in[s][c], 16)
                        sp.dma_start(k_lo[s][rows, :].bitcast(F32), flat(lo[k_tile, rows, toks])).then_inc(map_in[s][c], 16)
                    sp.dma_start(v[s][:], t["v"][toks, bass.ds((2 * g + s) * P, P)].rearrange("(n p) c -> p n c", p=P)).then_inc(v_in[s], 16)

        @block.gpsimd
        def _(pool_e):
            pool_e.dma_start(bias[:], t["alibi"][:, T_SAMPLE - T:T_SAMPLE - T + bias_w]).then_inc(bias_in, 16)
            with pool_e.Fori(0, rounds) as g:
                for u in range(units):
                    pool_e.wait_ge(inv0, units * g + (u + 1))
                    p = prob[0][u % 3]
                    pool_e.tensor_tensor(p[:], p[:], stat[u % 2][:, 8:9].broadcast_to([P, T]), ALU.mult).then_inc(scaled0, 1)

        @block.vector
        def _(dve):
            def scores_of(g, u, c, j):
                p, st = prob[c][u % (3 - c)], stat[u % 2]
                n = u * per_unit + c * n_chunk + j
                dve.wait_ge(scored, g * (units * per_unit) + (n + 1))
                if c == 0:
                    dve.wait_ge(turn_done, g * (units * groups) + max(u - 2, 0) * groups)
                else:
                    dve.wait_ge(mapped, units * g + max(u - 1, 0))
                dve.memset(tick[:, n % 2:n % 2 + 1], 0.0)
                at = j * chunk - (u % nq) * P + (T - P)
                dve.tensor_tensor_reduce(out=p[:, j * chunk:(j + 1) * chunk], in0=score[n % 2][:],
                                         in1=bias[:, at:at + chunk], scale=1.0, scalar=-3e38, op0=ALU.add,
                                         op1=ALU.max, accum_out=st[:, 2 * c + j:2 * c + j + 1]).then_inc(masked, 1)

            def maximum(g, u, c):
                st = stat[u % 2]
                dve.wait_ge(masked, g * (units * per_unit) + u * per_unit + (c + 1) * n_chunk)
                dve.tensor_reduce(st[:, 4 + c:5 + c], st[:, 2 * c:2 * c + n_chunk], axis=AX.X, op=ALU.max,
                                  negate=True).then_inc(max_ready, 1)

            def combine(g, u):
                st, n = stat[u % 2], units * g + (u + 1)
                dve.wait_ge(exp_done, 2 * n)
                dve.reciprocal(st[:, 9:10], st[:, 7:8]).then_inc(inv1, 1)
                dve.wait_ge(inv1, n)
                dve.tensor_tensor(st[:, 10:11], st[:, 9:10], const["neg_lam"][:], ALU.mult).then_inc(factor1, 1)
                dve.wait_ge(factor1, n)
                dve.wait_ge(scaled0, n)
                dve.scalar_tensor_tensor(prob[0][u % 3][:], prob[1][u % 2][:], st[:, 10:11], prob[0][u % 3][:],
                                         ALU.mult, ALU.add).then_inc(mapped, 1)

            dve.wait_ge(bias_in, 16)
            with dve.Fori(0, rounds) as g:
                for u in range(units + 1):
                    if u < units:
                        if u % nq == 0:
                            dve.tensor_scalar(bias[:], bias[:], 0.25, None, ALU.mult).then_inc(bias_made, 1)
                            dve.wait_ge(bias_made, 2 * g + (u // nq + 1))
                        for j in range(n_chunk):
                            scores_of(g, u, 0, j)
                        maximum(g, u, 0)
                    if u:
                        combine(g, u - 1)
                    if u < units:
                        scores_of(g, u, 1, 0)
                        dve.wait_ge(exp_done, 2 * (units * g + u) + 1)
                        dve.reciprocal(stat[u % 2][:, 8:9], stat[u % 2][:, 6:7]).then_inc(inv0, 1)
                        for j in range(1, n_chunk):
                            scores_of(g, u, 1, j)
                        maximum(g, u, 1)

        @block.scalar
        def _(act):
            def exponent(g, u, c):
                st, p = stat[u % 2], prob[c][u % (3 - c)]
                act.wait_ge(max_ready, 2 * (units * g + u) + (c + 1))
                act.activation(p[:], p[:], ACT.Exp, bias=st[:, 4 + c:5 + c],
                               accum_out=st[:, 6 + c:7 + c]).then_inc(exp_done, 1)

            def take_turned(g, u, which):
                b = u // 2
                s, own = b // head_blocks, b % head_blocks
                for n in which:
                    act.wait_ge(turn_done, g * (units * groups) + u * groups + n + 1)
                    if own >= 2:
                        act.wait_ge(applied[s], head_blocks * g + (own - 1))
                    elif s == 1:
                        act.wait_ge(applied[0], head_blocks * g + (head_blocks - 1 + own))
                    else:
                        act.wait_ge(applied[1], head_blocks * g)
                    act.activation(turned[b % 2][:, 4 * n:4 * n + 4, (u % 2) * P:(u % 2 + 1) * P],
                                   turn[(u * groups + n) % 2][:].rearrange("p (k c) -> p k c", c=P),
                                   ACT.Copy).then_inc(turn_read, 1)

            def take_output(g, b):
                s, own = b // head_blocks, b % head_blocks
                act.wait_ge(applied[s], head_blocks * g + (own + 1))
                act.wait_ge(o_stored[b % 2], 16 * ((blocks // 2) * g + b // 2))
                act.activation(o_sb[b % 2][:], o_ps[b % 2][:, 0:2 * P], ACT.Copy).then_inc(o_done, 1)

            def store(g, b):
                s, at = b // head_blocks, (b % head_blocks) * 2 * P
                act.wait_ge(o_done, blocks * g + (b + 1))
                act.dma_start(flat(t["o"][bass.ds(2 * g + s, 1), :, tok0 + at:tok0 + at + 2 * P]),
                              o_sb[b % 2][:]).then_inc(o_stored[b % 2], 16)

            half = groups // 2
            with act.Fori(0, rounds) as g:
                for step in range(units + 6):
                    u = step
                    if step >= 7 and step % 2 == 1:
                        store(g, (step - 7) // 2)
                    if 1 <= step <= units:
                        exponent(g, u - 1, 1)
                    if 2 <= step < units + 2:
                        take_turned(g, u - 2, range(half))
                    if u < units:
                        exponent(g, u, 0)
                    if 2 <= step < units + 2:
                        take_turned(g, u - 2, range(half, groups))
                    if step >= 6 and step % 2 == 0:
                        take_output(g, (step - 6) // 2)
            for s in range(2):
                act.wait_ge(o_stored[s], 16 * (blocks // 2) * rounds)

        @block.tensor
        def _(pe):
            def scores(g, u, j):
                s, qt = u // nq, u % nq
                n = u * per_unit + j
                c, at = j // n_chunk, (j % n_chunk) * chunk
                if qt == 0 and j % n_chunk == 0:
                    pe.wait_ge(map_in[s][c], 16 * 5 * (g + 1))
                pe.wait_ge(masked, g * (units * per_unit) + max(n - 1, 0))
                rows, low = slice(qt * P, (qt + 1) * P), slice(c * HD, (c + 1) * HD)
                for b in range(0, chunk, BLK):
                    pe.matmul(score[n % 2][:, b:b + BLK], q[s][c][:, rows], k_hi[s][c][:, at + b:at + b + BLK],
                              start=True, stop=False)
                    last = pe.matmul(score[n % 2][:, b:b + BLK], q[s][c][low, rows],
                                     k_lo[s][low, at + b:at + b + BLK], start=False, stop=True)
                last.then_inc(scored, 1)

            def turn_maps(g, u, n):
                gid = u * groups + n
                pe.wait_ge(mapped, units * g + (u + 1))
                pe.wait_ge(turn_read, g * (units * groups) + max(gid - 1, 0))
                for k in range(4):
                    at = (4 * n + k) * P
                    last = pe.transpose(turn[gid % 2][:, k * P:(k + 1) * P], prob[0][u % 3][:, at:at + P],
                                        const["ident"][:])
                last.then_inc(turn_done, 1)

            def apply(g, b, piece):
                s = b // head_blocks
                if piece == 0:
                    pe.wait_ge(v_in[s], 16 * (g + 1))
                    pe.wait_ge(turn_read, g * (units * groups) + (2 * b + 2) * groups)
                    pe.wait_ge(o_done, blocks * g + max(b - 1, 0))
                for k in range(piece * n_key // 8, (piece + 1) * n_key // 8):
                    last = pe.matmul(o_ps[b % 2][:, 0:2 * P], v[s][:, k, :], turned[b % 2][:, k, :],
                                     start=(k == 0), stop=(k == n_key - 1))
                if piece == 7:
                    last.then_inc(applied[s], 1)

            with pe.Fori(0, rounds) as g:
                for step in range(units + 4):
                    for j in range(4):
                        if step < units and j < per_unit:
                            scores(g, step, j)
                        if step >= 4:
                            apply(g, (step - 4) // 2, 4 * (step % 2) + j)
                        if 2 <= step < units + 2 and j < groups:
                            turn_maps(g, step - 2, j)


def stage_attend_window(nc, t, const, tag, tok0, T, heads, per_round, q_tile, kv_of, n_kv, window, width, tables,
                        sink, o_tile):
    nt = T // P
    units = per_round * nt
    rounds = heads // per_round
    lag = 7
    group = 4
    n_turn = 1 if width > BLK else 2
    stores = per_round // 2
    with ExitStack() as ctx:
        pool = Pool(nc, ctx, tag)
        q = [pool.sb(f"q{s}", [P, T], F32R) for s in range(per_round)]
        k_hi = [pool.sb(f"k_hi{s}", [P, T], F32R) for s in range(n_kv)]
        k_lo = [pool.sb(f"k_lo{s}", [P, T], F32R) for s in range(n_kv)]
        v = [pool.sb(f"v{s}", [P, nt, HD]) for s in range(n_kv)]
        table = [pool.sb(f"table{s}", [P, tables["width"]]) for s in range(2)]
        prob = [pool.sb(f"prob{s}", [P, width]) for s in range(4)]
        turned = [pool.sb(f"turned{s}", [P, width]) for s in range(2)]
        stat = [pool.sb(f"stat{s}", [P, 6]) for s in range(8)]
        sinks = pool.sb("sinks", [P, per_round])
        tick = pool.sb("tick", [P, 1])
        o_sb = pool.sb("o_sb", [P, per_round // 2, T])
        score = [pool.ps(f"score{s}", [P, width if width <= BLK else 2 * BLK]) for s in range(2)]
        turn = [pool.ps(f"turn{s}", [P, width if width <= BLK else 2 * BLK]) for s in range(n_turn)]
        o_ps = [pool.ps(f"o_ps{s}", [P, BLK]) for s in range(2)]
        q_in, k_in, v_in = pool.sems("q_in", per_round), pool.sems("k_in", n_kv), pool.sems("v_in", n_kv)
        tab_done, sink_done = pool.sem("tab_done"), pool.sem("sink_done")
        scored, masked, max_ready = pool.sem("scored"), pool.sem("masked"), pool.sem("max_ready")
        exp_done, sum_done, inv, divided = pool.sem("exp_done"), pool.sem("sum_done"), pool.sem("inv"), pool.sem("divided")
        turn_done, read_a, read_b = pool.sem("turn_done"), pool.sem("read_a"), pool.sem("read_b")
        applied, o_done, o_stored = pool.sem("applied"), pool.sem("o_done"), pool.sem("o_stored")
        block = ctx.enter_context(nc.Block())
        toks = slice(tok0, tok0 + T)
        per_exp = 2 if sink else 1
        wide = [sum(window(m % nt)[1] * P > BLK for m in range(u)) for u in range(units + 1)]

        def done(g, n):
            return max(units * g + n, 0) if isinstance(g, int) else units * g + n

        def done_wide(g, n):
            if isinstance(g, int):
                return wide[units] * g + wide[n] if n >= 0 else max(wide[units] * (g - 1) + wide[n + units], 0)
            return wide[units] * g + (wide[n] if n >= 0 else wide[n + units] - wide[units])

        def groups_done(g, n):
            per = units // group
            return max(per * g + n, 0) if isinstance(g, int) else per * g + n

        def steps(g, last):
            return range(units + lag if last else units)

        def live(g, u):
            return u < units and (u >= 0 or not (isinstance(g, int) and g == 0))

        def run(eng, round_of):
            round_of(0, False)
            if rounds > 2:
                with eng.Fori(1, rounds - 1) as g:
                    round_of(g, False)
            round_of(rounds - 1, True)

        @block.sync
        def _(sp):
            def round_of(g, last):
                for s in range(per_round):
                    n, keys = kv_of(g, s)
                    sp.wait_ge(scored, done(g - 1, (s + 1) * nt))
                    if keys:
                        k_tile, k_rows, v_cols = keys
                        for dst, src in ((k_hi[n][0:HD, :], t["qk_hi"]), (k_hi[n][HD:P, :], t["qk_hi"]),
                                         (k_lo[n][0:HD, :], t["qk_lo"])):
                            sp.dma_start(dst.bitcast(F32), flat(src[k_tile, k_rows, toks])).then_inc(k_in[n], 16)
                    tile = bass.ds(g * (per_round // 2) + (q_tile + s // 2), 1)
                    rows = slice((s % 2) * HD, (s % 2 + 1) * HD)
                    sp.dma_start(q[s][0:HD, :].bitcast(F32), flat(t["qk_hi"][tile, rows, toks])).then_inc(q_in[s], 16)
                    sp.dma_start(q[s][HD:P, :].bitcast(F32), flat(t["qk_lo"][tile, rows, toks])).then_inc(q_in[s], 16)
                    if keys:
                        sp.wait_ge(applied, done(g - 1, (s + 1) * nt))
                        sp.dma_start(v[n][:], t["v"][toks, v_cols].rearrange("(n p) c -> p n c", p=P)).then_inc(v_in[n], 16)

            tables["load_first"](sp)
            round_of(0, False)
            tables["load_rest"](sp)
            if rounds > 2:
                with sp.Fori(1, rounds - 1) as g:
                    round_of(g, False)
            round_of(rounds - 1, True)

        @block.gpsimd
        def _(pool_e):
            def divide(g, u):
                w, st = window(u % nt)[1] * P, stat[u % 8]
                pool_e.wait_ge(inv, done(g, u + 1))
                pool_e.tensor_tensor(prob[u % 4][:, 0:w], prob[u % 4][:, 0:w], st[:, 4:5].broadcast_to([P, w]),
                                     ALU.mult).then_inc(divided, 1)

            def round_of(g, last):
                for step in steps(g, last):
                    if live(g, step - 2):
                        divide(g, step - 2)

            run(pool_e, round_of)

        @block.vector
        def _(dve):
            def take_turned(g, u):
                w = window(u % nt)[1] * P
                if w > BLK:
                    dve.wait_ge(turn_done, done(g, u + 1))
                    dve.wait_ge(applied, done(g, u - 1))
                    dve.tensor_copy(turned[u % 2][:, BLK:w], turn[u % n_turn][:, BLK:w]).then_inc(read_b, 1)

            def invert_sum(g, u):
                st = stat[u % 8]
                dve.wait_ge(exp_done, per_exp * done(g, u + 1))
                if sink:
                    dve.tensor_tensor(st[:, 2:3], st[:, 2:3], st[:, 3:4], ALU.add).then_inc(sum_done, 1)
                    dve.wait_ge(sum_done, done(g, u + 1))
                dve.reciprocal(st[:, 4:5], st[:, 2:3]).then_inc(inv, 1)

            def take_output(g, u):
                m = (u % units) // group
                s, at = m * group // nt, (m * group % nt) * P
                rows = slice((s % 2) * HD, (s % 2 + 1) * HD)
                dve.wait_ge(applied, done(g, u + 1))
                dve.wait_ge(o_stored, 16 * stores * (g if u >= 0 else g - 1))
                dve.tensor_copy(o_sb[rows, s // 2, at:at + group * P], o_ps[m % 2][rows, :]).then_inc(o_done, 1)

            def scores_of(g, u):
                s, n = u // nt, u % nt
                first, count, col = window(n)
                w = count * P
                dve.wait_ge(scored, done(g, u + 1))
                dve.wait_ge(turn_done, done(g, u - 3))
                dve.memset(tick[:], 0.0)
                dve.tensor_tensor_reduce(out=prob[u % 4][:, 0:w], in0=score[u % 2][:, 0:w],
                                         in1=table[s % 2][:, col:col + w], scale=1.0,
                                         scalar=(sinks[:, s:s + 1] if sink else -3e38), op0=ALU.add, op1=ALU.max,
                                         accum_out=stat[u % 8][:, 0:1]).then_inc(masked, 1)
                dve.wait_ge(masked, done(g, u + 1))
                dve.tensor_scalar(stat[u % 8][:, 1:2], stat[u % 8][:, 0:1], -1.0, None, ALU.mult).then_inc(max_ready, 1)

            def round_of(g, last):
                for step in steps(g, last):
                    if live(g, step - 4):
                        take_turned(g, step - 4)
                    if live(g, step - 2):
                        invert_sum(g, step - 2)
                    if (step - 5) % group == group - 1 and live(g, step - 5):
                        take_output(g, step - 5)
                    if step < units:
                        if step == 0 and sink:
                            dve.wait_ge(exp_done, per_exp * done(g, 0))
                            dve.tensor_copy(sinks[:], const["sink"][:, bass.ds(g * per_round, per_round)]).then_inc(sink_done, 1)
                            dve.wait_ge(sink_done, g + 1)
                        if step % nt == 0:
                            tables["make"](dve, g, step // nt, per_round, table[step // nt % 2], tab_done)
                        scores_of(g, step)
                        tables["with_unit"](dve, g, step)

            run(dve, round_of)

        @block.scalar
        def _(act):
            def take_turned(g, u):
                w = min(window(u % nt)[1] * P, BLK)
                act.wait_ge(turn_done, done(g, u + 1))
                act.wait_ge(applied, done(g, u - 1))
                act.activation(turned[u % 2][:, 0:w], turn[u % n_turn][:, 0:w], ACT.Copy).then_inc(read_a, 1)

            def exponent(g, u):
                s, w, st = u % units // nt, window(u % nt)[1] * P, stat[u % 8]
                act.wait_ge(max_ready, done(g, u + 1))
                act.activation(prob[u % 4][:, 0:w], prob[u % 4][:, 0:w], ACT.Exp, bias=st[:, 1:2],
                               accum_out=st[:, 2:3]).then_inc(exp_done, 1)
                if sink:
                    act.activation(st[:, 3:4], sinks[:, s:s + 1], ACT.Exp, bias=st[:, 1:2]).then_inc(exp_done, 1)

            def store(g, round_before):
                n = g if round_before else g + 1
                act.wait_ge(o_done, groups_done(n, 0))
                for c in range(stores):
                    tile = bass.ds(n * stores + (o_tile - stores + c), 1)
                    act.dma_start(flat(t["o"][tile, :, toks]), o_sb[:, c, :]).then_inc(o_stored, 16)

            def round_of(g, last):
                for step in steps(g, last):
                    if live(g, step - 4):
                        take_turned(g, step - 4)
                    if live(g, step - 1):
                        exponent(g, step - 1)
                    if step == 6 and live(g, -1):
                        store(g, True)
                    if step == units + 6:
                        store(g, False)

            run(act, round_of)
            act.wait_ge(o_stored, 16 * stores * rounds)

        @block.tensor
        def _(pe):
            def scores(g, u):
                s, n = u // nt, u % nt
                kv, _ = kv_of(g, s)
                first, count, _ = window(n)
                if n == 0:
                    pe.wait_ge(q_in[s], 32 * (g + 1))
                    pe.wait_ge(k_in[kv], 48 * (g + 1 if n_kv == per_round else 1))
                pe.wait_ge(masked, done(g, u - 1))
                rows = slice(n * P, (n + 1) * P)
                for a in range(0, count * P, BLK):
                    w = min(BLK, count * P - a)
                    at = first * P + a
                    pe.matmul(score[u % 2][:, a:a + w], q[s][:, rows], k_hi[kv][:, at:at + w],
                              start=True, stop=False)
                    last = pe.matmul(score[u % 2][:, a:a + w], q[s][0:HD, rows], k_lo[kv][0:HD, at:at + w],
                                     start=False, stop=True)
                last.then_inc(scored, 1)

            def turn_map(g, u):
                pe.wait_ge(divided, done(g, u + 1))
                pe.wait_ge(read_a, done(g, u + 1 - n_turn))
                if wide[units]:
                    pe.wait_ge(read_b, done_wide(g, u + 1 - n_turn))
                for k in range(window(u % nt)[1]):
                    last = pe.transpose(turn[u % n_turn][:, k * P:(k + 1) * P], prob[u % 4][:, k * P:(k + 1) * P],
                                        const["ident"][:])
                last.then_inc(turn_done, 1)

            def apply(g, u):
                before, m = u < 0, (u % units) // group
                s, n = u % units // nt, u % nt
                kv, _ = kv_of(g - 1 if before else g, s)
                first, count, _ = window(n)
                if n == 0:
                    pe.wait_ge(v_in[kv], 16 * ((g if before else g + 1) if n_kv == per_round else 1))
                pe.wait_ge(read_a, done(g, u + 1))
                if wide[units]:
                    pe.wait_ge(read_b, done_wide(g, u + 1))
                if u % group == 0:
                    pe.wait_ge(o_done, groups_done(g, u // group - 1))
                rows, at = slice((s % 2) * HD, (s % 2 + 1) * HD), u % group * P
                for k in range(count):
                    last = pe.matmul(o_ps[m % 2][rows, at:at + P], v[kv][:, first + k, :],
                                     turned[u % 2][:, k * P:(k + 1) * P], start=(k == 0), stop=(k == count - 1))
                last.then_inc(applied, 1)

            def round_of(g, last):
                for step in steps(g, last):
                    if step < units:
                        scores(g, step)
                    if live(g, step - 3):
                        turn_map(g, step - 3)
                    if live(g, step - 4):
                        apply(g, step - 4)

            run(pe, round_of)


def stage_attend_grid(nc, t, const):
    full, inner = 14 * GRID_W, 10 * GRID_W
    with ExitStack() as ctx:
        pool = Pool(nc, ctx, "grid")
        bias = pool.sb("bias", [P, H_B, full])
        raw = pool.sb("raw", [P, H_B, 14, GRID_W])
        col_mask = pool.sb("col_mask", [P, full])
        row_mask = pool.sb("row_mask", [P, inner])
        first_in, rest_in, forward = pool.sem("first_in"), pool.sem("rest_in"), pool.sem("forward")

        def load_head(sp, h, loaded):
            for a in range(2):
                start = (h * BIAS_ROWS + 1 - a) * PAD_W + 1
                src = bass.AP(t["rpb_pad"].tensor, start, [[1, GRID_W], [PAD_W, 14], [1, GRID_W]])
                sp.dma_start(raw[a * GRID_W:(a + 1) * GRID_W, h, :, :], src).then_inc(loaded, 16)

        def load_first(sp):
            sp.dma_start(col_mask[:], t["col_mask"]).then_inc(first_in, 16)
            sp.dma_start(row_mask[:], t["row_mask"]).then_inc(first_in, 16)
            load_head(sp, 0, first_in)

        def load_rest(sp):
            for h in range(1, H_B):
                load_head(sp, h, rest_in)

        def turn_rows(dve, h):
            dve.tensor_tensor(bias[:, h, :].rearrange("p (e c) -> p e c", c=GRID_W), raw[:, h, :, ::-1],
                              col_mask[:].rearrange("p (e c) -> p e c", c=GRID_W), ALU.add).then_inc(forward, 1)

        def make(dve, g, s, per_round, table, done):
            n = 2 * per_round * g + 2 * s
            dve.tensor_copy(table[:, 0:full], bias[:, bass.ds(g * per_round + s, 1), :].rearrange("p a n -> p (a n)")
                            ).then_inc(done, 1)
            dve.wait_ge(done, n + 1)
            dve.tensor_tensor(table[:, full:full + inner], table[:, 2 * GRID_W:2 * GRID_W + inner], row_mask[:],
                              ALU.add).then_inc(done, 1)
            dve.wait_ge(done, n + 2)

        def load_and_make(dve, g, s, per_round, table, done):
            if isinstance(g, int) and g == 0 and s == 0:
                dve.wait_ge(first_in, 16 * 4)
                turn_rows(dve, 0)
                dve.wait_ge(forward, 1)
            if isinstance(g, int) and g == 0 and s == 1:
                dve.wait_ge(rest_in, 16 * 2 * (H_B - 1))
                turn_rows(dve, 1)
                dve.wait_ge(forward, 2)
            if s == 0 and not (isinstance(g, int) and g == 0):
                dve.wait_ge(forward, H_B)
            make(dve, g, s, per_round, table, done)

        def turn_more(dve, g, step):
            h = (step - 18) // 2 + 2
            if isinstance(g, int) and g == 0 and step % 2 == 0 and 2 <= h < H_B:
                turn_rows(dve, h)

        for tag, (tok0, T) in zip(("gs", "gp"), SEQS):
            nt = T // P
            tables = {"width": full + inner, "load_first": load_first, "load_rest": load_rest, "make": load_and_make,
                      "with_unit": turn_more}
            if tok0:
                tables.update(load_first=lambda sp: None, load_rest=lambda sp: None, make=make,
                              with_unit=lambda dve, g, step: None)

            def window(n, nt=nt):
                if nt > 4 and 2 <= n < nt - 2:
                    return n - 2, 5, full
                first = 0 if n < nt - 2 or nt == 4 else nt - 4
                return first, 4, (first - n + 3) * P

            def kv_of(g, s):
                return s, (bass.ds(g + 12, 1), slice(s * HD, (s + 1) * HD), bass.ds(g * P + (512 + s * HD), HD))

            stage_attend_window(nc, t, const, tag, tok0, T, H_B, 2, 8, kv_of, 2, window, 5 * P if nt > 4 else 4 * P,
                                tables, False, H_A)


def stage_attend_slide(nc, t, const):
    with ExitStack() as ctx:
        pool = Pool(nc, ctx, "slide")
        mask = pool.sb("mask", [P, 3 * P])
        for tag, (tok0, T) in zip(("ss", "sp"), SEQS):
            with ExitStack() as own:
                inner = Pool(nc, own, tag + "t")
                dist = inner.sb("dist", [P, 3 * P])
                loaded = inner.sem("loaded")

                def load_first(sp):
                    sp.dma_start(dist[:], t["slide_dist"]).then_inc(loaded, 16)
                    sp.dma_start(mask[:], t["slide_mask"]).then_inc(loaded, 16)

                def make(dve, g, s, per_round, table, done):
                    n = 2 * per_round * g + 2 * s
                    dve.wait_ge(loaded, 32)
                    dve.tensor_scalar(dist[:], dist[:], 0.5, None, ALU.mult).then_inc(done, 1)
                    dve.wait_ge(done, n + 1)
                    dve.tensor_tensor(table[:], dist[:], mask[:], ALU.add).then_inc(done, 1)
                    dve.wait_ge(done, n + 2)

                nt = T // P

                def window(n, nt=nt):
                    first, end = max(n - 1, 0), min(n + 2, nt)
                    return first, end - first, (first - n + 1) * P

                def kv_of(g, s):
                    return g, (slice(20, 21), slice(g * HD, (g + 1) * HD), slice(1024 + g * HD, 1024 + (g + 1) * HD)) if s == 0 else None

                tables = {"width": 3 * P, "load_first": load_first, "load_rest": lambda sp: None, "make": make,
                          "with_unit": lambda dve, g, step: None}
                stage_attend_window(nc, t, const, tag, tok0, T, H_C, 4, 16, kv_of, KV_C, window, 3 * P,
                                    tables, True, H_A + H_B // 2)


def stage_merge(nc, t, const):
    n_u = 12
    row_tiles = BLK // P
    halves = D // BLK
    y_jobs = [(r, e) for r in range(row_tiles) for e in range(halves)]
    n_y = len(y_jobs)
    last_blk = NBLK - 1
    order = [0, 4, 1, 5, 2, 6, 3, 7, 8, 9, 10, 11]

    def preps(j):
        return [p for p in (2 * j - 1, 2 * j) if 0 <= p < n_u]

    def in_a(p):
        return order[p] < H_A

    with ExitStack() as ctx:
        pool = Pool(nc, ctx, "mrg")
        wo_hi = pool.sb("wo_hi", [P, KD, D], F32R)
        wo_lo = pool.sb("wo_lo", [P, KD, D], F32R)
        w_raw = [pool.sb(f"w_raw{s}", [P, n_u * P]) for s in range(2)]
        wp_hi = [pool.sb(f"wp_hi{s}", [P, n_u, P], F32R) for s in range(2)]
        wp_lo = [pool.sb(f"wp_lo{s}", [P, n_u, P], F32R) for s in range(2)]
        u_hi = pool.sb("u_hi", [P, n_u, BLK], F32R)
        u_lo = pool.sb("u_lo", [P, n_u, BLK], F32R)
        m_hi = pool.sb("m_hi", [P, KD, BLK], F32R)
        m_lo = pool.sb("m_lo", [P, KD, BLK], F32R)
        root = pool.sb("root", [P, BLK])
        g_in = pool.sb("g_in", [P, 3, BLK])
        m = pool.sb("m", [P, BLK])
        part = pool.sb("part", [P, BLK])
        o_in = [pool.sb(f"o_in{s}", [P, BLK]) for s in range(2)] + [part]
        z_in = [pool.sb(f"z_in{s}", [P, BLK]) for s in range(2)] + [m]
        xy = [pool.sb(f"xy{s}", [P, BLK]) for s in range(2)]
        acc = [pool.ps(f"acc{b}", [P, BLK]) for b in range(3)]
        y_ps = [pool.ps(f"y_ps{s}", [P, BLK]) for s in range(2)]
        sums = pool.ps("sums", [P, BLK])
        wo_in, wo_high, wo_low = pool.sems("wo_in", 2), pool.sem("wo_high"), pool.sem("wo_low")
        w_in, wp_high, wp_low = pool.sems("w_in", 2), pool.sem("wp_high"), pool.sem("wp_low")
        oz_in = pool.sems("oz_in", 3)
        squared, summed, rooted, inverted, normed = (pool.sem(n) for n in ("squared", "summed", "rooted", "inverted", "normed"))
        u_made, u_high, u_low = pool.sem("u_made"), pool.sem("u_high"), pool.sem("u_low")
        acc_ready, gated, g_loaded = pool.sem("acc_ready"), pool.sem("gated"), pool.sems("g_loaded", 3)
        m_high, m_low = pool.sem("m_high"), pool.sem("m_low")
        x_in, y_ready, y_added, y_stored = pool.sems("x_in", 2), pool.sem("y_ready"), pool.sem("y_added"), pool.sems("y_stored", 2)
        block = ctx.enter_context(nc.Block())

        def product_step(n, b):
            return 5 * n + (1, 2, 4)[b]

        @block.sync
        def _(sp):
            def load_prep(i, p):
                n, s = order[p], p % 3
                sp.wait_ge(u_low, n_u * i + max(p - 2, 0))
                if p == 2:
                    sp.wait_ge(m_low, KD * i)
                cols = bass.ds(i * BLK, BLK)
                sp.dma_start(o_in[s][:], t["o"][n, :, cols]).then_inc(oz_in[s], 16)
                sp.dma_start(z_in[s][:], t["z"][n, :, cols]).then_inc(oz_in[s], 16)

            def load_weights(i, d):
                sp.wait_ge(wp_low, KD * i + max(d - 1, 0))
                sp.dma_start(w_raw[d % 2][:], t["w_proj"][d]).then_inc(w_in[d % 2], 16)

            def load_gates(i, d):
                for b in range(3):
                    sp.wait_ge(gated, 5 * KD * i + (product_step(d - 1, b) if d else 0))
                    sp.dma_start(g_in[:, b, :], t["g"][b * KD + d, :, bass.ds(i * BLK, BLK)]).then_inc(g_loaded[b], 16)

            def load_x(i, j):
                r, e = y_jobs[j]
                sp.wait_ge(y_stored[j % 2], 16 * (4 * i + j // 2))
                rows = bass.ds(i * BLK + r * P, P)
                sp.dma_start(xy[j % 2][:], t["x"][rows, e * BLK:(e + 1) * BLK]).then_inc(x_in[j % 2], 16)

            def round_of(i, last):
                for d in range(KD):
                    if d + 1 < KD:
                        load_weights(i, d + 1)
                    load_gates(i, d)
                if not last:
                    load_weights(i + 1, 0)
                    for p in range(3):
                        load_prep(i + 1, p)
                for j in range(n_y):
                    load_x(i, j)
                    if not last:
                        for p in (2 * j + 3, 2 * j + 4):
                            if p < n_u:
                                load_prep(i + 1, p)

            for k in range(KD):
                if k >= 2:
                    sp.wait_ge(wo_high, k - 1)
                    sp.wait_ge(wo_low, k - 1)
                sp.dma_start(w_raw[k % 2][:, 0:D], t["w_out"][k]).then_inc(wo_in[k % 2], 16)
                load_prep(0, k)
            sp.wait_ge(wo_high, KD)
            sp.wait_ge(wo_low, KD)
            load_weights(0, 0)
            for p in range(KD, n_u):
                load_prep(0, p)
            with sp.Fori(0, last_blk) as i:
                round_of(i, False)
            round_of(last_blk, True)

        @block.gpsimd
        def _(pool_e):
            def low_u(i, p):
                pool_e.wait_ge(u_high, n_u * i + (p + 1))
                pool_e.tensor_tensor(u_lo[:, order[p], :], z_in[p % 3][:], u_hi[:, order[p], :].bitcast(F32),
                                     ALU.subtract).then_inc(u_low, 1)

            def low_weights(i, d):
                pool_e.wait_ge(wp_high, KD * i + (d + 1))
                pool_e.tensor_tensor(wp_lo[d % 2][:], w_raw[d % 2][:].rearrange("p (k c) -> p k c", c=P),
                                     wp_hi[d % 2][:].bitcast(F32), ALU.subtract).then_inc(wp_low, 1)

            def round_of(i, last):
                for d in range(1, KD):
                    low_weights(i, d)
                if not last:
                    low_weights(i + 1, 0)
                    for p in range(n_u):
                        low_u(i + 1, p)

            for p in range(n_u):
                if p < KD:
                    pool_e.wait_ge(wo_high, p + 1)
                    pool_e.tensor_tensor(wo_lo[:, p, :], w_raw[p % 2][:, 0:D], wo_hi[:, p, :].bitcast(F32),
                                         ALU.subtract).then_inc(wo_low, 1)
                if p:
                    low_u(0, p - 1)
                if p == KD:
                    low_weights(0, 0)
            low_u(0, n_u - 1)
            with pool_e.Fori(0, last_blk) as i:
                round_of(i, False)
            round_of(last_blk, True)

        @block.scalar
        def _(act):
            def square(i, p):
                a = order[p]
                act.wait_ge(oz_in[p % 3], 32 * (n_u // 3) * i + 32 * (p // 3 + 1))
                act.wait_ge(normed, H_A * i + a)
                act.activation(root[:], o_in[p % 3][:], ACT.Square).then_inc(squared, 1)

            def take_root(i, p):
                act.wait_ge(summed, H_A * i + (order[p] + 1))
                act.activation(root[:], sums[:], ACT.Sqrt, bias=const["eps"][:], scale=1.0 / P).then_inc(rooted, 1)

            def high_u(i, p):
                act.wait_ge(u_made, n_u * i + (p + 1))
                act.activation(u_hi[:, order[p], :], z_in[p % 3][:], ACT.Copy).then_inc(u_high, 1)

            def high_weights(i, d):
                act.wait_ge(w_in[d % 2], 16 * (KD // 2) * i + 16 * (d // 2 + 1))
                if d or not isinstance(i, int) or i:
                    act.wait_ge(acc_ready, 24 * i + 3 * (d - 1))
                act.activation(wp_hi[d % 2][:], w_raw[d % 2][:].rearrange("p (k c) -> p k c", c=P),
                               ACT.Copy).then_inc(wp_high, 1)

            def high_m(i, d):
                act.wait_ge(gated, 5 * KD * i + 5 * (d + 1))
                act.activation(m_hi[:, d, :], m[:], ACT.Copy).then_inc(m_high, 1)

            def store_y(i, j):
                r, e = y_jobs[j]
                act.wait_ge(y_added, n_y * i + (j + 1))
                act.dma_start(t["y"][bass.ds(i * BLK + r * P, P), e * BLK:(e + 1) * BLK], xy[j % 2][:]).then_inc(y_stored[j % 2], 16)

            def round_of(i, last):
                for d in range(KD):
                    if d + 1 < KD:
                        high_weights(i, d + 1)
                    elif not last:
                        high_weights(i + 1, 0)
                        square(i + 1, 0)
                    high_m(i, d)
                for j in range(n_y):
                    if not last:
                        for p in preps(j):
                            if in_a(p):
                                take_root(i + 1, p)
                        for p in preps(j):
                            if in_a(p) and order[p] + 1 < H_A:
                                square(i + 1, p + 2)
                            high_u(i + 1, p)
                    if j:
                        store_y(i, j - 1)
                store_y(i, n_y - 1)

            for p in range(n_u):
                if p < KD:
                    act.wait_ge(wo_in[p % 2], 16 * (p // 2 + 1))
                    act.activation(wo_hi[:, p, :], w_raw[p % 2][:, 0:D], ACT.Copy).then_inc(wo_high, 1)
                if in_a(p):
                    square(0, p)
                    take_root(0, p)
                if p:
                    high_u(0, p - 1)
                if p == KD:
                    high_weights(0, 0)
            high_u(0, n_u - 1)
            with act.Fori(0, last_blk) as i:
                round_of(i, False)
            round_of(last_blk, True)
            for s in range(2):
                act.wait_ge(y_stored[s], 16 * (n_y // 2) * NBLK)

        @block.vector
        def _(dve):
            def prepare(i, p):
                n, s = order[p], p % 3
                if n < H_A:
                    at = H_A * i + (n + 1)
                    dve.wait_ge(rooted, at)
                    dve.reciprocal(root[:], root[:]).then_inc(inverted, 1)
                    dve.wait_ge(inverted, at)
                    dve.scalar_tensor_tensor(o_in[s][:], o_in[s][:], const["subln_g"][:], root[:],
                                             ALU.mult, ALU.mult).then_inc(normed, 1)
                    dve.wait_ge(normed, at)
                    dve.tensor_tensor(z_in[s][:], o_in[s][:], z_in[s][:], ALU.mult).then_inc(u_made, 1)
                else:
                    dve.wait_ge(oz_in[s], 32 * (n_u // 3) * i + 32 * (p // 3 + 1))
                    dve.tensor_tensor(z_in[s][:], o_in[s][:], z_in[s][:], ALU.mult).then_inc(u_made, 1)

            def merge_tile(i, d):
                n = KD * i + d
                dve.wait_ge(m_low, n)
                for b in range(3):
                    dve.wait_ge(g_loaded[b], 16 * (n + 1))
                    dve.wait_ge(acc_ready, 3 * n + b + 1)
                    dve.tensor_tensor((part if b else m)[:], acc[b][:], g_in[:, b, :], ALU.mult).then_inc(gated, 1)
                    dve.wait_ge(gated, product_step(n, b))
                    if b:
                        dve.tensor_tensor(m[:], m[:], part[:], ALU.add).then_inc(gated, 1)
                        dve.wait_ge(gated, product_step(n, b) + 1)
                dve.wait_ge(m_high, n + 1)
                dve.tensor_tensor(m_lo[:, d, :], m[:], m_hi[:, d, :].bitcast(F32), ALU.subtract).then_inc(m_low, 1)

            def round_of(i, last):
                for d in range(KD):
                    merge_tile(i, d)
                for j in range(n_y):
                    if not last:
                        for p in preps(j):
                            prepare(i + 1, p)
                    dve.wait_ge(y_ready, n_y * i + (j + 1))
                    dve.wait_ge(x_in[j % 2], 16 * (n_y // 2) * i + 16 * (j // 2 + 1))
                    dve.tensor_tensor(xy[j % 2][:], y_ps[j % 2][:], xy[j % 2][:], ALU.add).then_inc(y_added, 1)

            for p in range(n_u):
                prepare(0, p)
            with dve.Fori(0, last_blk) as i:
                round_of(i, False)
            round_of(last_blk, True)

        @block.tensor
        def _(pe):
            def sum_squares(i, p):
                pe.wait_ge(squared, H_A * i + (order[p] + 1))
                pe.matmul(sums[:], const["all_ones"][:, 0:P], root[:], start=True, stop=True).then_inc(summed, 1)

            def project(i, d):
                pe.wait_ge(wp_low, KD * i + (d + 1))
                for b in range(3):
                    pe.wait_ge(gated, 5 * KD * i + (product_step(d - 1, b) if d else 0))
                    for k in range(4):
                        w = 4 * b + k
                        pe.matmul(acc[b][:], wp_hi[d % 2][:, w, :], u_hi[:, w, :], start=(k == 0), stop=False)
                        pe.matmul(acc[b][:], wp_hi[d % 2][:, w, :], u_lo[:, w, :], start=False, stop=False)
                        last = pe.matmul(acc[b][:], wp_lo[d % 2][:, w, :], u_hi[:, w, :], start=False, stop=(k == 3))
                    last.then_inc(acc_ready, 1)

            def output(i, j, last_round):
                r, e = y_jobs[j]
                rows, cols = slice(r * P, (r + 1) * P), slice(e * BLK, (e + 1) * BLK)
                if not last_round:
                    for p in preps(j):
                        if in_a(p):
                            sum_squares(i + 1, p)
                pe.wait_ge(y_added, n_y * i + max(j - 1, 0))
                for k in range(KD):
                    if j == 0:
                        pe.wait_ge(m_low, KD * i + (k + 1))
                    pe.matmul(y_ps[j % 2][:], m_hi[:, k, rows], wo_hi[:, k, cols], start=(k == 0), stop=False)
                    pe.matmul(y_ps[j % 2][:], m_hi[:, k, rows], wo_lo[:, k, cols], start=False, stop=False)
                    last = pe.matmul(y_ps[j % 2][:], m_lo[:, k, rows], wo_hi[:, k, cols], start=False, stop=(k == KD - 1))
                last.then_inc(y_ready, 1)

            def round_of(i, last):
                pe.wait_ge(u_low, n_u * (i + 1))
                for d in range(KD):
                    project(i, d)
                for j in range(n_y):
                    output(i, j, last)

            for p in range(n_u):
                if in_a(p):
                    sum_squares(0, p)
            with pe.Fori(0, last_blk) as i:
                round_of(i, False)
            round_of(last_blk, True)


def scratch(nc, t):
    def dram(name, shape):
        t[name] = nc.dram_tensor(name, shape, F32, kind="Internal").ap()
    dram("qk_hi", [N_NORM, P, TOK])
    dram("qk_lo", [N_NORM, P, TOK])
    dram("v", [TOK, N_V * P])
    dram("z", [N_Z, P, TOK])
    dram("g", [N_G, P, TOK])
    dram("o", [(H_A * 2 + H_B + H_C) // 2, P, TOK])
    dram("rpb_pad", [H_B * BIAS_ROWS, PAD_W])


def build_program(nc, t):
    scratch(nc, t)
    with ExitStack() as ctx:
        keep = Pool(nc, ctx, "keep")
        const = {
            "ident": keep.sb("ident", [P, P]), "head_ones": keep.sb("head_ones", [P, P], F32R),
            "all_ones": keep.sb("all_ones", [P, BLK]), "gains": keep.sb("gains", [P, N_NORM]),
            "sink": keep.sb("sink", [P, H_C]), "subln_g": keep.sb("subln_g", [P, 1]),
            "eps": keep.sb("eps", [P, 1]), "neg_lam": keep.sb("neg_lam", [P, 1]),
        }
        with ExitStack() as first:
            early = Pool(nc, first, "early")
            stage_constants(nc, t, const)
            h_hi = early.sb("h_hi", [P, KD, TOK], F32R)
            h_lo = early.sb("h_lo", [P, KD, TOK], F32R)
            stage_normalise(nc, t, const, h_hi, h_lo)
            tile = 0
            for tag, kinds, pairs, outs in (("pqk", ("norm", "g"), N_NORM, (0, 0)),
                                            ("pvz", ("v", "z"), N_V, (0, 0)),
                                            ("pzg", ("z", "g"), N_Z - N_V, (N_V, N_NORM))):
                stage_project(nc, t, const, h_hi, h_lo, tag, kinds, pairs, tile, outs)
                tile += 2 * pairs
        for tag, (tok0, T) in zip(("as", "ap"), SEQS):
            stage_attend_a(nc, t, const, tag, tok0, T)
        stage_attend_grid(nc, t, const)
        stage_attend_slide(nc, t, const)
        stage_merge(nc, t, const)


def column_tiles():
    starts, at = {}, 0
    for name, width in (("qa", 512), ("ka", 512), ("va", 512), ("za", 512), ("qb", 512), ("kb", 512), ("vb", 512),
                        ("zb", 512), ("qc", 512), ("kc", 128), ("vc", 128), ("zc", 512),
                        ("ga", 1024), ("gb", 1024), ("gc", 1024)):
        starts[name] = list(range(at // P, (at + width) // P))
        at += width
    kinds = {"norm": ("qa", "ka", "qb", "kb", "qc", "kc"), "v": ("va", "vb", "vc"), "z": ("za", "zb", "zc"),
             "g": ("ga", "gb", "gc")}
    tiles = {k: [n for name in names for n in starts[name]] for k, names in kinds.items()}
    order = []
    for i in range(N_NORM):
        order += [tiles["norm"][i], tiles["g"][i]]
    for i in range(N_V):
        order += [tiles["v"][i], tiles["z"][i]]
    for i in range(N_Z - N_V):
        order += [tiles["z"][N_V + i], tiles["g"][N_NORM + i]]
    return order


def shape_constants():
    p = np.arange(P)
    out = {"ident": np.eye(P, dtype=np.float32)}
    out["head_ones"] = (p[:, None] // HD == p[None, :] // HD).astype(np.float32)
    x = np.arange(2 * T_SAMPLE - P)
    out["alibi"] = -np.abs(p[:, None] - (x[None, :] - (T_SAMPLE - P))).astype(np.float32)
    dist = np.abs(p[:, None] + P - np.arange(3 * P)[None, :])
    out["slide_dist"] = -dist.astype(np.float32)
    out["slide_mask"] = np.where(dist <= P, 0.0, NEG).astype(np.float32)
    col, row = p % GRID_W, p // GRID_W
    start = np.clip(col - KW // 2, 0, GRID_W - KW)
    key = np.arange(GRID_W)
    seen = (key[None, :] >= start[:, None]) & (key[None, :] < start[:, None] + KW)
    out["col_mask"] = np.tile(np.where(seen, 0.0, NEG).astype(np.float32), (1, 14))
    delta = np.arange(-4, 6)[None, :] - row[:, None]
    rows = np.where((delta >= -(MAX_KH // 2)) & (delta < MAX_KH // 2), 0.0, NEG).astype(np.float32)
    out["row_mask"] = np.repeat(rows, GRID_W, axis=1)
    return out


def laid_out(a):
    a = {k: np.asarray(v) for k, v in a.items()}
    out = {"x": np.concatenate([a["x_sample"][0], a["x_prompt"][0]], axis=0)}
    w = a["w_in"][0].reshape(KD, P, -1, P).transpose(2, 1, 0, 3)[column_tiles()]
    out["w_in"] = w.reshape(w.shape[0], P, KD * P)
    out["norm_g"] = a["norm_g"]
    gains = []
    for name, n_q, n_k in (("qk_gain_a", 4, 4), ("qk_gain_b", 4, 4), ("qk_gain_c", 4, 1)):
        gains += [a[name][0, 0]] * n_q + [a[name][0, 1]] * n_k
    out["gains"] = np.stack([np.concatenate([g, g]) for g in gains], axis=1)
    out["lambda_a"], out["subln_g"], out["sink_c"] = a["lambda_a"][0], a["subln_g_a"], a["sink_c"]
    out["rpb"] = a["rpb_b"][0].reshape(H_B * BIAS_ROWS, BIAS_COLS)[:, ::-1].copy()
    w3 = [a[f"w_proj_{n}"][0].reshape(4, P, KD, P) for n in "abc"]
    out["w_proj"] = np.stack(w3).transpose(3, 2, 0, 1, 4).reshape(KD, P, 12 * P)
    out["w_out"] = a["w_out"][0].reshape(KD, P, D)
    out.update(shape_constants())
    return {k: np.ascontiguousarray(v) for k, v in out.items()}


def kernel(**inputs):
    import concourse.bacc as bacc
    from concourse.bass_utils import run_bass_kernel_spmd

    nc = bacc.Bacc("TRN2", target_bir_lowering=False, num_devices=1)
    arrays = laid_out(inputs)
    t = {n: nc.dram_tensor(f"in_{n}", a.shape, mybir.dt.from_np(a.dtype), kind="ExternalInput").ap()
         for n, a in arrays.items()}
    t["y"] = nc.dram_tensor("y", (TOK, D), F32, kind="ExternalOutput").ap()
    build_program(nc, t)
    result = run_bass_kernel_spmd(nc, [{f"in_{n}": a for n, a in arrays.items()}], core_ids=[0])
    y = result.results[0]["y"]
    return y[T_SAMPLE:].reshape(1, T_PROMPT, D), y[:T_SAMPLE].reshape(1, T_SAMPLE, D)
```
